# Optimizing a Trainium2 kernel written in Bass

```python
import jax
import jax.numpy as jnp
from jax import lax
import numpy as np
import math
import jax, jax.numpy as jnp

D_MODEL = 1024
BATCH = 1
SEQ = 256
DEPTH = 1

M_HEADS = 4
M_HEAD_DIM = 128
M_WIDTH = M_HEADS * M_HEAD_DIM
M_CONV = 4
M_CHUNK = 64

A_HEADS = 8
A_HEAD_DIM = 64
A_WIDTH = A_HEADS * A_HEAD_DIM
MOBA_BLOCK = 256
MOBA_TOPK = 3
Q_BLOCK = 64
ROPE_THETA = 10000.0

D_FF = ((8 * D_MODEL + 3 * 256 - 1) // (3 * 256)) * 256

N_MOD = 6
IN_SPLITS = (M_WIDTH, M_WIDTH, M_WIDTH, M_WIDTH, M_HEADS, M_HEADS, A_WIDTH, A_WIDTH, A_WIDTH, D_MODEL, D_MODEL)
D_IN = 4 * M_WIDTH + 2 * M_HEADS + 3 * A_WIDTH + 2 * D_MODEL
F_GATE_OFFSET = 4 * M_WIDTH + M_HEADS
RMS_EPS = 1e-6


def rms_norm(x, g):
    xf = x.astype(jnp.float32)
    y = xf * lax.rsqrt(jnp.mean(xf * xf, axis=-1, keepdims=True) + RMS_EPS)
    return (y * g.astype(jnp.float32)).astype(x.dtype)

def modulate(h, shift, scale):
    return h * (1 + scale[:, None, :]) + shift[:, None, :]

def causal_dwconv(x, w, b):
    K = w.shape[0]
    S = x.shape[1]
    xp = jnp.pad(x, ((0, 0), (K - 1, 0), (0, 0)))
    y = b
    for j in range(K):
        y = y + xp[:, j:j + S, :] * w[j]
    return y

def split_heads(t, n_heads, head_dim):
    B, S, _ = t.shape
    return t.reshape(B, S, n_heads, head_dim).transpose(0, 2, 1, 3)

def merge_heads(t):
    B, H, S, Dh = t.shape
    return t.transpose(0, 2, 1, 3).reshape(B, S, H * Dh)

def rope(x, positions):
    half = x.shape[-1] // 2
    inv_freq = ROPE_THETA ** (-jnp.arange(half, dtype=jnp.float32) / half)
    ang = positions.astype(jnp.float32)[:, None, :, None] * inv_freq
    cos, sin = jnp.cos(ang), jnp.sin(ang)
    xf = x.astype(jnp.float32)
    x1, x2 = xf[..., :half], xf[..., half:]
    out = jnp.concatenate([x1 * cos - x2 * sin, x2 * cos + x1 * sin], axis=-1)
    return out.astype(x.dtype)

def mlstm_chunkwise(q, k, v, i_pre, f_pre):
    B, H, S, Dh = q.shape
    L = M_CHUNK
    NC = S // L
    f32 = jnp.float32
    q = q.astype(f32).reshape(B, H, NC, L, Dh)
    k = (k.astype(f32) * (Dh ** -0.5)).reshape(B, H, NC, L, Dh)
    v = v.astype(f32).reshape(B, H, NC, L, Dh)
    log_i = i_pre.astype(f32).reshape(B, H, NC, L)
    log_f = jax.nn.log_sigmoid(f_pre.astype(f32)).reshape(B, H, NC, L)
    b = jnp.cumsum(log_f, axis=-1)
    b_last = b[..., -1]
    a = b_last[..., None] - b + log_i

    def step(carry, inp):
        C, n, m = carry
        a_c, bl_c, k_c, v_c = inp
        m_new = jnp.maximum(bl_c + m, jnp.max(a_c, axis=-1))
        decay = jnp.exp(bl_c + m - m_new)
        w = jnp.exp(a_c - m_new[..., None])
        C_new = decay[..., None, None] * C + jnp.einsum('bhl,bhld,bhle->bhde', w, v_c, k_c)
        n_new = decay[..., None] * n + jnp.einsum('bhl,bhle->bhe', w, k_c)
        return (C_new, n_new, m_new), (C, n, m)

    init = (jnp.zeros((B, H, Dh, Dh), f32), jnp.zeros((B, H, Dh), f32), jnp.zeros((B, H), f32))
    xs = (jnp.moveaxis(a, 2, 0), jnp.moveaxis(b_last, 2, 0), jnp.moveaxis(k, 2, 0), jnp.moveaxis(v, 2, 0))
    _, (C_prev, n_prev, m_prev) = lax.scan(step, init, xs)
    C_prev = jnp.moveaxis(C_prev, 0, 2)
    n_prev = jnp.moveaxis(n_prev, 0, 2)
    m_prev = jnp.moveaxis(m_prev, 0, 2)

    causal = jnp.tril(jnp.ones((L, L), dtype=bool))
    D = b[..., :, None] - b[..., None, :] + log_i[..., None, :]
    D = jnp.where(causal, D, -jnp.inf)
    inter = b + m_prev[..., None]
    m_t = jnp.maximum(inter, jnp.max(D, axis=-1))
    W = jnp.exp(D - m_t[..., None])
    SW = jnp.einsum('bhctd,bhcsd->bhcts', q, k) * W
    inter_w = jnp.exp(inter - m_t)
    num = inter_w[..., None] * jnp.einsum('bhcde,bhcte->bhctd', C_prev, q) + jnp.einsum('bhcts,bhcsd->bhctd', SW, v)
    den = inter_w * jnp.einsum('bhce,bhcte->bhct', n_prev, q) + jnp.sum(SW, axis=-1)
    h = num / jnp.maximum(jnp.abs(den), jnp.exp(-m_t))[..., None]
    return h.reshape(B, H, S, Dh)

def moba_attention(q, k, v):
    B, H, S, Dh = q.shape
    NB = -(-S // MOBA_BLOCK)
    K_SEL = min(MOBA_TOPK, NB)
    pad = NB * MOBA_BLOCK - S
    NQ = S // Q_BLOCK
    scale = Dh ** -0.5
    kp = jnp.pad(k, ((0, 0), (0, 0), (0, pad), (0, 0)))
    vp = jnp.pad(v, ((0, 0), (0, 0), (0, pad), (0, 0)))
    kb = kp.reshape(B, H, NB, MOBA_BLOCK, Dh)
    vb = vp.reshape(B, H, NB, MOBA_BLOCK, Dh)
    kmean = jnp.mean(kb.astype(jnp.float32), axis=3).astype(k.dtype)
    bi = jnp.arange(B)[:, None, None, None]
    hi = jnp.arange(H)[None, :, None, None]
    blk_ids = jnp.arange(NB)

    def one_block(qi):
        q0 = qi * Q_BLOCK
        qc = lax.dynamic_slice_in_dim(q, q0, Q_BLOCK, axis=2)
        cur = q0 // MOBA_BLOCK
        gate = jnp.einsum('bhqd,bhnd->bhqn', qc, kmean).astype(jnp.float32)
        gate = jnp.where(blk_ids < cur, gate, -jnp.inf)
        _, gidx = lax.top_k(gate, K_SEL)
        valid = gidx < cur
        kg = kb[bi, hi, gidx]
        vg = vb[bi, hi, gidx]
        s_sel = jnp.einsum('bhqd,bhqjkd->bhqjk', qc, kg).astype(jnp.float32) * scale
        s_sel = jnp.where(valid[..., None], s_sel, -jnp.inf).reshape(B, H, Q_BLOCK, K_SEL * MOBA_BLOCK)
        k_own = lax.dynamic_slice_in_dim(kp, cur * MOBA_BLOCK, MOBA_BLOCK, axis=2)
        v_own = lax.dynamic_slice_in_dim(vp, cur * MOBA_BLOCK, MOBA_BLOCK, axis=2)
        s_own = jnp.einsum('bhqd,bhkd->bhqk', qc, k_own).astype(jnp.float32) * scale
        qpos = q0 + jnp.arange(Q_BLOCK)
        kpos = cur * MOBA_BLOCK + jnp.arange(MOBA_BLOCK)
        s_own = jnp.where(kpos[None, :] <= qpos[:, None], s_own, -jnp.inf)
        p = jax.nn.softmax(jnp.concatenate([s_sel, s_own], axis=-1), axis=-1).astype(v.dtype)
        p_sel = p[..., :K_SEL * MOBA_BLOCK].reshape(B, H, Q_BLOCK, K_SEL, MOBA_BLOCK)
        p_own = p[..., K_SEL * MOBA_BLOCK:]
        return jnp.einsum('bhqjk,bhqjkd->bhqd', p_sel, vg) + jnp.einsum('bhqk,bhkd->bhqd', p_own, v_own)

    outs = lax.map(one_block, jnp.arange(NQ))
    return outs.transpose(1, 2, 0, 3, 4).reshape(B, H, S, Dh)

def first_inputs(seed: int = 0) -> dict:
    key = jax.random.key(seed)
    ks = jax.random.split(key, 20)
    f32 = jnp.float32

    def nrm(k, shape, scale):
        return jax.random.normal(k, shape, f32) * scale

    x = nrm(ks[0], (BATCH, SEQ, D_MODEL), 1.0)
    c = nrm(ks[1], (BATCH, D_MODEL), 1.0)
    positions = jnp.broadcast_to(jnp.arange(SEQ, dtype=jnp.int32), (BATCH, SEQ))
    ada_w = nrm(ks[2], (DEPTH, D_MODEL, N_MOD * D_MODEL), 0.5 * D_MODEL ** -0.5)
    ada_b = nrm(ks[3], (DEPTH, N_MOD * D_MODEL), 0.02)
    norm1_g = 1.0 + nrm(ks[4], (DEPTH, D_MODEL), 0.02)
    norm2_g = 1.0 + nrm(ks[5], (DEPTH, D_MODEL), 0.02)
    normf_g = 1.0 + nrm(ks[6], (D_MODEL,), 0.02)
    w_in = nrm(ks[7], (DEPTH, D_MODEL, D_IN), D_MODEL ** -0.5)
    b_in = nrm(ks[8], (DEPTH, D_IN), 0.02)
    b_in = b_in.at[:, F_GATE_OFFSET:F_GATE_OFFSET + M_HEADS].add(jnp.linspace(3.0, 6.0, M_HEADS, dtype=f32))
    conv_w = nrm(ks[9], (DEPTH, M_CONV, 2 * M_WIDTH), M_CONV ** -0.5)
    conv_b = nrm(ks[10], (DEPTH, 2 * M_WIDTH), 0.02)
    m_norm_g = 1.0 + nrm(ks[11], (DEPTH, M_WIDTH), 0.02)
    p_mlstm = nrm(ks[12], (DEPTH, M_WIDTH, D_MODEL), M_WIDTH ** -0.5)
    p_moba = nrm(ks[13], (DEPTH, A_WIDTH, D_MODEL), A_WIDTH ** -0.5)
    w_out = nrm(ks[14], (DEPTH, D_MODEL, D_MODEL), D_MODEL ** -0.5)
    w_gate = nrm(ks[15], (DEPTH, D_MODEL, D_FF), D_MODEL ** -0.5)
    w_up = nrm(ks[16], (DEPTH, D_MODEL, D_FF), D_MODEL ** -0.5)
    w_down = nrm(ks[17], (DEPTH, D_FF, D_MODEL), D_FF ** -0.5)
    return {'x': x, 'c': c, 'positions': positions, 'ada_w': ada_w, 'ada_b': ada_b,
            'norm1_g': norm1_g, 'norm2_g': norm2_g, 'normf_g': normf_g, 'w_in': w_in, 'b_in': b_in,
            'conv_w': conv_w, 'conv_b': conv_b, 'm_norm_g': m_norm_g, 'p_mlstm': p_mlstm,
            'p_moba': p_moba, 'w_out': w_out, 'w_gate': w_gate, 'w_up': w_up, 'w_down': w_down}

def first_block(x, c, positions, ada_w, ada_b, norm1_g, norm2_g, normf_g, w_in, b_in,
              conv_w, conv_b, m_norm_g, p_mlstm, p_moba, w_out, w_gate, w_up, w_down):
    B, S, D = x.shape
    split_points = np.cumsum(IN_SPLITS)[:-1].tolist()
    c_act = jax.nn.silu(c)
    for l in range(DEPTH):
        mod = jnp.dot(c_act, ada_w[l]) + ada_b[l]
        sh1, sc1, g1, sh2, sc2, g2 = jnp.split(mod, N_MOD, axis=-1)

        h = modulate(rms_norm(x, norm1_g[l]), sh1, sc1)
        z = jnp.einsum('bsd,de->bse', h, w_in[l]) + b_in[l]
        mq, mk, mv, mo, mi, mf, aq, ak, av, ga, gb = jnp.split(z, split_points, axis=-1)

        qk = jax.nn.silu(causal_dwconv(jnp.concatenate([mq, mk], axis=-1), conv_w[l], conv_b[l]))
        mq, mk = jnp.split(qk, 2, axis=-1)
        hm = mlstm_chunkwise(split_heads(mq, M_HEADS, M_HEAD_DIM), split_heads(mk, M_HEADS, M_HEAD_DIM),
                             split_heads(mv, M_HEADS, M_HEAD_DIM), mi.transpose(0, 2, 1), mf.transpose(0, 2, 1))
        hm = rms_norm(hm.transpose(0, 2, 1, 3), m_norm_g[l].reshape(M_HEADS, M_HEAD_DIM))
        ym = (hm.reshape(B, S, M_WIDTH) * jax.nn.sigmoid(mo)).astype(x.dtype)

        qa = rope(split_heads(aq, A_HEADS, A_HEAD_DIM), positions)
        ka = rope(split_heads(ak, A_HEADS, A_HEAD_DIM), positions)
        va = split_heads(av, A_HEADS, A_HEAD_DIM)
        ya = merge_heads(moba_attention(qa, ka, va))

        merged = (jax.nn.sigmoid(ga) * jnp.einsum('bsm,md->bsd', ym, p_mlstm[l])
                  + jax.nn.sigmoid(gb) * jnp.einsum('bsa,ad->bsd', ya, p_moba[l]))
        x = x + g1[:, None, :] * jnp.einsum('bsd,de->bse', merged, w_out[l])

        h = modulate(rms_norm(x, norm2_g[l]), sh2, sc2)
        f = jax.nn.silu(jnp.einsum('bsd,df->bsf', h, w_gate[l])) * jnp.einsum('bsd,df->bsf', h, w_up[l])
        x = x + g2[:, None, :] * jnp.einsum('bsf,fd->bsd', f, w_down[l])
    return rms_norm(x, normf_g)


DEPTH_2 = 2

N_MEM = 256
EPS = 1e-6

A_WIDTH_2 = 512
CONV_WIDTH = 3
POOL_WINDOWS = (2, 4, 8, 16)
POOL_GROUP = 128
B_WIDTH = 512
C_HEADS = 8
C_LATENT = 128
C_HEAD_DIM = 64
IDX_HEADS = 8
IDX_DIM = 64
DSA_TOPK_MAX = 256
Q_BLOCK_2 = 128
REL_BUCKETS = 32
REL_MAX_DIST = 128
D_HEADS = 4
D_KEY = 128
D_VAL = 128
CHUNK = 64
X_HEADS = 4
X_HEAD_DIM = 256
N_KEYS = 128
N_EXPERTS = 16384
PEER_HEADS = 8
PEER_QDIM = 256
PEER_HALF = 128
PEER_TOPK = 16
PEER_BLOCK = 128

EVEN_SPLITS = (512, 512, 512, 512)
ODD_SPLITS = (1024, 128, 512, 64, 8, 512, 512, 512, 512)
EVEN_IN = 2048
ODD_IN = 3784
MIX_WIDTH = 1024


def _split(a, sizes):
    offs = np.cumsum(sizes)[:-1].tolist()
    return jnp.split(a, offs, axis=-1)

def rmsnorm(x, g):
    xf = x.astype(jnp.float32)
    y = xf * lax.rsqrt(jnp.mean(xf * xf, axis=-1, keepdims=True) + EPS)
    return (y * g.astype(jnp.float32)).astype(x.dtype)

def softmax32(logits, dtype):
    return jax.nn.softmax(logits.astype(jnp.float32), axis=-1).astype(dtype)

def t5_bucket(dist):
    max_exact = REL_BUCKETS // 2
    d = jnp.maximum(dist, 0)
    log_ratio = jnp.log(jnp.maximum(d, 1).astype(jnp.float32) / max_exact) / math.log(REL_MAX_DIST / max_exact)
    large = max_exact + (log_ratio * (REL_BUCKETS - max_exact)).astype(jnp.int32)
    large = jnp.minimum(large, REL_BUCKETS - 1)
    return jnp.where(d < max_exact, d, large)

def short_conv_pool_mixer(h, w_in, conv_w, pool_w, pool_scale, w_out):
    B_, S_, _ = h.shape
    u, gate_c, gate_b, pv = _split(h @ w_in, EVEN_SPLITS)
    z = lax.conv_general_dilated(gate_c * u, conv_w, window_strides=(1,), padding=[(CONV_WIDTH - 1, 0)],
                                 dimension_numbers=('NWC', 'WIO', 'NWC'), feature_group_count=A_WIDTH_2)
    y_a = gate_b * z
    cs = jnp.cumsum(pv.astype(jnp.float32), axis=1)
    cs = jnp.concatenate([jnp.zeros((B_, 1, B_WIDTH), jnp.float32), cs], axis=1)
    pos = jnp.arange(S_)
    groups = []
    for gi, w in enumerate(POOL_WINDOWS):
        sl = slice(gi * POOL_GROUP, (gi + 1) * POOL_GROUP)
        lo = jnp.maximum(pos + 1 - w, 0)
        cnt = jnp.minimum(pos + 1, w).astype(jnp.float32)
        mean = (cs[:, 1:, sl] - cs[:, lo, sl]) / cnt[None, :, None]
        groups.append(mean.astype(h.dtype) - pv[..., sl])
    pooled = jnp.stack(groups, axis=2)
    y_b = jnp.einsum('bsgc,gcd->bsgd', pooled, pool_w).reshape(B_, S_, B_WIDTH) * pool_scale
    return jnp.concatenate([y_a, y_b], axis=-1) @ w_out

def dsa_attention(q_lat, c_kv, iq, ik, iw, rel_bias):
    B_, S_ = c_kv.shape[:2]
    topk = min(DSA_TOPK_MAX, S_ // 4)
    n_blocks = S_ // Q_BLOCK_2
    scale = C_LATENT ** -0.5
    idx_scale = IDX_DIM ** -0.5
    key_pos = jnp.arange(S_)

    def block(start):
        qb = lax.dynamic_slice_in_dim(q_lat, start, Q_BLOCK_2, axis=1)
        iqb = lax.dynamic_slice_in_dim(iq, start, Q_BLOCK_2, axis=1)
        iwb = lax.dynamic_slice_in_dim(iw, start, Q_BLOCK_2, axis=1)
        t = start + jnp.arange(Q_BLOCK_2)
        rel = jax.nn.relu(jnp.einsum('bthd,bsd->bths', iqb, ik) * idx_scale)
        score = jnp.einsum('bths,bth->bts', rel, iwb).astype(jnp.float32)
        causal = key_pos[None, :] <= t[:, None]
        score = jnp.where(causal[None], score, -jnp.inf)
        _, sel = lax.top_k(score, topk)
        c_sel = jax.vmap(lambda c, i: c[i])(c_kv, sel)
        valid = sel <= t[None, :, None]
        bias = rel_bias[t5_bucket(t[None, :, None] - sel)]
        logits = (jnp.einsum('bthr,btkr->bhtk', qb, c_sel).astype(jnp.float32) * scale
                  + jnp.moveaxis(bias, -1, 1).astype(jnp.float32))
        logits = jnp.where(valid[:, None], logits, -jnp.inf)
        p = softmax32(logits, c_kv.dtype)
        return jnp.einsum('bhtk,btkr->bthr', p, c_sel)

    out = lax.map(block, jnp.arange(n_blocks) * Q_BLOCK_2)
    return jnp.moveaxis(out, 0, 1).reshape(B_, S_, C_HEADS, C_LATENT)

def hgrn2(q, f_logit, inp, gate, lb, norm_g):
    B_, S_, _ = q.shape
    nc = S_ // CHUNK
    f = lb + (1.0 - lb) * jax.nn.sigmoid(f_logit.astype(jnp.float32))
    log_f = jnp.log(f)
    k = 1.0 - f

    def to_chunks(a, d):
        return a.astype(jnp.float32).reshape(B_, nc, CHUNK, D_HEADS, d).transpose(1, 0, 3, 2, 4)

    qc, kc, lfc = to_chunks(q, D_KEY), to_chunks(k, D_KEY), to_chunks(log_f, D_KEY)
    ic = to_chunks(inp, D_VAL)
    causal = jnp.tril(jnp.ones((CHUNK, CHUNK), bool))

    def step(state, xs):
        qj, kj, ij, lfj = xs
        A = jnp.cumsum(lfj, axis=2)
        o_inter = jnp.einsum('bhtk,bhkv->bhtv', qj * jnp.exp(A), state)
        diff = A[:, :, :, None, :] - A[:, :, None, :, :]
        decay = jnp.exp(jnp.where(causal[:, :, None], diff, -jnp.inf))
        scores = jnp.einsum('bhtk,bhsk,bhtsk->bhts', qj, kj, decay)
        o_intra = jnp.einsum('bhts,bhsv->bhtv', scores, ij)
        A_end = A[:, :, -1]
        new_state = (jnp.exp(A_end)[..., None] * state
                     + jnp.einsum('bhsk,bhsv->bhkv', kj * jnp.exp(A_end[:, :, None] - A), ij))
        return new_state, o_inter + o_intra

    state0 = jnp.zeros((B_, D_HEADS, D_KEY, D_VAL), jnp.float32)
    _, o = lax.scan(step, state0, (qc, kc, ic, lfc))
    o = o.transpose(1, 0, 3, 2, 4).reshape(B_, S_, D_HEADS, D_VAL)
    o = o * lax.rsqrt(jnp.mean(o * o, axis=-1, keepdims=True) + EPS) * norm_g.astype(jnp.float32).reshape(D_HEADS, D_VAL)
    return (o.reshape(B_, S_, D_HEADS * D_VAL) * jax.nn.silu(gate.astype(jnp.float32))).astype(q.dtype)

def sparse_attn_hgrn_mixer(h, w_in, kv_norm, w_uv, hg_norm, w_out, rel_bias, lb):
    B_, S_, _ = h.shape
    q_lat, c_kv, iq, ik, iw, hq, hf, hi, hg = _split(h @ w_in, ODD_SPLITS)
    c_kv = rmsnorm(c_kv, kv_norm)
    lat = dsa_attention(q_lat.reshape(B_, S_, C_HEADS, C_LATENT), c_kv,
                        iq.reshape(B_, S_, IDX_HEADS, IDX_DIM), ik, iw * IDX_HEADS ** -0.5, rel_bias)
    y_c = jnp.einsum('bshr,hrd->bshd', lat, w_uv).reshape(B_, S_, C_HEADS * C_HEAD_DIM)
    y_d = hgrn2(hq, hf, hi, hg, lb, hg_norm)
    return jnp.concatenate([y_c, y_d], axis=-1) @ w_out

def memory_cross_attn(h, mem_n, wq, wkv, wo):
    B_, S_, _ = h.shape
    q = (h @ wq).reshape(B_, S_, X_HEADS, X_HEAD_DIM)
    k, v = jnp.split(mem_n @ wkv, 2, axis=-1)
    k = k.reshape(B_, -1, X_HEADS, X_HEAD_DIM)
    v = v.reshape(B_, -1, X_HEADS, X_HEAD_DIM)
    logits = jnp.einsum('bshd,bmhd->bhsm', q, k).astype(jnp.float32) * X_HEAD_DIM ** -0.5
    p = softmax32(logits, h.dtype)
    o = jnp.einsum('bhsm,bmhd->bshd', p, v).reshape(B_, S_, D_MODEL)
    return o @ wo

def peer_ffn(h, wq, sub_keys, u, v):
    B_, S_, D_ = h.shape
    T = B_ * S_
    ht = h.reshape(T, D_)

    def block(start):
        xb = lax.dynamic_slice_in_dim(ht, start, PEER_BLOCK, axis=0)
        q = (xb @ wq).reshape(PEER_BLOCK, PEER_HEADS, 2, PEER_HALF)
        s = jnp.einsum('thpd,hpnd->thpn', q, sub_keys).astype(jnp.float32)
        s1, i1 = lax.top_k(s[:, :, 0], PEER_TOPK)
        s2, i2 = lax.top_k(s[:, :, 1], PEER_TOPK)
        cand = (s1[..., :, None] + s2[..., None, :]).reshape(PEER_BLOCK, PEER_HEADS, PEER_TOPK * PEER_TOPK)
        cand_id = (i1[..., :, None] * N_KEYS + i2[..., None, :]).reshape(PEER_BLOCK, PEER_HEADS, PEER_TOPK * PEER_TOPK)
        top, pos = lax.top_k(cand, PEER_TOPK)
        eid = jnp.take_along_axis(cand_id, pos, axis=-1).reshape(PEER_BLOCK, PEER_HEADS * PEER_TOPK)
        g = jax.nn.softmax(top, axis=-1).reshape(PEER_BLOCK, PEER_HEADS * PEER_TOPK).astype(xb.dtype)
        act = jax.nn.gelu(jnp.einsum('td,ted->te', xb, u[eid]))
        return jnp.einsum('te,ted->td', g * act, v[eid])

    out = lax.map(block, jnp.arange(T // PEER_BLOCK) * PEER_BLOCK)
    return out.reshape(B_, S_, D_)

def second_inputs(seed: int = 0) -> dict:
    key = jax.random.key(seed)
    ks = iter(jax.random.split(key, 32))
    n_even = (DEPTH_2 + 1) // 2
    n_odd = DEPTH_2 // 2

    def nrm(shape, scale):
        return jax.random.normal(next(ks), shape, jnp.float32) * scale

    def gain(shape):
        return 1.0 + 0.02 * jax.random.normal(next(ks), shape, jnp.float32)

    return {
        'x': nrm((BATCH, SEQ, D_MODEL), 1.0),
        'mem': nrm((BATCH, N_MEM, D_MODEL), 1.0),
        'mix_norm': gain((DEPTH_2, D_MODEL)),
        'even_w_in': nrm((n_even, D_MODEL, EVEN_IN), D_MODEL ** -0.5),
        'even_conv_w': nrm((n_even, CONV_WIDTH, 1, A_WIDTH_2), CONV_WIDTH ** -0.5),
        'even_pool_w': nrm((n_even, len(POOL_WINDOWS), POOL_GROUP, POOL_GROUP), POOL_GROUP ** -0.5),
        'even_pool_scale': gain((n_even, B_WIDTH)),
        'even_w_out': nrm((n_even, MIX_WIDTH, D_MODEL), MIX_WIDTH ** -0.5),
        'odd_w_in': nrm((n_odd, D_MODEL, ODD_IN), D_MODEL ** -0.5),
        'odd_kv_norm': gain((n_odd, C_LATENT)),
        'odd_w_uv': nrm((n_odd, C_HEADS, C_LATENT, C_HEAD_DIM), C_LATENT ** -0.5),
        'odd_hg_norm': gain((n_odd, D_HEADS * D_VAL)),
        'odd_w_out': nrm((n_odd, MIX_WIDTH, D_MODEL), MIX_WIDTH ** -0.5),
        'hgrn_gamma': nrm((DEPTH_2, D_HEADS * D_KEY), 0.5),
        'rel_bias': nrm((REL_BUCKETS, C_HEADS), 0.5),
        'mem_norm': gain((D_MODEL,)),
        'xattn_norm': gain((DEPTH_2, D_MODEL)),
        'xattn_wq': nrm((DEPTH_2, D_MODEL, D_MODEL), D_MODEL ** -0.5),
        'xattn_wkv': nrm((DEPTH_2, D_MODEL, 2 * D_MODEL), D_MODEL ** -0.5),
        'xattn_wo': nrm((DEPTH_2, D_MODEL, D_MODEL), D_MODEL ** -0.5),
        'peer_norm': gain((DEPTH_2, D_MODEL)),
        'peer_wq': nrm((DEPTH_2, D_MODEL, PEER_HEADS * PEER_QDIM), D_MODEL ** -0.5),
        'peer_keys': nrm((DEPTH_2, PEER_HEADS, 2, N_KEYS, PEER_HALF), PEER_HALF ** -0.5),
        'peer_u': nrm((DEPTH_2, N_EXPERTS, D_MODEL), D_MODEL ** -0.5),
        'peer_v': nrm((DEPTH_2, N_EXPERTS, D_MODEL), (PEER_HEADS * PEER_TOPK) ** -0.5),
        'final_norm': gain((D_MODEL,)),
    }

def second_block(x, mem, mix_norm, even_w_in, even_conv_w, even_pool_w, even_pool_scale, even_w_out,
              odd_w_in, odd_kv_norm, odd_w_uv, odd_hg_norm, odd_w_out, hgrn_gamma, rel_bias, mem_norm,
              xattn_norm, xattn_wq, xattn_wkv, xattn_wo, peer_norm, peer_wq, peer_keys, peer_u, peer_v,
              final_norm):
    mem_n = rmsnorm(mem, mem_norm)
    p = jax.nn.softmax(hgrn_gamma.astype(jnp.float32), axis=0)
    lower_bounds = jnp.cumsum(p, axis=0) - p
    h = x
    for l in range(DEPTH_2):
        j = l // 2
        hn = rmsnorm(h, mix_norm[l])
        if l % 2 == 0:
            h = h + short_conv_pool_mixer(hn, even_w_in[j], even_conv_w[j], even_pool_w[j],
                                          even_pool_scale[j], even_w_out[j])
        else:
            h = h + sparse_attn_hgrn_mixer(hn, odd_w_in[j], odd_kv_norm[j], odd_w_uv[j], odd_hg_norm[j],
                                           odd_w_out[j], rel_bias, lower_bounds[l])
        h = h + memory_cross_attn(rmsnorm(h, xattn_norm[l]), mem_n, xattn_wq[l], xattn_wkv[l], xattn_wo[l])
        h = h + peer_ffn(rmsnorm(h, peer_norm[l]), peer_wq[l], peer_keys[l], peer_u[l], peer_v[l])
    return rmsnorm(h, final_norm)


def setup_inputs(seed=0):
    out = dict(first_inputs(seed))
    for name, value in second_inputs(seed + 1).items():
        if name != "x":
            out[name + "_2"] = value
    return out


def reference(
    x, c, positions, ada_w, ada_b, norm1_g, norm2_g, normf_g, w_in, b_in, conv_w, conv_b,
    m_norm_g, p_mlstm, p_moba, w_out, w_gate, w_up, w_down, mem_2, mix_norm_2, even_w_in_2,
    even_conv_w_2, even_pool_w_2, even_pool_scale_2, even_w_out_2, odd_w_in_2, odd_kv_norm_2,
    odd_w_uv_2, odd_hg_norm_2, odd_w_out_2, hgrn_gamma_2, rel_bias_2, mem_norm_2, xattn_norm_2,
    xattn_wq_2, xattn_wkv_2, xattn_wo_2, peer_norm_2, peer_wq_2, peer_keys_2, peer_u_2,
    peer_v_2, final_norm_2,
):
    x = first_block(
        x, c, positions, ada_w, ada_b, norm1_g, norm2_g, normf_g, w_in, b_in, conv_w, conv_b,
        m_norm_g, p_mlstm, p_moba, w_out, w_gate, w_up, w_down,
    )
    return second_block(
        x, mem_2, mix_norm_2, even_w_in_2, even_conv_w_2, even_pool_w_2, even_pool_scale_2,
        even_w_out_2, odd_w_in_2, odd_kv_norm_2, odd_w_uv_2, odd_hg_norm_2, odd_w_out_2,
        hgrn_gamma_2, rel_bias_2, mem_norm_2, xattn_norm_2, xattn_wq_2, xattn_wkv_2, xattn_wo_2,
        peer_norm_2, peer_wq_2, peer_keys_2, peer_u_2, peer_v_2, final_norm_2,
    )


_drawn_inputs = setup_inputs


def setup_inputs(seed=0):
    import zlib

    import numpy as np

    out = dict(_drawn_inputs(seed))
    spreads = {}
    factors = {'norm1_g': 7.333,
     'norm2_g': 4.44,
     'conv_b': 8.0,
     'm_norm_g': 7.896,
     'even_pool_scale_2': 3.864,
     'odd_kv_norm_2': 8.0,
     'odd_hg_norm_2': 8.0,
     'mem_norm_2': 8.0,
     'xattn_norm_2': 8.0,
     'peer_norm_2': 5.382,
     'final_norm_2': 2.826}
    for name, (base, spread) in spreads.items():
        noise = np.random.default_rng([zlib.crc32(name.encode()), seed]).standard_normal(out[name].shape)
        drawn = base * np.exp(spread * noise) if base else spread * noise
        out[name] = jnp.asarray(drawn.astype(out[name].dtype))
    for name, factor in factors.items():
        out[name] = (out[name] * factor).astype(out[name].dtype)
    return out
```

```python
from contextlib import ExitStack

import numpy as np
import concourse.bass as bass
from concourse import mybir

ALU = mybir.AluOpType
ACT = mybir.ActivationFunctionType
AXX = mybir.AxisListType.X
F32 = mybir.dt.float32
U32 = mybir.dt.uint32
I32 = mybir.dt.int32

P = 128
S = 256
NT = S // P
D = 1024
KD = D // P
BLK = 512
EPS = 1e-6
NEG = -1e30
REMOVED = -3e38
MH, MDH, MW = 4, 128, 512
AH, ADH, AW = 8, 64, 512
DFF = 2816
NF = DFF // P
CH, CR, CDH = 8, 128, 64
IH, IDH = 8, 64
TOPK = 64
BUCKETS, MAXDIST = 32, 128
HH, HK = 4, 128
XH, XDH = 4, 256
PH, NK, PK = 8, 128, 16
NE = NK * NK
SEL = PH * PK
LEVELS = [128, 64, 32, 16, 8, 4, 2, 1]
NSLOT = 3
RING = 8
HALF = RING // 2

COLS = {}
for _n, _w in (("c", 8), ("b_qk", 8), ("conv_w", 32), ("conv_b", 8), ("even_conv", 12), ("pool_scale", 4)):
    COLS[_n] = (sum(w for _, w in COLS.values()), _w)
NCOL = sum(w for _, w in COLS.values())
CONST = {}
for _n, _w in (("ident", P), ("flip", P), ("ones", P), ("causal", 2 * S), ("tri", P), ("freq", 32), ("iota", 16)):
    CONST[_n] = (sum(w for _, w in CONST.values()), _w)
NCONST = sum(w for _, w in CONST.values())
SMALL = {}
for _n, _w in (("gates", KD * 8), ("pool_w", 4 * P), ("w_uv", CH * CDH)):
    SMALL[_n] = (sum(w for _, w in SMALL.values()), _w)
NSMALL = sum(w for _, w in SMALL.values())
ROWS = {}
for _n, _w in (("ada_b", 6 * D), ("gate_b", 8), ("b_n", 5 * BLK), ("b_g", 2 * D), ("m_norm", MW), ("gamma", 2 * 512),
               ("kv_norm", CR), ("hg_norm", 512), ("norm", 11 * D)):
    ROWS[_n] = (sum(w for _, w in ROWS.values()), _w)
NROW = sum(w for _, w in ROWS.values())
NMASK = 2 + (len(LEVELS) - 1) * 2


class Plan:

    def __init__(self):
        self.first, self.fills = {}, []
        self.marks, self.taken = 0, {"vector": 0, "scalar": 0}

    def add(self, stage, n=1, taker="vector", marks=None):
        self.first[stage] = len(self.fills), self.marks
        for i in range(n):
            self.taken[taker] += 1
            self.fills.append((self.marks + (marks or i + 1), taker, self.taken[taker]))
        self.marks += marks or n

    def mark(self, stage, i=0):
        return self.fills[self.first[stage][0] + i][0]

    def bank(self, stage, i=0):
        return (self.first[stage][0] + i) % 8

    def before(self, stage, i=0):
        n = self.first[stage][0] + i - 8
        return self.fills[n][1:] if n >= 0 else None

    def took(self, stage, i=0):
        return self.fills[self.first[stage][0] + i][1:]


def head_of(slot):
    return slot // 4 * 4 + slot % 2 * 2 + slot // 2 % 2


def place_of(slot, size):
    h = head_of(slot)
    return h // 2, slice(h % 2 * size, (h % 2 + 1) * size)


def units_of(plan, name, n):
    plan.add(f"{name}_s0")
    for u in range(n):
        if u + 1 < n:
            plan.add(f"{name}_s{u + 1}")
        plan.add(f"{name}_t{u}", taker="scalar")


def make_plan():
    p = Plan()
    p.add("bias_rows")
    p.add("ada", 12)
    p.add("T0", 4)
    p.add("z_qk", 4)
    p.add("z_gate")
    p.add("z_n", 10)
    p.add("m_cum")
    p.add("m_g0")
    p.add("m_g1")
    units_of(p, "m", 4)
    p.add("m_pv", NT)
    p.add("a_T", 4)
    units_of(p, "a", 8)
    p.add("a_pv", NT)
    p.add("y_T", 4)
    p.add("merge", 16)
    p.add("mg_T", 4)
    p.add("w_out", 4)
    p.add("T1", 4)
    for i in range(NF // 2):
        p.add(f"ff_g{i}", taker="scalar")
        p.add(f"ff_u{i}")
    p.add("down", 4, marks=6)
    p.add("T2", 4)
    p.add("T4", 4)
    p.add("e_z", 8)
    p.add("e_pool", 2)
    p.add("e_out", 4)
    for l in range(2):
        if l:
            p.add("T7", 4)
            p.add("o_ql", 4)
            p.add("o_ckv")
            p.add("o_ik")
            p.add("o_iq", 2)
            p.add("o_hq", 2)
            p.add("o_hf", 2, "scalar")
            p.add("o_hi", 2)
            p.add("o_hg", 2)
            p.add("o_cT")
            p.add("o_kT", 2)
            for n, h in enumerate(LEVELS):
                p.add(f"h_d{n}", 2, "scalar")
                p.add(f"h_s{n}", 1 if h == P else NT)
            p.add("h_diag", NT)
            p.add("h_pv", NT)
            p.add("idx", 8, "scalar")
            units_of(p, "o", 8)
            p.add("o_pv", 4)
            p.add("lat_T", 4)
            p.add("o_yc", NT)
            p.add("o_yT", 4)
            p.add("o_out", 4)
        p.add(f"x_k{l}", 4)
        p.add(f"x_v{l}", 4)
        p.add(f"T{5 + 3 * l}", 4)
        p.add(f"x_q{l}", 4)
        units_of(p, f"x{l}", 4)
        p.add(f"x_pv{l}", 4)
        p.add(f"x_oT{l}", 4)
        p.add(f"x_o{l}", 4)
        p.add(f"T{6 + 3 * l}", 4)
        p.add(f"p_q{l}", 8)
        p.add(f"p_s{l}", 8)
    return p


def tiles_in_order():
    t = [("ada", i) for i in range(12)]
    t += [("z_qk", 1), ("z_qk", 3)] + [("z_n", 2 * i + 1) for i in range(5)]
    for c in range(2):
        t += [("merge", 8 * c + 1), ("merge", 8 * c + 3), ("merge", 8 * c + 7)]
    t += [("w_out", 1), ("w_out", 3)] + [(f"ff_u{i}", 0) for i in range(NF // 2)]
    t += [("down", i) for i in range(6)]
    t += [("e_z", 2 * i + 1) for i in range(4)] + [("e_out", 1), ("e_out", 3)]
    for l in range(2):
        if l:
            t += [("o_ql", 1), ("o_ql", 3), ("o_ik", 0), ("o_iq", 1), ("o_hq", 1), ("o_hf", 1), ("o_hi", 1), ("o_hg", 1)]
            t += [("o_out", 1), ("o_out", 3)]
        t += [(f"x_k{l}", 1), (f"x_k{l}", 3), (f"x_v{l}", 1), (f"x_v{l}", 3), (f"x_q{l}", 1), (f"x_q{l}", 3)]
        t += [(f"x_o{l}", 1), (f"x_o{l}", 3)]
        t += [(f"p_q{l}", 2 * i + 1) for i in range(4)] + [(f"p_s{l}", 7)]
    return t


def build(nc, io):
    plan = make_plan()
    tiles = tiles_in_order()
    tile_no = {}
    for n, (stage, _) in enumerate(tiles):
        tile_no.setdefault(stage, n)

    with ExitStack() as ctx:
        def sb(name, shape, dt=F32):
            return ctx.enter_context(nc.sbuf_tensor(name, shape, dt))

        def sem(name):
            return ctx.enter_context(nc.semaphore(name))

        X = sb("X", [P, NT, D])
        H = sb("H", [P, NT, D])
        HT = sb("HT", [P, KD, S])
        W = sb("W", [P, NSLOT, 4096])
        gain = sb("gain", [P, 2, D])
        cols = sb("cols", [P, NCOL])
        const = sb("const", [P, NCONST])
        small = sb("small", [P, NSMALL])
        pos_i = sb("pos_i", [P, NT], I32)
        rel_sb = sb("rel_sb", [BUCKETS, 8])
        junk = sb("junk", [P, D])
        st = sb("st", [P, 640])
        arena = sb("arena", [P, 24576])
        banks = ctx.enter_context(nc.psum_tensor("banks", [P, 8, 512], F32))
        bias_scratch = nc.dram_tensor("bias_scratch", [8, 2 * S], F32).ap()

        def area(at, *shape):
            n = int(np.prod(shape))
            v = arena[:, at:at + n]
            if len(shape) == 1:
                return v
            names = "abc"[:len(shape)]
            return v.rearrange(f"p ({' '.join(names)}) -> p {' '.join(names)}", **dict(zip(names[1:], shape[1:])))

        def stat(at, *shape):
            n = int(np.prod(shape))
            v = st[:, at:at + n]
            if len(shape) == 1:
                return v
            names = "abc"[:len(shape)]
            return v.rearrange(f"p ({' '.join(names)}) -> p {' '.join(names)}", **dict(zip(names[1:], shape[1:])))

        def part(t, table, name):
            a, n = table[name]
            return t[:, a:a + n]

        ident, flip, ones = (part(const, CONST, n) for n in ("ident", "flip", "ones"))
        tri = part(const, CONST, "tri")
        causal = part(const, CONST, "causal").rearrange("p (t s) -> p t s", t=NT)
        freq, iota = part(const, CONST, "freq"), part(const, CONST, "iota")
        mod = area(0, 6, D)
        b_rows = area(6144, 8 + 5 * BLK)
        Z = area(8712, NT, 5 * BLK)
        MV, MO, AQ, AV = 0, 512, 1024, 2048
        qk_raw = area(13832, 8, S + 3)
        aT = area(13832, 8, S)
        qkT = area(15904, 8, S)
        yT = area(15904, 8, S)
        PT1 = area(17952, 8, NT, S)
        scrA = area(22048, 2, 512)
        probs = area(23072, 2, 512)
        rope_t = area(17952, 4, 512)
        m_row = area(22048, MW)
        g_log = area(17952, 2, 2, S)
        sg = area(17952, 4, 512)
        mW = area(18976, 2, 512)
        fT = area(8712, NF, S)
        silu_g = area(14344, 2, 512)
        memT = area(0, KD, S)
        e_z = area(2048, 16, S)
        e_cu = area(6144, 4, S + 2)
        e_pv = area(7176, 4, S + 16)
        e_t = area(8264, 2, S + 16)
        e_pool = area(8808, 4, S)
        e_inv = area(9832, 4, S)
        e_yT = area(10856, 8, S)
        x_qT = area(2048, 8, S)
        x_kT = area(4096, 8, S)
        x_v = area(6144, NT, D)
        x_PT = area(8192, 4, NT, S)
        p_qT = area(2048, 16, S)
        p_s = area(6144, 16, NK)
        p_work = area(8192, 2048)
        p_cand = area(10240, 2048)
        p_eq = area(12288, 2048)
        rows_u = area(14336, RING, D)
        p_v16 = area(22528, 16, PK)
        p_top = area(22784, PH, PK)
        p_eid = sb("p_eid", [P, NT, SEL], U32)
        p_idx = sb("p_idx", [P, 16, PK], U32)
        p_pos = sb("p_pos", [P, PH, PK], U32)
        p_bits = sb("p_bits", [P, 2, SEL], U32)
        p_ab = area(22912, 2, SEL)
        p_i16 = area(23168, 16, PK)
        p_g = area(23424, NT, SEL)
        p_act = area(23680, NT, SEL)
        p_w = area(23936, NT, SEL)
        p_i12 = area(24192, 2, SEL)
        stage_idx = sb("stage_idx", [P, 2, HALF], U32)
        o_qT = area(2048, 8, S)
        o_c = area(4096, NT, P + 8)
        o_cT = area(4368, S)
        o_iqT = area(4624, 4, S)
        o_ikT = area(5648, S)
        h_qT = area(5904, HH, S)
        h_f = area(6928, NT, 512)
        h_kn = area(7952, NT, 512)
        h_kT = area(8976, HH, S)
        h_i = area(10000, NT, 512)
        h_g = area(11024, NT, 512)
        lb_row = area(12048, 2, 512)
        h_row = area(13072, 512)
        kv_row = area(13584, P)
        h_mask = area(13712, NMASK, P)
        h_E = area(15760, HH, S)
        h_KE = area(16784, HH, S)
        h_QE = area(17808, HH, S)
        h_x = area(18832, HH, P)
        h_sc = area(19344, NT, HH, P)
        h_tmp = area(20368, HH, P)
        h_o = area(20880, NT, 512)
        yd = area(10000, NT, 512)
        o_PT = area(11024, 8, NT, S)
        hankel = area(15120, NT, 8 * S)
        o_mask = area(19216, NT, S)
        o_score = area(19728, NT, S)
        o_work = area(20240, NT, S)
        o_rel = area(20752, 2, 512)
        onehot = sb("onehot", [BUCKETS, 2 * S])
        rb_sb = sb("rb_sb", [8, 2 * S])

        pe_filled = sem("pe_filled")
        took = {"vector": sem("vector_took"), "scalar": sem("scalar_took")}
        tile_landed = [sem(f"tile_landed{i}") for i in range(NSLOT)]
        row_landed = [sem(f"row_landed{i}") for i in range(RING)]
        rows_used = sem("rows_used")
        idx_staged = sem("idx_staged")
        named = {}

        def S_(name):
            if name not in named:
                named[name] = sem(name)
            return named[name]

        class Steps:

            def __init__(self, eng, own, name):
                self.eng, self.own, self.name, self.count = eng, S_(own), name, {}

            def __call__(self, ins, signal=None):
                s = self.own if signal is None else S_(signal)
                self.count[id(s)] = self.count.get(id(s), 0) + 1
                ins.then_inc(s, 1)
                self.eng.wait_ge(s, self.count[id(s)])

            def free(self, ins, stage, i=0):
                who, n = plan.took(stage, i)
                assert who == self.name
                ins.then_inc(took[who], 1)
                self.eng.wait_ge(took[who], n)

        def filled(eng, stage, i=0):
            eng.wait_ge(pe_filled, plan.mark(stage, i))
            return banks[:, plan.bank(stage, i), :]

        def after(eng, stage, i=0):
            who, n = plan.took(stage, i)
            eng.wait_ge(took[who], n)

        block = ctx.enter_context(nc.Block())

        @block.sync
        def _(sp):
            for n in range(len(tiles)):
                if n >= NSLOT:
                    stage, i = tiles[n - NSLOT]
                    sp.wait_ge(pe_filled, plan.first["down"][1] + i + 1 if stage == "down" else plan.mark(stage, i))
                sp.dma_start(W[:, n % NSLOT, :], io["weights"][n]).then_inc(tile_landed[n % NSLOT], 16)
            sp.wait_ge(S_("final_ready"), NT)
            sp.dma_start(io["out"].rearrange("b (t p) d -> p (b t) d", p=P), H[:]).then_inc(S_("out_written"), 16)
            sp.wait_ge(S_("out_written"), 16)

        @block.gpsimd
        def _(po):
            def row(dst, name, at=0, n=None):
                a, w = ROWS[name]
                n = n or w
                return po.dma_start(dst, io["rows"][0:1, a + at:a + at + n].to_broadcast([P, n]))

            po.dma_start(cols[:], io["cols"]).then_inc(S_("cols_in"), 16)
            row(mod.rearrange("p a b -> p (a b)"), "ada_b").then_inc(S_("ada_b_in"), 16)
            po.dma_start(rel_sb[:], io["rel_bias"]).then_inc(S_("rel_in"), 16)
            po.dma_start(onehot[:], io["onehot"]).then_inc(S_("onehot_in"), 16)
            po.dma_start(X[:], io["x"].rearrange("b (t p) d -> p (b t) d", p=P)).then_inc(S_("x_in"), 16)
            po.dma_start(const[:], io["const"]).then_inc(S_("const_in"), 16)
            row(gain[:, 0, :], "norm", 0, D).then_inc(S_("gain_in0"), 16)
            row(gain[:, 1, :], "norm", D, D).then_inc(S_("gain_in1"), 16)
            a, w = ROWS["gate_b"]
            row(b_rows, "gate_b", 0, 8 + 5 * BLK).then_inc(S_("b_rows_in"), 16)
            po.dma_start(small[:], io["small"]).then_inc(S_("small_in"), 16)
            po.dma_start(pos_i[:], io["pos"]).then_inc(S_("pos_in"), 16)
            po.wait_ge(S_("bias_rows_ready"), 1)
            po.dma_start(bias_scratch, rb_sb[:]).then_inc(S_("scratch_written"), 16)
            po.wait_ge(S_("h_ready"), NT)
            row(area(0, 2 * D), "b_g").then_inc(S_("b_g_in"), 16)
            po.wait_ge(S_("m_row_free"), 1)
            row(m_row, "m_norm").then_inc(S_("m_row_in"), 16)

            def load_gain(n):
                po.wait_ge(S_("h_ready"), NT * (n - 1))
                row(gain[:, n % 2, :], "norm", n * D, D).then_inc(S_(f"gain_in{n % 2}"), 16)

            load_gain(2)
            po.wait_ge(S_("h_ready"), 2 * NT)
            po.wait_ge(pe_filled, plan.mark("down", 3))
            po.dma_start(area(8712, NT, D), io["mem"].rearrange("b (t p) d -> p (b t) d", p=P)).then_inc(S_("mem_in"), 16)
            load_gain(3)
            load_gain(4)
            po.wait_ge(S_("h_ready"), 3 * NT)
            po.dma_start(e_inv.rearrange("p a b -> p (a b)"), io["pool_inv"]).then_inc(S_("inv_in"), 16)
            load_gain(5)
            load_gain(6)

            def gathers(layer):
                for phase in range(2 * NT):
                    table = io[("u", "v")[phase // NT] + str(layer)]
                    t = phase % NT
                    base = (layer * 2 * NT + phase) * SEL
                    if phase < NT:
                        po.wait_ge(S_("eid_ready"), NT * layer + t + 1)

                    def step(i):
                        for half in range(2):
                            g0 = base + HALF * half
                            if not (base == 0 and isinstance(i, int)):
                                po.wait_ge(rows_used, i * RING + (g0 - RING + HALF))
                            po.tensor_copy(stage_idx[:, half, :], p_eid[:, t, bass.ds(i * RING + HALF * half, HALF)])\
                                .then_inc(idx_staged, 1)
                            po.wait_ge(idx_staged, i * 2 + (base // HALF + half + 1))
                            if not isinstance(i, int):
                                po.sem_inc(S_("gather_turns"), 1)
                            for r in range(HALF):
                                po.indirect_dma_start(rows_u[:, half * HALF + r, :], None, table,
                                                      bass.IndirectOffsetOnAxis(ap=stage_idx[:, half, r:r + 1], axis=0))\
                                    .then_inc(row_landed[half * HALF + r], 16)

                    if base == 0:
                        step(0)
                    with po.Fori(1 if base == 0 else 0, SEL // RING) as i:
                        step(i)

            gathers(0)
            load_gain(7)
            load_gain(8)
            po.wait_ge(S_("x_ready"), NT)
            row(lb_row.rearrange("p a b -> p (a b)"), "gamma").then_inc(S_("odd_in"), 16)
            row(h_row, "hg_norm").then_inc(S_("odd_in"), 16)
            row(kv_row, "kv_norm").then_inc(S_("odd_in"), 16)
            po.dma_start(h_mask.rearrange("p a b -> p (a b)"), io["masks"]).then_inc(S_("odd_in"), 16)
            po.wait_ge(S_("hgrn_done"), 1)
            po.wait_ge(S_("scratch_written"), 16)
            for t in range(NT):
                src = bass.AP(tensor=bias_scratch.tensor, offset=P * (1 - t), ap=[[1, P], [2 * S, 8], [1, S]])
                po.dma_start(hankel[:, t, :].rearrange("p (h s) -> p h s", h=8), src).then_inc(S_("hankel_in"), 16)
            load_gain(9)
            gathers(1)
            load_gain(10)

        @block.tensor
        def _(pe):
            def claim(stage, i=0):
                b = plan.before(stage, i)
                if b:
                    pe.wait_ge(took[b[0]], b[1])
                return banks[:, plan.bank(stage, i), :]

            def tile(n):
                pe.wait_ge(tile_landed[n % NSLOT], 16 * (n // NSLOT + 1))
                return W[:, n % NSLOT, :]

            def std(n):
                return tile(n).rearrange("p (k n) -> p k n", k=KD)

            def transposes(stage, blocks, wait):
                i = 0
                for t in range(NT):
                    for g in range(len(blocks) // 4):
                        wait(t)
                        bank = claim(stage, i)
                        for j in range(4):
                            mm = pe.transpose(bank[:, j * P:(j + 1) * P], blocks[4 * g + j](t), ident)
                        mm.then_inc(pe_filled, 1)
                        i += 1

            def norm_T(n):
                transposes(f"T{n}", [lambda t, b=b: H[:, t, b * P:(b + 1) * P] for b in range(KD)],
                           lambda t: pe.wait_ge(S_("h_ready"), NT * n + t + 1))

            def transposed(stage, n_tiles, act, first=None):
                first = tile_no[stage] if first is None else first
                for i in range(2 * n_tiles):
                    w = std(first + i // 2)
                    bank = claim(stage, i)
                    for b in range(2):
                        c = (i % 2 * 2 + b) * P
                        for k in range(KD):
                            mm = pe.matmul(bank[:, b * S:(b + 1) * S], w[:, k, c:c + P], act[:, k, :],
                                           start=(k == 0), stop=(k == KD - 1))
                    mm.then_inc(pe_filled, 1)

            def natural(stage, n_tiles, act):
                for i in range(2 * n_tiles):
                    w = std(tile_no[stage] + i // 2)
                    bank = claim(stage, i)
                    for k in range(KD):
                        mm = pe.matmul(bank, act[:, k, (i % 2) * P:(i % 2 + 1) * P], w[:, k, :],
                                       start=(k == 0), stop=(k == KD - 1))
                    mm.then_inc(pe_filled, 1)

            def attend(name, units, scores, n_keys, probs_sem, base):
                def score(u):
                    mm = scores(u, claim(f"{name}_s{u}"))
                    mm.then_inc(pe_filled, 1)
                score(0)
                for u, (p, t) in enumerate(units):
                    if u + 1 < len(units):
                        score(u + 1)
                    pe.wait_ge(S_(probs_sem), base + u + 1)
                    bank = claim(f"{name}_t{u}")
                    kt = n_keys(t)
                    for h in range(2):
                        for s in range(kt):
                            mm = pe.transpose(bank[:, (h * NT + s) * P:(h * NT + s + 1) * P],
                                              probs[:, u % 2, h * S + s * P:h * S + (s + 1) * P], ident)
                    mm.then_inc(pe_filled, 1)

            def weighted(stage, i, t, heads, PT, values, width, n_keys, last, slot=lambda h: h):
                after(pe, last)
                bank = claim(stage, i)
                for j, h in enumerate(heads):
                    for s in range(n_keys(t)):
                        mm = pe.matmul(bank[:, j * width:(j + 1) * width], PT[:, slot(h), s, t * P:(t + 1) * P],
                                       values(h, s),
                                       start=(s == 0), stop=(s == n_keys(t) - 1))
                mm.then_inc(pe_filled, 1)

            causal_keys = lambda t: t + 1
            all_keys = lambda t: NT

            pe.wait_ge(S_("rel_in"), 16)
            pe.wait_ge(S_("onehot_in"), 16)
            pe.matmul(claim("bias_rows")[0:8, :], rel_sb[:], onehot[:], start=True, stop=True).then_inc(pe_filled, 1)
            pe.wait_ge(S_("c_ready"), 1)
            for i in range(12):
                w = std(i)
                bank = claim("ada", i)
                for k in range(KD):
                    mm = pe.matmul(bank, HT[:, k, 0:P], w[:, k, :], start=(k == 0), stop=(k == KD - 1))
                mm.then_inc(pe_filled, 1)
            pe.wait_ge(S_("const_in"), 16)
            norm_T(0)
            after(pe, "T0", 3)
            transposed("z_qk", 2, HT)
            pe.wait_ge(S_("small_in"), 16)
            bank = claim("z_gate")
            wg = part(small, SMALL, "gates").rearrange("p (k n) -> p k n", k=KD)
            for t in range(NT):
                for k in range(KD):
                    mm = pe.matmul(bank[:, t * 8:(t + 1) * 8], HT[:, k, t * P:(t + 1) * P], wg[:, k, :],
                                   start=(k == 0), stop=(k == KD - 1))
            mm.then_inc(pe_filled, 1)
            natural("z_n", 5, HT)
            pe.wait_ge(S_("logf_ready"), 1)
            lf, gcol = stat(0, NT, 4), stat(16, NT, 4)
            bank = claim("m_cum")
            pe.matmul(bank[:, 0:4], tri, lf[:, 0, :], start=True, stop=True)
            pe.matmul(bank[:, 4:8], tri, lf[:, 1, :], start=True, stop=False)
            pe.matmul(bank[:, 4:8], ones, lf[:, 0, :], start=False, stop=True).then_inc(pe_filled, 1)
            pe.wait_ge(S_("g_ready"), 1)
            for p in range(2):
                bank = claim(f"m_g{p}")
                for h in range(2):
                    for t in range(NT):
                        g = gcol[:, t, 2 * p + h:2 * p + h + 1]
                        mm = pe.transpose(bank[:, h * S + t * P:h * S + (t + 1) * P], g.to_broadcast([P, P]), ident)
                mm.then_inc(pe_filled, 1)
            pe.wait_ge(S_("qk_ready"), 1)
            m_units = [(p, t) for p in range(2) for t in range(NT)]

            def m_scores(u, bank):
                p, t = m_units[u]
                for h in range(2):
                    mm = pe.matmul(bank[:, h * S:(h + 1) * S], qkT[:, 2 * p + h, t * P:(t + 1) * P],
                                   qkT[:, 4 + 2 * p + h, :], start=True, stop=True)
                return mm
            attend("m", m_units, m_scores, causal_keys, "m_probs", 0)
            for t in range(NT):
                weighted("m_pv", t, t, range(MH), PT1, lambda h, s: Z[:, s, MV + h * MDH:MV + (h + 1) * MDH], MDH,
                         causal_keys, "m_t3")
            transposes("a_T", [lambda t, b=b: Z[:, t, AQ + b * P:AQ + (b + 1) * P] for b in range(8)],
                       lambda t: pe.wait_ge(S_("rope_done"), 1))
            after(pe, "a_T", 3)
            a_units = [(p, t) for p in range(4) for t in range(NT)]

            def a_scores(u, bank):
                p, t = a_units[u]
                for h in range(2):
                    b, q = place_of(2 * p + h, ADH)
                    mm = pe.matmul(bank[:, h * S:(h + 1) * S], aT[q, b, t * P:(t + 1) * P], aT[q, 4 + b, :],
                                   start=True, stop=True)
                return mm
            attend("a", a_units, a_scores, causal_keys, "probs_ready", 0)
            for t in range(NT):
                weighted("a_pv", t, t, range(AH), PT1, lambda h, s: Z[:, s, AV + h * ADH:AV + (h + 1) * ADH], ADH,
                         causal_keys, "a_t7", slot=head_of)
            transposes("y_T", [lambda t, b=b: Z[:, t, MO + b * P:MO + (b + 1) * P] for b in range(8)],
                       lambda t: pe.wait_ge(S_("y_ready"), NT))
            after(pe, "y_T", 3)
            for c in range(2):
                n = tile_no["merge"] + 3 * c
                for j in range(4):
                    w = std(n + j // 2)
                    bank = claim("merge", 8 * c + j)
                    for k in range(KD):
                        mm = pe.matmul(bank, HT[:, k, (j % 2) * P:(j % 2 + 1) * P], w[:, k, :],
                                       start=(k == 0), stop=(k == KD - 1))
                    mm.then_inc(pe_filled, 1)
                w = std(n + 2)
                for j in range(4):
                    t, m = j // 2, j % 2
                    bank = claim("merge", 8 * c + 4 + j)
                    for k in range(4):
                        mm = pe.matmul(bank, yT[:, 4 * m + k, t * P:(t + 1) * P], w[:, 4 * m + k, :],
                                       start=(k == 0), stop=(k == 3))
                    mm.then_inc(pe_filled, 1)
            transposes("mg_T", [lambda t, b=b: H[:, t, b * P:(b + 1) * P] for b in range(KD)],
                       lambda t: pe.wait_ge(S_("merged_ready"), 4))
            after(pe, "mg_T", 3)
            natural("w_out", 2, HT)
            norm_T(1)
            after(pe, "T1", 3)
            for i in range(NF // 2):
                w = std(tile_no["ff_u0"] + i)
                for stage, c0 in ((f"ff_g{i}", 0), (f"ff_u{i}", 2 * P)):
                    bank = claim(stage)
                    for b in range(2):
                        for k in range(KD):
                            mm = pe.matmul(bank[:, b * S:(b + 1) * S], w[:, k, c0 + b * P:c0 + (b + 1) * P], HT[:, k, :],
                                           start=(k == 0), stop=(k == KD - 1))
                    mm.then_inc(pe_filled, 1)
            for i in range(4):
                claim("down", i)
            after(pe, f"ff_u{NF // 2 - 1}")
            pe.wait_ge(S_("f_ready"), NF // 2)
            for i in range(6):
                w = tile(tile_no["down"] + i).rearrange("p (k n) -> p k n", k=4)
                for j in range(min(4, NF - 4 * i)):
                    k = 4 * i + j
                    for t in range(NT):
                        for c in range(2):
                            mm = pe.matmul(banks[:, plan.bank("down", 2 * c + t), :], fT[:, k, t * P:(t + 1) * P],
                                           w[:, j, c * BLK:(c + 1) * BLK], start=(k == 0), stop=(k == NF - 1))
                mm.then_inc(pe_filled, 1)
            norm_T(2)
            norm_T(4)
            after(pe, "T4", 3)
            transposed("e_z", 4, HT)
            pe.wait_ge(S_("pooled_ready"), 1)
            pw = part(small, SMALL, "pool_w").rearrange("p (g n) -> p g n", g=4)
            for i in range(2):
                bank = claim("e_pool", i)
                for b in range(2):
                    mm = pe.matmul(bank[:, b * S:(b + 1) * S], pw[:, 2 * i + b, :], e_pool[:, 2 * i + b, :],
                                   start=True, stop=True)
                mm.then_inc(pe_filled, 1)
            after(pe, "e_pool", 1)
            natural("e_out", 2, e_yT)

            def odd():
                norm_T(7)
                after(pe, "T7", 3)
                transposed("o_ql", 2, HT)
                w = std(tile_no["o_ik"])
                bank = claim("o_ckv")
                for t in range(NT):
                    for a, b, n in ((0, 0, P), (P, 2 * P, 8)):
                        for k in range(KD):
                            mm = pe.matmul(bank[:, t * (P + 8) + a:t * (P + 8) + a + n], HT[:, k, t * P:(t + 1) * P],
                                           w[:, k, b:b + n], start=(k == 0), stop=(k == KD - 1))
                mm.then_inc(pe_filled, 1)
                bank = claim("o_ik")
                for k in range(KD):
                    mm = pe.matmul(bank[:, 0:S], w[:, k, P:2 * P], HT[:, k, :], start=(k == 0), stop=(k == KD - 1))
                mm.then_inc(pe_filled, 1)
                transposed("o_iq", 1, HT)
                transposed("o_hq", 1, HT)
                natural("o_hf", 1, HT)
                natural("o_hi", 1, HT)
                natural("o_hg", 1, HT)
                pe.wait_ge(S_("ckv_ready"), 1)
                bank = claim("o_cT")
                for t in range(NT):
                    mm = pe.transpose(bank[:, t * P:(t + 1) * P], o_c[:, t, 0:P], ident)
                mm.then_inc(pe_filled, 1)
                transposes("o_kT", [lambda t, b=b: h_kn[:, t, b * P:(b + 1) * P] for b in range(4)],
                           lambda t: pe.wait_ge(S_("forget_ready"), NT))
                pe.wait_ge(S_("hlog_ready"), NT)
                pe.wait_ge(S_("odd_in"), 64)
                after(pe, "o_kT", 1)
                for n, h in enumerate(LEVELS):
                    for i in range(2):
                        bank = claim(f"h_d{n}", i)
                        for j in range(2):
                            for t in range(NT):
                                m = h_mask[:, t if h == P else 2 * n, :]
                                hd = 2 * i + j
                                mm = pe.matmul(bank[:, j * S + t * P:j * S + (t + 1) * P],
                                               h_f[:, t, hd * P:(hd + 1) * P], m, start=True, stop=True)
                        mm.then_inc(pe_filled, 1)
                    pe.wait_ge(S_("level_ready"), n + 1)
                    for i in range(1 if h == P else NT):
                        bank = claim(f"h_s{n}", i)
                        for hd in range(HH):
                            s = slice(i * P, (i + 1) * P)
                            q = slice(P, 2 * P) if h == P else s
                            mm = pe.matmul(bank[:, hd * P:(hd + 1) * P], h_KE[:, hd, s], h_QE[:, hd, q],
                                           start=True, stop=True)
                        mm.then_inc(pe_filled, 1)
                for t in range(NT):
                    bank = claim("h_diag", t)
                    for hd in range(HH):
                        mm = pe.matmul(bank[:, hd * P:(hd + 1) * P], h_kT[:, hd, t * P:(t + 1) * P],
                                       h_qT[:, hd, t * P:(t + 1) * P], start=True, stop=True)
                    mm.then_inc(pe_filled, 1)
                pe.wait_ge(S_("hscores_ready"), NT)
                for t in range(NT):
                    bank = claim("h_pv", t)
                    for hd in range(HH):
                        d = slice(hd * P, (hd + 1) * P)
                        mm = pe.matmul(bank[:, d], h_sc[:, t, hd, :], h_i[:, t, d], start=True, stop=(t == 0))
                        if t:
                            mm = pe.matmul(bank[:, d], h_x[:, hd, :], h_i[:, 0, d], start=False, stop=True)
                    mm.then_inc(pe_filled, 1)
                for u in range(8):
                    t, p = u // 4, u % 4
                    bank = claim("idx", u)
                    for h in range(2):
                        b, q = place_of(2 * p + h, IDH)
                        mm = pe.matmul(bank[:, h * S:(h + 1) * S], o_iqT[q, b, t * P:(t + 1) * P], o_ikT[q, :],
                                       start=True, stop=True)
                    mm.then_inc(pe_filled, 1)
                o_units = [(p, t) for t in range(NT) for p in range(4)]
                pe.wait_ge(S_("hankel_in"), 32)

                def o_scores(u, bank):
                    p, t = o_units[u]
                    for h in range(2):
                        hd = 2 * p + h
                        pe.matmul(bank[:, h * S:(h + 1) * S], o_qT[:, hd, t * P:(t + 1) * P], o_cT,
                                  start=True, stop=False)
                        mm = pe.matmul(bank[:, h * S:(h + 1) * S], flip, hankel[:, t, hd * S:(hd + 1) * S],
                                       start=False, stop=True)
                    return mm
                attend("o", o_units, o_scores, causal_keys, "probs_ready", 12)
                for i in range(4):
                    t, g = i // 2, i % 2
                    weighted("o_pv", i, t, range(4 * g, 4 * g + 4), o_PT, lambda h, s: o_c[:, s, 0:P], P,
                             causal_keys, "o_t7")
                transposes("lat_T", [lambda t, b=b: H[:, t, b * P:(b + 1) * P] for b in range(KD)],
                           lambda t: after(pe, "o_pv", 2 * t + 1))
                after(pe, "lat_T", 3)
                uv = part(small, SMALL, "w_uv").rearrange("p (h n) -> p h n", h=CH)
                for t in range(NT):
                    bank = claim("o_yc", t)
                    for h in range(CH):
                        mm = pe.matmul(bank[:, h * CDH:(h + 1) * CDH], HT[:, h, t * P:(t + 1) * P], uv[:, h, :],
                                       start=True, stop=True)
                    mm.then_inc(pe_filled, 1)
                transposes("o_yT", [lambda t, b=b: H[:, t, b * P:(b + 1) * P] if b < 4 else
                                    yd[:, t, (b - 4) * P:(b - 3) * P] for b in range(KD)],
                           lambda t: after(pe, "o_yc", t))
                after(pe, "o_yT", 3)
                natural("o_out", 2, HT)

            for l in range(2):
                if l:
                    odd()
                transposed(f"x_k{l}", 2, memT)
                natural(f"x_v{l}", 2, memT)
                norm_T(5 + 3 * l)
                after(pe, f"T{5 + 3 * l}", 3)
                transposed(f"x_q{l}", 2, HT)
                after(pe, f"x_q{l}", 3)
                x_units = [(p, t) for p in range(2) for t in range(NT)]

                def x_scores(u, bank):
                    p, t = x_units[u]
                    for h in range(2):
                        for j in range(2):
                            b = 2 * (2 * p + h) + j
                            mm = pe.matmul(bank[:, h * S:(h + 1) * S], x_qT[:, b, t * P:(t + 1) * P], x_kT[:, b, :],
                                           start=(j == 0), stop=(j == 1))
                    return mm
                attend(f"x{l}", x_units, x_scores, all_keys, "probs_ready", 8 + 12 * l)
                for i in range(4):
                    t, g = i // 2, i % 2
                    weighted(f"x_pv{l}", i, t, (2 * g, 2 * g + 1), x_PT,
                             lambda h, s: x_v[:, s, h * XDH:(h + 1) * XDH], XDH, all_keys, f"x{l}_t3")
                transposes(f"x_oT{l}", [lambda t, b=b: H[:, t, b * P:(b + 1) * P] for b in range(KD)],
                           lambda t: after(pe, f"x_pv{l}", 2 * t + 1))
                after(pe, f"x_oT{l}", 3)
                natural(f"x_o{l}", 2, HT)
                norm_T(6 + 3 * l)
                after(pe, f"T{6 + 3 * l}", 3)
                transposed(f"p_q{l}", 4, HT)
                keys = tile(tile_no[f"p_s{l}"])
                after(pe, f"p_q{l}", 7)
                for i in range(8):
                    bank = claim(f"p_s{l}", i)
                    t = i // 4
                    for j in range(4):
                        b = 4 * (i % 4) + j
                        mm = pe.matmul(bank[:, j * P:(j + 1) * P], p_qT[:, b, t * P:(t + 1) * P],
                                       keys[:, b * NK:(b + 1) * NK], start=True, stop=True)
                    mm.then_inc(pe_filled, 1)

        @block.scalar
        def _(act):
            step = Steps(act, "scalar_step", "scalar")

            def rstd(n_heads, sums, out, width, signal=None):
                step(act.activation(out, sums, ACT.Ln, scale=1.0 / width, bias=eps_col))
                step(act.activation(out, out, ACT.Exp, scale=-0.5), signal)

            eps_col = stat(600, 1)

            def norm(n, src, ready):
                for t in range(NT):
                    ready(t)
                    at = n % 2 * NT + t
                    step(act.activation(junk[:], src[:, t, :], ACT.Square, accum_out=stat(604 + at, 1)))
                    rstd(1, stat(604 + at, 1), stat(608 + at, 1), D, "rstd_ready")

            def attend(name, units, scale, PT, n_keys, base, sums):
                def probabilities(u):
                    p, t = units[u]
                    act.wait_ge(S_("smax_ready"), base + u + 1)
                    for h in range(2):
                        hd = 2 * p + h
                        step(act.activation(probs[:, u % 2, h * S:(h + 1) * S], scrA[:, u % 2, h * S:(h + 1) * S], ACT.Exp,
                                            bias=stat(612 + 2 * (u % 2) + h, 1), scale=scale,
                                            accum_out=sums[:, t, hd:hd + 1]), "probs_ready" if h else None)
                probabilities(0)
                for u, (p, t) in enumerate(units):
                    if u + 1 < len(units):
                        probabilities(u + 1)
                    leave(name, u, p, t, PT, n_keys)

            def leave(name, u, p, t, PT, n_keys):
                bank = filled(act, f"{name}_t{u}")
                kt = n_keys(t)
                src = bank.rearrange("p (h s t) -> p h s t", h=2, s=NT)[:, :, 0:kt, :]
                step.free(act.activation(PT[:, 2 * p:2 * p + 2, 0:kt, t * P:(t + 1) * P], src, ACT.Copy),
                          f"{name}_t{u}")

            act.wait_ge(S_("cols_in"), 16)
            step(act.activation(stat(620, 8), part(cols, COLS, "c"), ACT.Silu), "silu_c")
            act.wait_ge(S_("eps_set"), 1)
            act.wait_ge(S_("x_in"), 16)
            norm(0, X, lambda t: None)
            act.wait_ge(S_("conv_ready"), 1)
            step(act.activation(qkT, qkT, ACT.Silu), "qk_ready")
            act.wait_ge(S_("mo_ready"), NT)
            for t in range(NT):
                step(act.activation(Z[:, t, MO:MO + MW], Z[:, t, MO:MO + MW], ACT.Sigmoid), "mo_gated")
            act.wait_ge(S_("absf_ready"), 1)
            step(act.activation(stat(32, 8), stat(32, 8), ACT.Exp, scale=-1.0))
            step(act.activation(stat(32, 8), stat(32, 8), ACT.Ln, bias=1.0), "log1p_ready")
            m_units = [(p, t) for p in range(2) for t in range(NT)]
            for u, (p, t) in enumerate(m_units):
                act.wait_ge(S_("m_max_ready"), u + 1)
                for h in range(2):
                    step(act.activation(scrA[:, u % 2, h * S:(h + 1) * S], scrA[:, u % 2, h * S:(h + 1) * S], ACT.Exp,
                                        bias=stat(64 + 4 * t + 2 * p + h, 1)), "m_w_ready" if h else None)
                if u:
                    leave("m", u - 1, *m_units[u - 1], PT1, lambda t: t + 1)
            leave("m", 3, *m_units[3], PT1, lambda t: t + 1)
            act.wait_ge(S_("m_stab_ready"), 1)
            step(act.activation(stat(80, 8), stat(80, 8), ACT.Exp, scale=-1.0), "m_floor_ready")
            act.wait_ge(S_("hm_squares"), 1)
            rstd(MH, stat(96, 8), stat(104, 8), MDH, "hm_rstd")
            act.wait_ge(S_("angle_ready"), 1)
            step(act.activation(stat(128, 128), stat(128, 128), ACT.Sin), "sincos_ready")
            a_units = [(p, t) for p in range(4) for t in range(NT)]
            attend("a", a_units, ADH ** -0.5, PT1, lambda t: t + 1, 0, stat(272, NT, 8))
            for c in range(2):
                act.wait_ge(S_("gate_pre"), c + 1)
                step(act.activation(sg, sg, ACT.Sigmoid), "gate_ready")
            norm(1, X, lambda t: after(act, "w_out", 2 + t))
            for i in range(NF // 2):
                bank = filled(act, f"ff_g{i}")
                if i >= 2:
                    act.wait_ge(S_("f_ready"), i - 1)
                step.free(act.activation(silu_g[:, i % 2, :], bank, ACT.Silu), f"ff_g{i}")
            act.wait_ge(S_("mem_in"), 16)
            norm(2, area(8712, NT, D), lambda t: None)
            norm(3, X, lambda t: after(act, "down", 2 + t))
            norm(4, X, lambda t: act.wait_ge(S_("h_ready"), 3 * NT + t + 1))
            for l in range(2):
                if l:
                    norm(7, X, lambda t: act.wait_ge(S_("x_ready"), t + 1))
                    for t in range(NT):
                        bank = filled(act, "o_hf", t)
                        step.free(act.activation(h_f[:, t, :], bank, ACT.Sigmoid), "o_hf", t)
                    act.wait_ge(S_("hg_in"), NT)
                    for t in range(NT):
                        step(act.activation(h_g[:, t, :], h_g[:, t, :], ACT.Silu), "hg_ready")
                    act.wait_ge(S_("lb_diff"), 1)
                    step(act.activation(lb_row[:, 0, :], lb_row[:, 0, :], ACT.Exp))
                    step(act.activation(lb_row[:, 1, :], lb_row[:, 1, :], ACT.Exp), "lb_exp")
                    act.wait_ge(S_("ckv_squares"), 1)
                    rstd(1, stat(288, 2), stat(290, 2), CR, "ckv_rstd")
                    for t in range(NT):
                        act.wait_ge(S_("forget_ready"), t + 1)
                        step(act.activation(h_f[:, t, :], h_f[:, t, :], ACT.Ln), "hlog_ready")
                    for n in range(len(LEVELS)):
                        for i in range(2):
                            bank = filled(act, f"h_d{n}", i)
                            if n:
                                act.wait_ge(S_("level_ready"), n)
                            step.free(act.activation(h_E[:, 2 * i:2 * i + 2, :].rearrange("p a b -> p (a b)"), bank,
                                                     ACT.Exp), f"h_d{n}", i)
                    act.wait_ge(S_("yd_squares"), 1)
                    rstd(HH, stat(296, 8), stat(304, 8), P, "yd_rstd")
                    for u in range(8):
                        bank = filled(act, "idx", u)
                        if u >= 2:
                            act.wait_ge(S_("rel_used"), u - 1)
                        if u == 0:
                            act.wait_ge(S_("hgrn_done"), 1)
                        step.free(act.activation(o_rel[:, u % 2, :], bank, ACT.Relu, scale=IDH ** -0.5), "idx", u)
                    attend("o", [(p, t) for t in range(NT) for p in range(4)], 1.0, o_PT, lambda t: t + 1, 12,
                           stat(272, NT, 8))
                norm(5 + 3 * l, X, lambda t: after(act, "o_out" if l else "e_out", 2 + t))
                attend(f"x{l}", [(p, t) for p in range(2) for t in range(NT)], XDH ** -0.5, x_PT, lambda t: NT,
                       8 + 12 * l, stat(272, NT, 8))
                norm(6 + 3 * l, X, lambda t: after(act, f"x_o{l}", 2 + t))
                for t in range(NT):
                    act.wait_ge(S_("top_ready"), NT * l + t + 1)
                    step(act.activation(p_g[:, t, :], p_g[:, t, :], ACT.Exp), "top_exp")
                for t in range(NT):
                    act.wait_ge(S_("dots_ready"), NT * l + t + 1)
                    step(act.activation(p_act[:, t, :], p_act[:, t, :], ACT.Gelu_apprx_tanh), "gelu_ready")
            norm(10, X, lambda t: act.wait_ge(S_("x_ready"), NT + t + 1))

        @block.vector
        def _(v):
            step = Steps(v, "vector_step", "vector")

            def tt(out, a, b, op, signal=None):
                step(v.tensor_tensor(out, a, b, op), signal)

            def ts(out, a, s1, op0, s2=None, op1=None, signal=None):
                step(v.tensor_scalar(out, a, s1, s2, op0, op1) if op1 else v.tensor_scalar(out, a, s1, None, op0), signal)

            def stt(out, a, s, b, op0, op1, signal=None, accum=None):
                step(v.scalar_tensor_tensor(out=out, in0=a, scalar=s, in1=b, op0=op0, op1=op1, accum_out=accum), signal)

            def norm(n, src, g, shift=None, signal="h_ready", dst=H):
                for t in range(NT):
                    v.wait_ge(S_("rstd_ready"), NT * n + t + 1)
                    stt(dst[:, t, :], src[:, t, :], stat(608 + n % 2 * NT + t, 1), g, ALU.mult, ALU.mult,
                        signal if shift is None else None)
                    if shift is not None:
                        tt(H[:, t, :], H[:, t, :], shift, ALU.add, signal)

            def gain_of(n):
                v.wait_ge(S_(f"gain_in{n % 2}"), 16 * (n // 2 + 1))
                return gain[:, n % 2, :]

            def take_T(stage, dst, n_blocks=KD):
                i = 0
                for t in range(NT):
                    for g in range(n_blocks // 4):
                        bank = filled(v, stage, i)
                        step.free(v.tensor_copy(dst[:, 4 * g:4 * g + 4, t * P:(t + 1) * P],
                                                bank.rearrange("p (b t) -> p b t", b=4)), stage, i)
                        i += 1

            def take_blocks(stage, n, dst, scale=None):
                for i in range(n):
                    bank = filled(v, stage, i).rearrange("p (b t) -> p b t", b=2)
                    out = dst[:, 2 * i:2 * i + 2, :]
                    ins = v.tensor_copy(out, bank) if scale is None else v.tensor_scalar(out, bank, scale, None, ALU.mult)
                    step.free(ins, stage, i)

            def softmax_max(name, units, mask, scale):
                for u, (p, t) in enumerate(units):
                    bank = filled(v, f"{name}_s{u}").rearrange("p (h s) -> p h s", h=2)
                    out = scrA[:, u % 2, :].rearrange("p (h s) -> p h s", h=2)
                    if u >= 2:
                        v.wait_ge(S_("probs_ready"), self_base[0] + u - 1)
                    if mask is None:
                        ins = v.tensor_copy(out, bank)
                    else:
                        ins = v.tensor_tensor(out, bank, mask(t).unsqueeze(1).to_broadcast([P, 2, S]), ALU.add)
                    step.free(ins, f"{name}_s{u}")
                    step(v.tensor_reduce(stat(616, 2), out, AXX, ALU.max))
                    ts(stat(612 + 2 * (u % 2), 2), stat(616, 2), -scale, ALU.mult, signal="smax_ready")
                self_base[0] += len(units)
            self_base = [0]

            def take_weighted(stage, i, out, sums, width, ready=None):
                n = out.shape[-1] // width
                bank = filled(v, stage, i)
                r = stat(640 - 8, n)
                if len(sums.shape) == 4:
                    r = r.rearrange("p (a b c) -> p a b c", b=2, c=2)
                step(v.reciprocal(r, sums))
                step.free(v.tensor_tensor(out.rearrange("p (h d) -> p h d", h=n), bank.rearrange("p (h d) -> p h d", h=n),
                                          stat(640 - 8, n).unsqueeze(2).to_broadcast([P, n, width]), ALU.mult), stage, i)

            def head_norm(x, heads, squares, tmp, t):
                tt(tmp, x, x, ALU.mult)
                step(v.tensor_reduce(squares[:, t, :], tmp.rearrange("p (h d) -> p h d", h=heads), AXX, ALU.add))

            def add_to_x(stage, scale=None):
                for i in range(4):
                    c, t = i // 2, i % 2
                    xs = X[:, t, c * BLK:(c + 1) * BLK]
                    bank = filled(v, stage, i)
                    if scale is None:
                        step.free(v.tensor_tensor(xs, bank, xs, ALU.add), stage, i)
                    else:
                        step(v.tensor_tensor(junk_v, bank, scale[:, c * BLK:(c + 1) * BLK], ALU.mult))
                        step.free(v.tensor_tensor(xs, junk_v, xs, ALU.add), stage, i)

            junk_v = area(22048, 512)
            step(v.memset(stat(600, 1), EPS), "eps_set")
            bank = filled(v, "bias_rows")
            step.free(v.tensor_copy(rb_sb[:], bank[0:8, :]), "bias_rows")
            step(v.tensor_copy(rb_sb[:, 0:1], rb_sb[:, 0:1]), "bias_rows_ready")
            v.wait_ge(S_("silu_c"), 1)
            step(v.tensor_copy(HT[:, :, 0:P], stat(620, 8).unsqueeze(2).to_broadcast([P, KD, P])), "c_ready")
            v.wait_ge(S_("ada_b_in"), 16)
            modf = mod.rearrange("p a b -> p (a b)")
            for i in range(12):
                m = modf[:, i * BLK:(i + 1) * BLK]
                bank = filled(v, "ada", i)
                step.free(v.tensor_tensor(m, bank, m, ALU.add), "ada", i)
            for n in range(2):
                stt(mod[:, 1 + 3 * n, :], mod[:, 1 + 3 * n, :], 1.0, gain_of(n), ALU.add, ALU.mult)
            norm(0, X, mod[:, 1, :], mod[:, 0, :])
            take_T("T0", HT)
            step(v.memset(qk_raw[:, :, 0:3], 0.0))
            bq = part(cols, COLS, "b_qk")
            for i in range(4):
                bank = filled(v, "z_qk", i)
                step(v.tensor_scalar(qk_raw[:, 2 * i, 3:], bank[:, 0:S], bq[:, 2 * i:2 * i + 1], None, ALU.add))
                step.free(v.tensor_scalar(qk_raw[:, 2 * i + 1, 3:], bank[:, S:2 * S], bq[:, 2 * i + 1:2 * i + 2], None,
                                          ALU.add), "z_qk", i)
            v.wait_ge(S_("b_rows_in"), 16)
            bank = filled(v, "z_gate")
            gates = stat(48, NT, 8)
            step.free(v.tensor_tensor(gates, bank[:, 0:16].rearrange("p (t g) -> p t g", t=NT),
                                      b_rows[:, 0:8].unsqueeze(1).to_broadcast([P, NT, 8]), ALU.add), "z_gate")
            absf = stat(32, NT, 4)
            stt(absf, gates[:, :, 4:8], -1.0, gates[:, :, 4:8], ALU.mult, ALU.max, "absf_ready")
            cw, cb = part(cols, COLS, "conv_w"), part(cols, COLS, "conv_b")
            for b in range(8):
                ts(qkT[:, b, :], qk_raw[:, b, 0:S], cw[:, b:b + 1], ALU.mult, cb[:, b:b + 1], ALU.add)
                for j in range(1, 4):
                    stt(qkT[:, b, :], qk_raw[:, b, j:j + S], cw[:, 8 * j + b:8 * j + b + 1], qkT[:, b, :],
                        ALU.mult, ALU.add, "conv_ready" if (b, j) == (7, 3) else None)
            for i in range(10):
                f, t = i // 2, i % 2
                bank = filled(v, "z_n", i)
                step.free(v.tensor_tensor(Z[:, t, f * BLK:(f + 1) * BLK], bank, b_rows[:, 8 + f * BLK:8 + (f + 1) * BLK],
                                          ALU.add), "z_n", i)
                if f == 1:
                    step(v.tensor_copy(Z[:, t, MO:MO + 1], Z[:, t, MO:MO + 1]), "mo_ready")
            v.wait_ge(S_("log1p_ready"), 1)
            lf, gcol, cum = stat(0, NT, 4), stat(16, NT, 4), stat(24, NT, 4)
            stt(lf, gates[:, :, 4:8], 0.0, absf, ALU.min, ALU.subtract, "logf_ready")
            bank = filled(v, "m_cum")
            step.free(v.tensor_copy(cum, bank[:, 0:8].rearrange("p (t g) -> p t g", t=NT)), "m_cum")
            tt(gcol, gates[:, :, 0:4], cum, ALU.subtract, "g_ready")
            negM = stat(64, NT, 4)
            m_units = [(p, t) for p in range(2) for t in range(NT)]
            den = stat(88, NT, 4)
            g_row = area(18976 + 1024, 2, 512)
            for p in range(2):
                bank = filled(v, f"m_g{p}")
                step.free(v.tensor_copy(g_row[:, p, :], bank), f"m_g{p}")

            def m_log(u):
                p, t = m_units[u]
                w = scrA[:, u % 2, :].rearrange("p (h s) -> p h s", h=2)
                tt(w, g_row[:, p, :].rearrange("p (h s) -> p h s", h=2),
                   causal[:, t, :].unsqueeze(1).to_broadcast([P, 2, S]), ALU.add)
                step(v.tensor_reduce(stat(616, 2), w, AXX, ALU.max))
                ts(negM[:, t, 2 * p:2 * p + 2], stat(616, 2), 0.0, ALU.max, -1.0, ALU.mult, signal="m_max_ready")

            m_log(0)
            for u, (p, t) in enumerate(m_units):
                if u + 1 < 4:
                    m_log(u + 1)
                v.wait_ge(S_("m_w_ready"), u + 1)
                bank = filled(v, f"m_s{u}")
                if u >= 2:
                    v.wait_ge(pe_filled, plan.mark(f"m_t{u - 2}"))
                for h in range(2):
                    c = slice(h * S, (h + 1) * S)
                    ins = v.scalar_tensor_tensor(out=probs[:, u % 2, c], in0=bank[:, c], scalar=MDH ** -0.5,
                                                 in1=scrA[:, u % 2, c], op0=ALU.mult, op1=ALU.mult,
                                                 accum_out=den[:, t, 2 * p + h:2 * p + h + 1])
                    if h:
                        step.free(ins, f"m_s{u}")
                    else:
                        step(ins)
                step(v.tensor_copy(probs[:, u % 2, 0:1], probs[:, u % 2, 0:1]), "m_probs")
            step(v.memset(junk_v[:, 0:1], 0.0), "m_row_free")
            floor = stat(80, NT, 4)
            tt(floor, cum, negM, ALU.subtract, "m_stab_ready")
            stt(den, den, -1.0, den, ALU.mult, ALU.max)
            v.wait_ge(S_("m_floor_ready"), 1)
            tt(den, den, floor, ALU.max)
            step(v.reciprocal(den, den))
            hm = area(23072, NT, 512)
            sq = stat(96, NT, 4)
            for t in range(NT):
                bank = filled(v, "m_pv", t)
                step.free(v.tensor_tensor(hm[:, t, :].rearrange("p (h d) -> p h d", h=MH),
                                          bank.rearrange("p (h d) -> p h d", h=MH),
                                          den[:, t, :].unsqueeze(2).to_broadcast([P, MH, MDH]), ALU.mult), "m_pv", t)
                head_norm(hm[:, t, :], MH, sq, area(22560, 512), t)
            step(v.tensor_copy(sq, sq), "hm_squares")
            v.wait_ge(S_("hm_rstd"), 1)
            v.wait_ge(S_("m_row_in"), 16)
            v.wait_ge(S_("mo_gated"), NT)
            for t in range(NT):
                x = hm[:, t, :]
                tt(x.rearrange("p (h d) -> p h d", h=MH), x.rearrange("p (h d) -> p h d", h=MH),
                   stat(104, NT, 4)[:, t, :].unsqueeze(2).to_broadcast([P, MH, MDH]), ALU.mult)
                tt(x, x, m_row, ALU.mult)
                tt(Z[:, t, MO:MO + MW], x, Z[:, t, MO:MO + MW], ALU.mult)
            v.wait_ge(S_("pos_in"), 16)
            step(v.tensor_copy(stat(260, 2), pos_i[:]))
            TWO_PI = [6.28125, 1.9353071795e-3, 1.0253e-11]
            ang, turns = stat(320, NT, 32), stat(384, NT, 32)
            sc = stat(128, 2, NT, 32)
            for t in range(NT):
                ts(ang[:, t, :], freq, stat(260 + t, 1), ALU.mult)
            ts(turns, ang, 1 / (2 * np.pi), ALU.mult, 12582912.0, ALU.add)
            ts(turns, turns, 12582912.0, ALU.subtract)
            for c in TWO_PI:
                stt(ang, turns, -c, ang, ALU.mult, ALU.add)
            ts(sc[:, 0, :, :], ang, 3.1415925, ALU.min, -3.1415925, ALU.max)
            stt(ang, ang, -1.0, ang, ALU.mult, ALU.max)
            ts(sc[:, 1, :, :], ang, -1.0, ALU.mult, float(np.float32(np.pi / 2)), ALU.add, signal="angle_ready")
            v.wait_ge(S_("sincos_ready"), 1)
            for t in range(NT):
                x = Z[:, t, AQ:AQ + 2 * AW].rearrange("p (h a d) -> p h a d", a=2, d=32)
                tmp = [rope_t[:, j, :].rearrange("p (h d) -> p h d", d=32) for j in range(4)]
                sin, cos = (sc[:, j, t, :].unsqueeze(1).to_broadcast([P, 16, 32]) for j in range(2))
                x1, x2 = x[:, :, 0, :], x[:, :, 1, :]
                for j, (a, b) in enumerate(((x1, cos), (x2, sin), (x2, cos), (x1, sin))):
                    tt(tmp[j], a, b, ALU.mult)
                tt(x1, tmp[0], tmp[1], ALU.subtract)
                tt(x2, tmp[2], tmp[3], ALU.add, "rope_done" if t else None)
            take_T("a_T", aT)
            a_units = [(p, t) for p in range(4) for t in range(NT)]
            softmax_max("a", a_units, lambda t: causal[:, t, :], ADH ** -0.5)
            sums = stat(272, NT, 8)
            for t in range(NT):
                by_head = sums[:, t, :].rearrange("p (a b c) -> p a c b", b=2, c=2)
                take_weighted("a_pv", t, Z[:, t, AQ:AQ + AW], by_head, ADH)
                step(v.tensor_copy(Z[:, t, AQ:AQ + 1], Z[:, t, AQ:AQ + 1]), "y_ready")
            take_T("y_T", yT)
            v.wait_ge(S_("b_g_in"), 16)
            b_g = area(0, 2, D)
            for c in range(2):
                for j in range(4):
                    bank = filled(v, "merge", 8 * c + j)
                    step.free(v.tensor_tensor(sg[:, j, :], bank, b_g[:, j // 2, c * BLK:(c + 1) * BLK], ALU.add),
                              "merge", 8 * c + j)
                step(v.tensor_copy(sg[:, 0, 0:1], sg[:, 0, 0:1]), "gate_pre")
                v.wait_ge(S_("gate_ready"), c + 1)
                for t in range(NT):
                    h = H[:, t, c * BLK:(c + 1) * BLK]
                    for m in range(2):
                        i = 8 * c + 4 + 2 * t + m
                        bank = filled(v, "merge", i)
                        step.free(v.tensor_tensor(sg[:, 2 * m + t, :], bank, sg[:, 2 * m + t, :], ALU.mult), "merge", i)
                    tt(h, sg[:, t, :], sg[:, 2 + t, :], ALU.add, "merged_ready")
            take_T("mg_T", HT)
            add_to_x("w_out", mod[:, 2, :])
            norm(1, X, mod[:, 4, :], mod[:, 3, :])
            take_T("T1", HT)
            for i in range(NF // 2):
                after(v, f"ff_g{i}")
                bank = filled(v, f"ff_u{i}")
                f = fT[:, 2 * i:2 * i + 2, :].rearrange("p a b -> p (a b)")
                step.free(v.tensor_tensor(f, bank, silu_g[:, i % 2, :], ALU.mult), f"ff_u{i}")
                step(v.tensor_copy(f[:, 0:1], f[:, 0:1]), "f_ready")
            add_to_x("down", mod[:, 5, :])
            norm(2, area(8712, NT, D), gain_of(2))
            take_T("T2", memT)
            norm(3, X, gain_of(3), dst=X)
            norm(4, X, gain_of(4))
            take_T("T4", HT)
            take_blocks("e_z", 8, e_z)
            ec = part(cols, COLS, "even_conv")
            step(v.memset(e_cu[:, :, 0:2], 0.0))
            tt(e_cu[:, :, 2:], e_z[:, 4:8, :], e_z[:, 0:4, :], ALU.mult)
            for b in range(4):
                y = e_yT[:, b, :]
                ts(y, e_cu[:, b, 0:S], ec[:, b:b + 1], ALU.mult)
                for j in (1, 2):
                    stt(y, e_cu[:, b, j:j + S], ec[:, 4 * j + b:4 * j + b + 1], y, ALU.mult, ALU.add)
            tt(e_yT[:, 0:4, :], e_yT[:, 0:4, :], e_z[:, 8:12, :], ALU.mult)
            step(v.memset(e_pv[:, :, 0:16], 0.0))
            step(v.tensor_copy(e_pv[:, :, 16:], e_z[:, 12:16, :]))
            v.wait_ge(S_("inv_in"), 16)
            for g in range(4):
                src = e_pv[:, g, :]
                for j in range(g + 1):
                    dst = e_t[:, j % 2, :]
                    w = 1 << j
                    tt(dst[:, w:], src[:, w:], src[:, 0:S + 16 - w], ALU.add)
                    step(v.tensor_copy(dst[:, 0:w], src[:, 0:w]))
                    src = dst
                tt(e_pool[:, g, :], src[:, 16:], e_inv[:, g, :], ALU.mult)
                tt(e_pool[:, g, :], e_pool[:, g, :], e_pv[:, g, 16:], ALU.subtract, "pooled_ready" if g == 3 else None)
            ps = part(cols, COLS, "pool_scale")
            for i in range(2):
                bank = filled(v, "e_pool", i)
                for b in range(2):
                    g = 2 * i + b
                    ins = v.tensor_scalar(e_yT[:, 4 + g, :], bank[:, b * S:(b + 1) * S], ps[:, g:g + 1], None, ALU.mult)
                    if b:
                        step.free(ins, "e_pool", i)
                    else:
                        step(ins)
            add_to_x("e_out")

            def odd():
                norm(7, X, gain_of(7))
                take_T("T7", HT)
                take_blocks("o_ql", 4, o_qT, CR ** -0.5)
                bank = filled(v, "o_ckv")
                step.free(v.tensor_copy(o_c, bank[:, 0:NT * (P + 8)].rearrange("p (t n) -> p t n", t=NT)), "o_ckv")
                bank = filled(v, "o_ik")
                step.free(v.tensor_copy(o_ikT, bank[:, 0:S]), "o_ik")
                take_blocks("o_iq", 2, o_iqT)
                take_blocks("o_hq", 2, h_qT)
                v.wait_ge(S_("odd_in"), 64)
                tmp = h_KE[:, 0:2, :].rearrange("p a b -> p (a b)")
                tt(tmp, lb_row[:, 0, :], lb_row[:, 1, :], ALU.max)
                tt(lb_row[:, 0, :], lb_row[:, 0, :], tmp, ALU.subtract)
                tt(lb_row[:, 1, :], lb_row[:, 1, :], tmp, ALU.subtract, "lb_diff")
                for t in range(NT):
                    bank = filled(v, "o_hi", t)
                    step.free(v.tensor_copy(h_i[:, t, :], bank), "o_hi", t)
                for t in range(NT):
                    bank = filled(v, "o_hg", t)
                    step.free(v.tensor_copy(h_g[:, t, :], bank), "o_hg", t)
                    step(v.tensor_copy(h_g[:, t, 0:1], h_g[:, t, 0:1]), "hg_in")
                for t in range(NT):
                    stt(h_QE[:, 0, 0:P], o_c[:, t, 0:P], 1.0, o_c[:, t, 0:P], ALU.mult, ALU.mult,
                        accum=stat(288 + t, 1))
                step(v.tensor_copy(stat(288, 2), stat(288, 2)), "ckv_squares")
                v.wait_ge(S_("lb_exp"), 1)
                tt(tmp, lb_row[:, 0, :], lb_row[:, 1, :], ALU.add)
                step(v.reciprocal(tmp, tmp))
                tt(lb_row[:, 0, :], lb_row[:, 0, :], tmp, ALU.mult)
                ts(lb_row[:, 1, :], lb_row[:, 0, :], -1.0, ALU.mult, 1.0, ALU.add)
                v.wait_ge(S_("ckv_rstd"), 1)
                for t in range(NT):
                    stt(o_c[:, t, 0:P], o_c[:, t, 0:P], stat(290 + t, 1), kv_row, ALU.mult, ALU.mult,
                        "ckv_ready" if t else None)
                for t in range(NT):
                    after(v, "o_hf", t)
                    tt(h_f[:, t, :], h_f[:, t, :], lb_row[:, 1, :], ALU.mult)
                    tt(h_f[:, t, :], h_f[:, t, :], lb_row[:, 0, :], ALU.add)
                    ts(h_kn[:, t, :], h_f[:, t, :], -1.0, ALU.mult, 1.0, ALU.add, signal="forget_ready")
                bank = filled(v, "o_cT")
                step.free(v.tensor_copy(o_cT, bank[:, 0:S]), "o_cT")
                take_T("o_kT", h_kT, 4)
                for n, h in enumerate(LEVELS):
                    after(v, f"h_d{n}", 1)
                    tt(h_KE, h_kT, h_E, ALU.mult)
                    tt(h_QE, h_qT, h_E, ALU.mult, "level_ready")
                    for i in range(1 if h == P else NT):
                        bank = filled(v, f"h_s{n}", i).rearrange("p (h t) -> p h t", h=HH)
                        if h == P:
                            step.free(v.tensor_copy(h_x, bank), f"h_s{n}", i)
                        else:
                            m = h_mask[:, 2 * n + 1, :].unsqueeze(1).to_broadcast([P, HH, P])
                            if n == 1:
                                step.free(v.tensor_tensor(h_sc[:, i, :, :], bank, m, ALU.mult), f"h_s{n}", i)
                            else:
                                step.free(v.tensor_tensor(h_tmp, bank, m, ALU.mult), f"h_s{n}", i)
                                tt(h_sc[:, i, :, :], h_sc[:, i, :, :], h_tmp, ALU.add)
                for t in range(NT):
                    bank = filled(v, "h_diag", t).rearrange("p (h t) -> p h t", h=HH)
                    step.free(v.tensor_tensor(h_tmp, bank, ident.unsqueeze(1).to_broadcast([P, HH, P]), ALU.mult),
                              "h_diag", t)
                    tt(h_sc[:, t, :, :], h_sc[:, t, :, :], h_tmp, ALU.add, "hscores_ready")
                sq = stat(296, NT, 4)
                for t in range(NT):
                    bank = filled(v, "h_pv", t)
                    step.free(v.tensor_copy(h_o[:, t, :], bank), "h_pv", t)
                    head_norm(h_o[:, t, :], HH, sq, h_tmp.rearrange("p a b -> p (a b)"), t)
                step(v.tensor_copy(sq, sq), "yd_squares")
                v.wait_ge(S_("yd_rstd"), 1)
                v.wait_ge(S_("hg_ready"), NT)
                for t in range(NT):
                    x = h_o[:, t, :]
                    tt(x.rearrange("p (h d) -> p h d", h=HH), x.rearrange("p (h d) -> p h d", h=HH),
                       stat(304, NT, 4)[:, t, :].unsqueeze(2).to_broadcast([P, HH, P]), ALU.mult)
                    tt(x, x, h_row, ALU.mult)
                    tt(yd[:, t, :], x, h_g[:, t, :], ALU.mult, "hgrn_done" if t else None)
                for u in range(8):
                    t, p = u // 4, u % 4
                    after(v, "idx", u)
                    for h in range(2):
                        if h == 0 and p == 0:
                            ts(o_iw, o_c[:, t, P:P + 8], IH ** -0.5, ALU.mult)
                        hd = head_of(2 * p + h)
                        if hd == 0:
                            ts(o_score[:, t, :], o_rel[:, u % 2, 0:S], o_iw[:, 0:1], ALU.mult)
                        else:
                            stt(o_score[:, t, :], o_rel[:, u % 2, h * S:(h + 1) * S], o_iw[:, hd:hd + 1],
                                o_score[:, t, :], ALU.mult, ALU.add, "rel_used" if h else None)
                for t in range(NT):
                    tt(o_work[:, t, :], o_score[:, t, :], causal[:, t, :], ALU.add)
                    for r in range(TOPK // 8):
                        step(v.max(stat(616, 8), o_work[:, t, :]))
                        step(v.match_replace(o_work[:, t, :], stat(616, 8), o_work[:, t, :], REMOVED))
                    ts(o_work[:, t, :], o_work[:, t, :], REMOVED / 2, ALU.is_gt, NEG, ALU.mult)
                    tt(o_mask[:, t, :], o_work[:, t, :], causal[:, t, :], ALU.add)
                softmax_max("o", [(p, t) for t in range(NT) for p in range(4)], lambda t: o_mask[:, t, :], 1.0)
                for i in range(4):
                    t, g = i // 2, i % 2
                    take_weighted("o_pv", i, H[:, t, g * BLK:(g + 1) * BLK], sums[:, t, 4 * g:4 * g + 4], P)
                take_T("lat_T", HT)
                for t in range(NT):
                    bank = filled(v, "o_yc", t)
                    step.free(v.tensor_copy(H[:, t, 0:BLK], bank), "o_yc", t)
                take_T("o_yT", HT)
                add_to_x("o_out")

            o_iw = stat(312, 8)

            def top16(src, work, values, index):
                step(v.max(values[:, 0:8], src))
                step(v.max_index(index[:, 0:8], values[:, 0:8], src))
                step(v.match_replace(work, values[:, 0:8], src, REMOVED))
                step(v.max(values[:, 8:16], work))
                step(v.max_index(index[:, 8:16], values[:, 8:16], work))

            def peer(l):
                norm(6 + 3 * l, X, gain_of(6 + 3 * l))
                take_T(f"T{6 + 3 * l}", HT)
                take_blocks(f"p_q{l}", 8, p_qT)
                for t in range(NT):
                    for i in range(4):
                        bank = filled(v, f"p_s{l}", 4 * t + i)
                        step.free(v.tensor_copy(p_s[:, 4 * i:4 * i + 4, :], bank.rearrange("p (b n) -> p b n", b=4)),
                                  f"p_s{l}", 4 * t + i)
                    for b in range(16):
                        top16(p_s[:, b, :], p_work[:, b * NK:(b + 1) * NK], p_v16[:, b, :], p_idx[:, b, :])
                    step(v.tensor_copy(p_i16, p_idx[:]))
                    v16 = p_v16.rearrange("p (h a) k -> p h a k", a=2)
                    cand = p_cand.rearrange("p (h a b) -> p h a b", h=PH, a=PK)
                    tt(cand, v16[:, :, 0, :].unsqueeze(3).to_broadcast([P, PH, PK, PK]),
                       v16[:, :, 1, :].unsqueeze(2).to_broadcast([P, PH, PK, PK]), ALU.add)
                    for h in range(PH):
                        c = p_cand[:, h * S:(h + 1) * S]
                        top16(c, p_work[:, h * S:(h + 1) * S], p_top[:, h, :], p_pos[:, h, :])
                    pos = p_pos[:].rearrange("p h k -> p (h k)")
                    step(v.tensor_scalar(p_bits[:, 0, :], pos, 4, None, ALU.logical_shift_right))
                    step(v.tensor_scalar(p_bits[:, 1, :], pos, 15, None, ALU.bitwise_and))
                    step(v.tensor_copy(p_ab, p_bits[:]))
                    i16 = p_i16.rearrange("p (h a) k -> p h a k", a=2)
                    for a in range(2):
                        eq = p_eq.rearrange("p (n m) -> p n m", m=PK)
                        tt(eq, p_ab[:, a, :].unsqueeze(2).to_broadcast([P, SEL, PK]),
                           iota.unsqueeze(1).to_broadcast([P, SEL, PK]), ALU.is_equal)
                        eq4 = p_eq.rearrange("p (h k m) -> p h k m", h=PH, k=PK)
                        tt(eq4, eq4, i16[:, :, a, :].unsqueeze(2).to_broadcast([P, PH, PK, PK]), ALU.mult)
                        step(v.tensor_reduce(p_i12[:, a, :], eq, AXX, ALU.add))
                    stt(p_eid[:, t, :], p_i12[:, 0, :], float(NK), p_i12[:, 1, :], ALU.mult, ALU.add, "eid_ready")
                    g = p_g[:, t, :].rearrange("p (h k) -> p h k", h=PH)
                    tt(g, p_top, p_top[:, :, 0:1].to_broadcast([P, PH, PK]), ALU.subtract, "top_ready")
                for t in range(NT):
                    g = p_g[:, t, :].rearrange("p (h k) -> p h k", h=PH)
                    v.wait_ge(S_("top_exp"), NT * l + t + 1)
                    step(v.tensor_reduce(stat(616, 8), g, AXX, ALU.add))
                    step(v.reciprocal(stat(616, 8), stat(616, 8)))
                    tt(g, g, stat(616, 8).unsqueeze(2).to_broadcast([P, PH, PK]), ALU.mult)
                for t in range(NT):
                    base = (l * 2 * NT + t) * SEL
                    with v.Fori(0, SEL // RING) as i:
                        for r in range(RING):
                            v.wait_ge(row_landed[r], i * 16 + 16 * (base // RING + 1))
                            v.scalar_tensor_tensor(out=rows_u[:, r, :], in0=rows_u[:, r, :], scalar=1.0, in1=H[:, t, :],
                                                   op0=ALU.mult, op1=ALU.mult,
                                                   accum_out=p_act[:, t, bass.ds(i * RING + r, 1)]).then_inc(rows_used, 1)
                    v.wait_ge(rows_used, base + SEL)
                    step(v.tensor_copy(p_act[:, t, 0:1], p_act[:, t, 0:1]), "dots_ready")
                for t in range(NT):
                    v.wait_ge(S_("gelu_ready"), NT * l + t + 1)
                    tt(p_w[:, t, :], p_act[:, t, :], p_g[:, t, :], ALU.mult)
                for t in range(NT):
                    base = (l * 2 * NT + NT + t) * SEL
                    with v.Fori(0, SEL // RING) as i:
                        for r in range(RING):
                            v.wait_ge(row_landed[r], i * 16 + 16 * (base // RING + 1))
                            v.wait_ge(rows_used, i * RING + (base + r))
                            v.scalar_tensor_tensor(out=X[:, t, :], in0=rows_u[:, r, :],
                                                   scalar=p_w[:, t, bass.ds(i * RING + r, 1)], in1=X[:, t, :],
                                                   op0=ALU.mult, op1=ALU.add).then_inc(rows_used, 1)
                    v.wait_ge(rows_used, base + SEL)
                    step(v.tensor_copy(X[:, t, 0:1], X[:, t, 0:1]), "x_ready")

            for l in range(2):
                if l:
                    odd()
                take_blocks(f"x_k{l}", 4, x_kT)
                for i in range(4):
                    c, t = i // 2, i % 2
                    bank = filled(v, f"x_v{l}", i)
                    step.free(v.tensor_copy(x_v[:, t, c * BLK:(c + 1) * BLK], bank), f"x_v{l}", i)
                norm(5 + 3 * l, X, gain_of(5 + 3 * l))
                take_T(f"T{5 + 3 * l}", HT)
                take_blocks(f"x_q{l}", 4, x_qT)
                softmax_max(f"x{l}", [(p, t) for p in range(2) for t in range(NT)], None, XDH ** -0.5)
                for i in range(4):
                    t, g = i // 2, i % 2
                    take_weighted(f"x_pv{l}", i, H[:, t, g * BLK:(g + 1) * BLK], sums[:, t, 2 * g:2 * g + 2], XDH)
                take_T(f"x_oT{l}", HT)
                add_to_x(f"x_o{l}")
                peer(l)
            norm(10, X, gain_of(10), signal="final_ready")


def constants():
    f = np.float32
    const = np.zeros((P, NCONST), f)

    def put(name, a):
        at, n = CONST[name]
        const[:, at:at + n] = a

    r = np.arange(P)
    put("ident", np.eye(P))
    put("flip", np.eye(P)[::-1])
    put("ones", 1.0)
    q = np.arange(S).reshape(NT, P).T
    put("causal", np.where(np.arange(S)[None, None] <= q[:, :, None], 0.0, NEG).reshape(P, NT * S))
    put("tri", r[:, None] <= r[None])
    half = ADH // 2
    put("freq", (f(10000.0) ** (-np.arange(half, dtype=f) / f(half)))[None])
    put("iota", np.arange(16)[None])

    dist = np.maximum(S - 1 - np.arange(2 * S), 0)
    exact = BUCKETS // 2
    ratio = np.log(np.maximum(dist, 1).astype(f) / f(exact)) / f(np.log(MAXDIST / exact))
    large = np.minimum(exact + (ratio * (BUCKETS - exact)).astype(np.int32), BUCKETS - 1)
    bucket = np.where(dist < exact, dist, large)
    onehot = (bucket[None] == np.arange(BUCKETS)[:, None]).astype(f)

    inv = np.stack([1.0 / np.minimum(np.arange(S) + 1, w) for w in (2, 4, 8, 16)]).astype(f)
    pool_inv = np.broadcast_to(inv.reshape(1, -1), (P, 4 * S)).copy()

    masks = [r[:, None] > r[None], r[:, None] <= r[None]]
    for h in LEVELS[1:]:
        mid = r // (2 * h) * 2 * h + h
        second = r % (2 * h) >= h
        a, x, m = r[:, None], r[None], mid[None]
        masks.append(np.where(second[None], (a >= m) & (a <= x), (a > x) & (a < m)))
        masks.append((r[:, None] // (2 * h) == r[None] // (2 * h)) & ~second[:, None] & second[None])
    masks = np.concatenate([m.astype(f) for m in masks], 1)
    return {"const": const, "onehot": onehot, "pool_inv": pool_inv, "masks": masks}


def lay_out(a):
    def std(w):
        k = w.shape[0] // P
        return w.reshape(k, P, w.shape[1]).transpose(1, 0, 2).reshape(P, -1)

    def cut(w):
        return [std(w[:, c:c + BLK]) for c in range(0, w.shape[1], BLK)]

    w_in = a["w_in"][0]
    o = MW * 4 + 2 * MH
    t = cut(a["ada_w"][0]) + cut(w_in[:, 0:2 * MW]) + cut(w_in[:, 2 * MW:4 * MW]) + cut(w_in[:, o:o + 3 * AW])
    g = o + 3 * AW
    for c in range(2):
        t.append(std(w_in[:, g + c * BLK:g + (c + 1) * BLK]))
        t.append(std(w_in[:, g + D + c * BLK:g + D + (c + 1) * BLK]))
        t.append(np.concatenate([std(a["p_mlstm"][0][:, c * BLK:(c + 1) * BLK]),
                                 std(a["p_moba"][0][:, c * BLK:(c + 1) * BLK])], 1))
    t += cut(a["w_out"][0])
    for i in range(NF // 2):
        c = slice(2 * P * i, 2 * P * (i + 1))
        t.append(std(np.concatenate([a["w_gate"][0][:, c], a["w_up"][0][:, c]], 1)))
    down = np.concatenate([a["w_down"][0], np.zeros((2 * P, D), np.float32)], 0)
    t += [std(down[4 * P * i:4 * P * (i + 1)]) for i in range(6)]
    t += cut(a["even_w_in_2"][0]) + cut(a["even_w_out_2"][0])
    wi = a["odd_w_in_2"][0]
    for l in range(2):
        if l:
            t += cut(wi[:, 0:1024])
            c0 = 1024
            iq0, ik0, iw0, h0 = c0 + CR, c0 + CR + 512, c0 + CR + 576, c0 + CR + 584
            ik = wi[:, ik0:ik0 + 64]
            t.append(std(np.concatenate([wi[:, c0:c0 + CR], ik, ik, wi[:, iw0:iw0 + 8],
                                         np.zeros((D, BLK - 264), np.float32)], 1)))
            t += cut(wi[:, iq0:iq0 + 512])
            t += cut(wi[:, h0:h0 + 2048])
            t += cut(a["odd_w_out_2"][0])
        kv = a["xattn_wkv_2"][l]
        t += cut(kv) + cut(a["xattn_wq_2"][l]) + cut(a["xattn_wo_2"][l]) + cut(a["peer_wq_2"][l])
        keys = a["peer_keys_2"][l].transpose(3, 0, 1, 2).reshape(P, 16 * NK)
        t.append(np.concatenate([keys, np.zeros((P, 4096 - 16 * NK), np.float32)], 1))
    weights = np.stack(t)

    col = lambda x: x.reshape(-1, P).T
    cols = np.concatenate([col(a["c"][0]), col(a["b_in"][0, 0:2 * MW]),
                           *[col(a["conv_w"][0, j]) for j in range(4)], col(a["conv_b"][0]),
                           *[col(a["even_conv_w_2"][0, j, 0]) for j in range(3)], col(a["even_pool_scale_2"][0])], 1)
    gates = std(w_in[:, 4 * MW:4 * MW + 8])
    small = np.concatenate([gates, a["even_pool_w_2"][0].transpose(1, 0, 2).reshape(P, -1),
                            a["odd_w_uv_2"][0].transpose(1, 0, 2).reshape(P, -1)], 1)
    b = a["b_in"][0]
    rows = np.concatenate([a["ada_b"][0], b[4 * MW:o], b[2 * MW:4 * MW], b[o:g], b[g:], a["m_norm_g"][0],
                           a["hgrn_gamma_2"].reshape(-1), a["odd_kv_norm_2"][0], a["odd_hg_norm_2"][0],
                           a["norm1_g"][0], a["norm2_g"][0], a["mem_norm_2"], a["normf_g"], a["mix_norm_2"][0], a["xattn_norm_2"][0],
                           a["peer_norm_2"][0], a["mix_norm_2"][1], a["xattn_norm_2"][1], a["peer_norm_2"][1],
                           a["final_norm_2"]])[None]
    pos = a["positions"].reshape(NT, P).T
    return {"weights": weights, "cols": cols, "small": small, "rows": rows, "pos": pos, "rel_bias": a["rel_bias_2"],
            "x": a["x"], "mem": a["mem_2"], "u0": a["peer_u_2"][0], "u1": a["peer_u_2"][1],
            "v0": a["peer_v_2"][0], "v1": a["peer_v_2"][1], **constants()}


def kernel(**inputs):
    import concourse.bacc as bacc
    from concourse.bass_utils import run_bass_kernel_spmd

    arrays = {"in_" + n: np.ascontiguousarray(x) for n, x in lay_out({k: np.asarray(x) for k, x in inputs.items()}).items()}
    nc = bacc.Bacc("TRN2", target_bir_lowering=False, num_devices=1)
    io = {n[3:]: nc.dram_tensor(n, x.shape, mybir.dt.from_np(x.dtype), kind="ExternalInput").ap() for n, x in arrays.items()}
    io["out"] = nc.dram_tensor("out_dram", (1, S, D), F32, kind="ExternalOutput").ap()
    build(nc, io)
    return run_bass_kernel_spmd(nc, [arrays], core_ids=[0]).results[0]["out_dram"]
```

```python
from contextlib import ExitStack

import numpy as np
import concourse.bass as bass
from concourse import mybir

ALU = mybir.AluOpType
ACT = mybir.ActivationFunctionType
AXX = mybir.AxisListType.X
F32 = mybir.dt.float32
U32 = mybir.dt.uint32
I32 = mybir.dt.int32

P = 128
S = 256
NT = S // P
D = 1024
KD = D // P
BLK = 512
EPS = 1e-6
NEG = -1e30
REMOVED = -3e38
MH, MDH, MW = 4, 128, 512
AH, ADH, AW = 8, 64, 512
DFF = 2816
NF = DFF // P
CH, CR, CDH = 8, 128, 64
IH, IDH = 8, 64
TOPK = 64
BUCKETS, MAXDIST = 32, 128
HH, HK = 4, 128
XH, XDH = 4, 256
PH, NK, PK = 8, 128, 16
NE = NK * NK
SEL = PH * PK
LEVELS = [128, 64, 32, 16, 8, 4, 2, 1]
NSLOT = 3
RING = 8
HALF = RING // 2
VE_SLOTS = [0, HALF]
PE_SLOTS = [r for r in range(RING) if r not in VE_SLOTS]
PE_ROWS = len(PE_SLOTS)
STEPS = SEL // RING

COLS = {}
for _n, _w in (("c", 8), ("b_qk", 8), ("conv_w", 32), ("conv_b", 8), ("even_conv", 12), ("pool_scale", 4)):
    COLS[_n] = (sum(w for _, w in COLS.values()), _w)
NCOL = sum(w for _, w in COLS.values())
CONST = {}
for _n, _w in (("ident", P), ("flip", P), ("ones", P), ("causal", 2 * S), ("tri", P), ("freq", 32), ("iota", 16)):
    CONST[_n] = (sum(w for _, w in CONST.values()), _w)
NCONST = sum(w for _, w in CONST.values())
SMALL = {}
for _n, _w in (("gates", KD * 8), ("pool_w", 4 * P), ("w_uv", CH * CDH)):
    SMALL[_n] = (sum(w for _, w in SMALL.values()), _w)
NSMALL = sum(w for _, w in SMALL.values())
ROWS = {}
for _n, _w in (("ada_b", 6 * D), ("gate_b", 8), ("b_n", 5 * BLK), ("b_g", 2 * D), ("m_norm", MW), ("gamma", 2 * 512),
               ("kv_norm", CR), ("hg_norm", 512), ("norm", 11 * D)):
    ROWS[_n] = (sum(w for _, w in ROWS.values()), _w)
NROW = sum(w for _, w in ROWS.values())
NMASK = 2 + (len(LEVELS) - 1) * 2


class Plan:

    def __init__(self):
        self.first, self.fills = {}, []
        self.marks, self.taken = 0, {"vector": 0, "scalar": 0}

    def add(self, stage, n=1, taker="vector", marks=None):
        self.first[stage] = len(self.fills), self.marks
        for i in range(n):
            self.taken[taker] += 1
            self.fills.append((self.marks + (i + 1 if marks is None else marks), taker, self.taken[taker]))
        self.marks += n if marks is None else marks

    def mark(self, stage, i=0):
        return self.fills[self.first[stage][0] + i][0]

    def bank(self, stage, i=0):
        return (self.first[stage][0] + i) % 8

    def before(self, stage, i=0):
        n = self.first[stage][0] + i - 8
        return self.fills[n][1:] if n >= 0 else None

    def took(self, stage, i=0):
        return self.fills[self.first[stage][0] + i][1:]


def head_of(slot):
    return slot // 4 * 4 + slot % 2 * 2 + slot // 2 % 2


def place_of(slot, size):
    h = head_of(slot)
    return h // 2, slice(h % 2 * size, (h % 2 + 1) * size)


def units_of(plan, name, n, between={}):
    plan.add(f"{name}_s0")
    for u in range(n):
        if u + 1 < n:
            plan.add(f"{name}_s{u + 1}")
        for i in between.get(u, ()):
            plan.add(f"ada{i}")
        plan.add(f"{name}_t{u}", taker="scalar")


ADA_IN_M = {0: [4], 1: [5], 2: [6], 3: [7]}
ADA_IN_A = {0: [8], 2: [9], 4: [10], 6: [11]}


def make_plan():
    p = Plan()
    p.add("ada", 4)
    p.add("bias_rows")
    p.add("T0", 4)
    p.add("z_qk", 4)
    p.add("z_gate")
    p.add("z_n", 10)
    p.add("m_cum")
    p.add("m_g0")
    p.add("m_g1")
    units_of(p, "m", 4, ADA_IN_M)
    p.add("m_pv", NT)
    p.add("a_T", 4)
    units_of(p, "a", 8, ADA_IN_A)
    p.add("a_pv", NT)
    p.add("y_T", 4)
    p.add("merge", 16)
    p.add("mg_T", 4)
    p.add("w_out", 4)
    p.add("T1", 4)
    for i in range(NF // 2):
        p.add(f"ff_g{i}", taker="scalar")
        p.add(f"ff_u{i}")
        if i == 4:
            p.add("T2", 4)
    p.add("down", 4, marks=6)
    p.add("x_k0", 4)
    p.add("x_v0", 4)
    p.add("T4", 4)
    p.add("e_z", 8)
    p.add("e_pool", 2)
    p.add("e_out", 4)
    for l in range(2):
        if l:
            p.add("T7", 4)
            p.add("o_ql", 4)
            p.add("o_ckv")
            p.add("o_ik")
            p.add("o_iq", 2)
            p.add("o_hq", 2)
            p.add("o_hf", 2, "scalar")
            p.add("o_hi", 2)
            p.add("o_hg", 2)
            p.add("o_cT")
            p.add("o_kT", 2)
            p.add("h_d0", 2, "scalar")
            for n, h in enumerate(LEVELS):
                if n + 1 < len(LEVELS):
                    p.add(f"h_d{n + 1}", 2, "scalar")
                p.add(f"h_s{n}", 1 if h == P else NT)
            p.add("h_diag", NT)
            p.add("h_pv", NT)
            p.add("idx", 8, "scalar")
            units_of(p, "o", 8)
            p.add("o_pv", 4)
            p.add("lat_T", 4)
            p.add("o_yc", NT)
            p.add("o_yT", 4)
            p.add("o_out", 4)
        p.add(f"T{5 + 3 * l}", 4)
        p.add(f"x_q{l}", 4)
        units_of(p, f"x{l}", 4)
        p.add(f"x_pv{l}", 4)
        p.add(f"x_oT{l}", 4)
        p.add(f"x_o{l}", 4)
        p.add(f"T{6 + 3 * l}", 4)
        p.add(f"p_q{l}", 8)
        p.add(f"p_s{l}", 8)
        if l == 0:
            p.add("x_k1", 4)
            p.add("x_v1", 4)
        for t in range(NT):
            p.add(f"p_v{l}{t}", 2, marks=0)
    return p


def tiles_in_order():
    t = [("ada", i) for i in range(4)]
    t += [("z_qk", 1), ("z_qk", 3)] + [("z_n", 2 * i + 1) for i in range(5)]
    t += [(f"ada{i}", 0) for i in range(4, 12)]
    for c in range(2):
        t += [("merge", 8 * c + 1), ("merge", 8 * c + 3), ("merge", 8 * c + 7)]
    t += [("w_out", 1), ("w_out", 3)] + [(f"ff_u{i}", 0) for i in range(NF // 2)]
    t += [("down", i) for i in range(6)] + [("x_k0", 1), ("x_k0", 3), ("x_v0", 1), ("x_v0", 3)]
    t += [("e_z", 2 * i + 1) for i in range(4)] + [("e_out", 1), ("e_out", 3)]
    for l in range(2):
        if l:
            t += [("o_ql", 1), ("o_ql", 3), ("o_ik", 0), ("o_iq", 1), ("o_hq", 1), ("o_hf", 1), ("o_hi", 1), ("o_hg", 1)]
            t += [("o_out", 1), ("o_out", 3)]
        t += [(f"x_q{l}", 1), (f"x_q{l}", 3)]
        t += [(f"x_o{l}", 1), (f"x_o{l}", 3)]
        t += [(f"p_q{l}", 2 * i + 1) for i in range(4)] + [(f"p_s{l}", 7)]
        if l == 0:
            t += [("x_k1", 1), ("x_k1", 3), ("x_v1", 1), ("x_v1", 3)]
    return t


def build(nc, io):
    plan = make_plan()
    tiles = tiles_in_order()
    tile_no = {}
    for n, (stage, _) in enumerate(tiles):
        tile_no.setdefault(stage, n)

    with ExitStack() as ctx:
        def sb(name, shape, dt=F32):
            return ctx.enter_context(nc.sbuf_tensor(name, shape, dt))

        def sem(name):
            return ctx.enter_context(nc.semaphore(name))

        X = sb("X", [P, NT, D])
        H = sb("H", [P, NT, D])
        HT = sb("HT", [P, KD, S])
        W = sb("W", [P, NSLOT, 4096])
        gain = sb("gain", [P, 2, D])
        cols = sb("cols", [P, NCOL])
        const = sb("const", [P, NCONST])
        small = sb("small", [P, NSMALL])
        pos_i = sb("pos_i", [P, NT], I32)
        rel_sb = sb("rel_sb", [BUCKETS, 8])
        junk = sb("junk", [P, D])
        st = sb("st", [P, 640])
        arena = sb("arena", [P, 24576])
        banks = ctx.enter_context(nc.psum_tensor("banks", [P, 8, 512], F32))
        bias_scratch = nc.dram_tensor("bias_scratch", [8, 2 * S], F32).ap()

        def area(at, *shape):
            n = int(np.prod(shape))
            v = arena[:, at:at + n]
            if len(shape) == 1:
                return v
            names = "abc"[:len(shape)]
            return v.rearrange(f"p ({' '.join(names)}) -> p {' '.join(names)}", **dict(zip(names[1:], shape[1:])))

        def stat(at, *shape):
            n = int(np.prod(shape))
            v = st[:, at:at + n]
            if len(shape) == 1:
                return v
            names = "abc"[:len(shape)]
            return v.rearrange(f"p ({' '.join(names)}) -> p {' '.join(names)}", **dict(zip(names[1:], shape[1:])))

        def part(t, table, name):
            a, n = table[name]
            return t[:, a:a + n]

        ident, flip, ones = (part(const, CONST, n) for n in ("ident", "flip", "ones"))
        tri = part(const, CONST, "tri")
        causal = part(const, CONST, "causal").rearrange("p (t s) -> p t s", t=NT)
        freq, iota = part(const, CONST, "freq"), part(const, CONST, "iota")
        mod = area(0, 6, D)
        b_rows = area(6144, 8 + 5 * BLK)
        Z = area(8712, NT, 5 * BLK)
        MV, MO, AQ, AV = 0, 512, 1024, 2048
        qk_raw = area(13832, 8, S + 3)
        aT = area(13832, 8, S)
        qkT = area(15904, 8, S)
        yT = area(15904, 8, S)
        PT1 = area(17952, 8, NT, S)
        scrA = area(22048, 2, 512)
        probs = area(23072, 2, 512)
        rope_t = area(17952, 4, 512)
        m_row = area(22048, MW)
        g_log = area(17952, 2, 2, S)
        sg = area(17952, 4, 512)
        mW = area(18976, 2, 512)
        fT = area(8712, NF, S)
        silu_g = area(14344, 2, 512)
        memT = area(0, KD, S)
        e_z = area(2048, 16, S)
        e_cu = area(6144, 4, S + 2)
        e_pv = area(7176, 4, S + 16)
        e_t = area(8264, 2, S + 16)
        e_pool = area(8808, 4, S)
        e_inv = area(9832, 4, S)
        e_yT = area(10856, 8, S)
        x_qT = area(2048, 8, S)
        x_PT = area(8192, 4, NT, S)
        p_qT = area(2048, 16, S)
        p_s = area(6144, 16, NK)
        p_work = area(8192, 2048)
        p_cand = area(10240, 2048)
        p_eq = area(12288, 2048)
        rows_u = area(14336, RING, D)
        p_v16 = area(22528, 16, PK)
        p_top = area(22784, PH, PK)
        p_eid = sb("p_eid", [P, NT, SEL], U32)
        p_idx = sb("p_idx", [P, 16, PK], U32)
        p_pos = sb("p_pos", [P, PH, PK], U32)
        p_bits = sb("p_bits", [P, 2, SEL], U32)
        p_ab = area(22912, 2, SEL)
        p_i16 = area(23168, 16, PK)
        p_g = area(23424, NT, SEL)
        p_act = area(23680, NT, SEL)
        p_w = area(23936, NT, SEL)
        p_i12 = area(24192, 2, SEL)
        stage_idx = sb("stage_idx", [P, 2, HALF], U32)
        o_qT = area(2048, 8, S)
        o_c = area(4096, NT, P + 8)
        o_cT = area(4368, S)
        o_iqT = area(4624, 4, S)
        o_ikT = area(5648, S)
        h_qT = area(5904, HH, S)
        h_f = area(6928, NT, 512)
        h_kn = area(7952, NT, 512)
        h_kT = area(8976, HH, S)
        h_i = area(10000, NT, 512)
        h_g = area(11024, NT, 512)
        lb_row = area(12048, 2, 512)
        h_row = area(13072, 512)
        kv_row = area(13584, P)
        h_mask = area(13712, NMASK, P)
        h_E = [area(15760 + 1024 * i, HH, S) for i in range(2)]
        h_KE = [area(17808 + 1024 * i, HH, S) for i in range(2)]
        h_QE = [area(19856 + 1024 * i, HH, S) for i in range(2)]
        h_x = area(21904, HH, P)
        h_sc = area(22416, NT, HH, P)
        h_tmp = area(23440, HH, P)
        h_o = area(15760, NT, 512)
        yd = area(10000, NT, 512)
        o_PT = area(11024, 8, NT, S)
        hankel = area(15120, NT, 8 * S)
        o_mask = area(19216, NT, S)
        o_score = area(19728, NT, S)
        o_work = area(20240, NT, S)
        o_rel = area(20752, 2, 512)
        onehot = arena[0:BUCKETS, 22048:22560]
        rb_sb = arena[0:8, 22560:23072]
        c_rep = sb("c_rep", [P, KD, P])
        x_kT1 = sb("x_kT1", [P, 8, S])
        x_kTs, x_vs = [area(12928, 8, S), x_kT1], [area(14976, NT, D), area(0, NT, D)]
        mem_in = area(15368, NT, D)
        p_s1 = area(2048, 16, NK)
        diag = area(4096, PE_ROWS, P)

        pe_filled = sem("pe_filled")
        took = {"vector": sem("vector_took"), "scalar": sem("scalar_took")}
        tile_landed = [sem(f"tile_landed{i}") for i in range(NSLOT)]
        row_landed = [sem(f"row_landed{i}") for i in range(RING)]
        rows_used = {"vector": sem("rows_used_vector"), "tensor": sem("rows_used_tensor")}
        idx_staged = sem("idx_staged")
        named = {}

        def S_(name):
            if name not in named:
                named[name] = sem(name)
            return named[name]

        class Steps:

            def __init__(self, eng, own, name):
                self.eng, self.own, self.name, self.count = eng, S_(own), name, {}

            def __call__(self, ins, signal=None):
                s = self.own if signal is None else S_(signal)
                self.count[id(s)] = self.count.get(id(s), 0) + 1
                ins.then_inc(s, 1)
                self.eng.wait_ge(s, self.count[id(s)])

            def free(self, ins, stage, i=0):
                who, n = plan.took(stage, i)
                assert who == self.name
                ins.then_inc(took[who], 1)
                self.eng.wait_ge(took[who], n)

        def filled(eng, stage, i=0):
            eng.wait_ge(pe_filled, plan.mark(stage, i))
            return banks[:, plan.bank(stage, i), :]

        def after(eng, stage, i=0):
            who, n = plan.took(stage, i)
            eng.wait_ge(took[who], n)

        def used_before(layer, phase):
            v_phases, u_phases = 2 * layer + phase // 2, 2 * layer + (phase + 1) // 2
            return (u_phases * SEL + v_phases * STEPS * len(VE_SLOTS), v_phases * STEPS * PE_ROWS)

        block = ctx.enter_context(nc.Block())

        @block.sync
        def _(sp):
            for n in range(len(tiles)):
                if n >= NSLOT:
                    stage, i = tiles[n - NSLOT]
                    sp.wait_ge(pe_filled, plan.first["down"][1] + i + 1 if stage == "down" else plan.mark(stage, i))
                sp.dma_start(W[:, n % NSLOT, :], io["weights"][n]).then_inc(tile_landed[n % NSLOT], 16)
            sp.wait_ge(S_("final_ready"), NT)
            sp.dma_start(io["out"].rearrange("b (t p) d -> p (b t) d", p=P), H[:]).then_inc(S_("out_written"), 16)
            sp.wait_ge(S_("out_written"), 16)

        @block.gpsimd
        def _(po):
            def row(dst, name, at=0, n=None):
                a, w = ROWS[name]
                n = n or w
                return po.dma_start(dst, io["rows"][0:1, a + at:a + at + n].to_broadcast([P, n]))

            po.dma_start(const[:], io["const"]).then_inc(S_("const_in"), 16)
            row(gain[:, 1, :], "norm", D, D).then_inc(S_("gain_in1"), 16)
            row(b_rows, "gate_b", 0, 8 + 5 * BLK).then_inc(S_("b_rows_in"), 16)
            po.dma_start(small[:], io["small"]).then_inc(S_("small_in"), 16)
            po.dma_start(rel_sb[:], io["rel_bias"]).then_inc(S_("rel_in"), 16)
            po.dma_start(onehot, io["onehot"]).then_inc(S_("onehot_in"), 16)
            po.dma_start(pos_i[:], io["pos"]).then_inc(S_("pos_in"), 16)
            row(mod[:, 2:, :].rearrange("p a b -> p (a b)"), "ada_b", 2 * D, 4 * D).then_inc(S_("ada_b_rest_in"), 16)
            po.wait_ge(S_("bias_rows_ready"), 1)
            po.dma_start(bias_scratch, rb_sb).then_inc(S_("scratch_written"), 16)
            po.wait_ge(S_("h_ready"), NT)
            row(area(0, 2 * D), "b_g").then_inc(S_("b_g_in"), 16)
            po.wait_ge(S_("m_row_free"), 1)
            row(m_row, "m_norm").then_inc(S_("m_row_in"), 16)

            def load_gain(n):
                po.wait_ge(S_("h_ready"), NT * (n - 1))
                row(gain[:, n % 2, :], "norm", n * D, D).then_inc(S_(f"gain_in{n % 2}"), 16)

            load_gain(2)
            po.wait_ge(pe_filled, plan.mark("merge", 15))
            po.dma_start(mem_in, io["mem"].rearrange("b (t p) d -> p (b t) d", p=P)).then_inc(S_("mem_in"), 16)
            load_gain(3)
            load_gain(4)
            po.wait_ge(pe_filled, plan.mark("down", 3))
            po.dma_start(e_inv.rearrange("p a b -> p (a b)"), io["pool_inv"]).then_inc(S_("inv_in"), 16)
            load_gain(5)
            load_gain(6)

            def gathers(layer):
                for phase in range(2 * NT):
                    table = io[("u", "v")[phase % 2] + str(layer)]
                    t = phase // 2
                    by_v, by_pe = used_before(layer, phase)
                    n = (layer * 2 * NT + phase) * STEPS
                    if phase % 2 == 0:
                        po.wait_ge(S_("eid_ready"), NT * layer + t + 1)

                    def half_step(i, half, first):
                        po.tensor_copy(stage_idx[:, half, :], p_eid[:, t, bass.ds(i * RING + HALF * half, HALF)])\
                            .then_inc(idx_staged, 1)
                        po.wait_ge(idx_staged, i * 2 + (2 * n + half + 1))
                        if not first:
                            po.sem_inc(S_("gather_turns"), 1)
                        for r in range(HALF):
                            po.indirect_dma_start(rows_u[:, half * HALF + r, :], None, table,
                                                  bass.IndirectOffsetOnAxis(ap=stage_idx[:, half, r:r + 1], axis=0))\
                                .then_inc(row_landed[half * HALF + r], 16)

                    for half in range(2):
                        if phase % 2:
                            po.wait_ge(rows_used["vector"], by_v - RING + HALF * (half + 1))
                        elif n:
                            po.wait_ge(rows_used["vector"], by_v - 2 + half + 1)
                            po.wait_ge(rows_used["tensor"], by_pe - PE_ROWS + PE_ROWS // 2 * (half + 1))
                        half_step(0, half, True)
                    with po.Fori(1, STEPS) as i:
                        for half in range(2):
                            if phase % 2:
                                po.wait_ge(rows_used["tensor"], i * PE_ROWS + (by_pe - PE_ROWS + PE_ROWS // 2 * (half + 1)))
                                po.wait_ge(rows_used["vector"], i * 2 + (by_v - 2 + half + 1))
                            else:
                                po.wait_ge(rows_used["vector"], i * RING + (by_v - RING + HALF * (half + 1)))
                            half_step(i, half, False)

            gathers(0)
            load_gain(7)
            load_gain(8)
            po.wait_ge(S_("x_ready"), NT)
            row(lb_row.rearrange("p a b -> p (a b)"), "gamma").then_inc(S_("odd_in"), 16)
            row(h_row, "hg_norm").then_inc(S_("odd_in"), 16)
            row(kv_row, "kv_norm").then_inc(S_("odd_in"), 16)
            po.dma_start(h_mask.rearrange("p a b -> p (a b)"), io["masks"]).then_inc(S_("odd_in"), 16)
            po.wait_ge(S_("hgrn_done"), 1)
            po.wait_ge(S_("scratch_written"), 16)
            for t in range(NT):
                src = bass.AP(tensor=bias_scratch.tensor, offset=P * (1 - t), ap=[[1, P], [2 * S, 8], [1, S]])
                po.dma_start(hankel[:, t, :].rearrange("p (h s) -> p h s", h=8), src).then_inc(S_("hankel_in"), 16)
            load_gain(9)
            gathers(1)
            load_gain(10)

        @block.tensor
        def _(pe):
            def claim(stage, i=0):
                b = plan.before(stage, i)
                if b:
                    pe.wait_ge(took[b[0]], b[1])
                return banks[:, plan.bank(stage, i), :]

            def tile(n):
                pe.wait_ge(tile_landed[n % NSLOT], 16 * (n // NSLOT + 1))
                return W[:, n % NSLOT, :]

            def std(n):
                return tile(n).rearrange("p (k n) -> p k n", k=KD)

            def transposes(stage, blocks, wait):
                i = 0
                for t in range(NT):
                    for g in range(len(blocks) // 4):
                        wait(t)
                        bank = claim(stage, i)
                        for j in range(4):
                            mm = pe.transpose(bank[:, j * P:(j + 1) * P], blocks[4 * g + j](t), ident)
                        mm.then_inc(pe_filled, 1)
                        i += 1

            def norm_T(n):
                transposes(f"T{n}", [lambda t, b=b: H[:, t, b * P:(b + 1) * P] for b in range(KD)],
                           lambda t: pe.wait_ge(S_("h_ready"), NT * n + t + 1))

            def transposed(stage, n_tiles, act, first=None):
                first = tile_no[stage] if first is None else first
                for i in range(2 * n_tiles):
                    w = std(first + i // 2)
                    bank = claim(stage, i)
                    for b in range(2):
                        c = (i % 2 * 2 + b) * P
                        for k in range(KD):
                            mm = pe.matmul(bank[:, b * S:(b + 1) * S], w[:, k, c:c + P], act[:, k, :],
                                           start=(k == 0), stop=(k == KD - 1))
                    mm.then_inc(pe_filled, 1)

            def natural(stage, n_tiles, act):
                for i in range(2 * n_tiles):
                    w = std(tile_no[stage] + i // 2)
                    bank = claim(stage, i)
                    for k in range(KD):
                        mm = pe.matmul(bank, act[:, k, (i % 2) * P:(i % 2 + 1) * P], w[:, k, :],
                                       start=(k == 0), stop=(k == KD - 1))
                    mm.then_inc(pe_filled, 1)

            def attend(name, units, scores, n_keys, probs_sem, base, between={}):
                def score(u):
                    mm = scores(u, claim(f"{name}_s{u}"))
                    mm.then_inc(pe_filled, 1)
                score(0)
                for u, (p, t) in enumerate(units):
                    if u + 1 < len(units):
                        score(u + 1)
                    for i in between.get(u, ()):
                        ada(f"ada{i}", 0, tile_no[f"ada{i}"])
                    pe.wait_ge(S_(probs_sem), base + u + 1)
                    bank = claim(f"{name}_t{u}")
                    kt = n_keys(t)
                    for h in range(2):
                        for s in range(kt):
                            mm = pe.transpose(bank[:, (h * NT + s) * P:(h * NT + s + 1) * P],
                                              probs[:, u % 2, h * S + s * P:h * S + (s + 1) * P], ident)
                    mm.then_inc(pe_filled, 1)

            def weighted(stage, i, t, heads, PT, values, width, n_keys, last, slot=lambda h: h):
                after(pe, last)
                bank = claim(stage, i)
                for j, h in enumerate(heads):
                    for s in range(n_keys(t)):
                        mm = pe.matmul(bank[:, j * width:(j + 1) * width], PT[:, slot(h), s, t * P:(t + 1) * P],
                                       values(h, s),
                                       start=(s == 0), stop=(s == n_keys(t) - 1))
                mm.then_inc(pe_filled, 1)

            def weighted_rows(l, t):
                sums = [claim(f"p_v{l}{t}", c) for c in range(2)]
                phase = 2 * t + 1
                n = (l * 2 * NT + phase) * STEPS
                before = used_before(l, phase)[1]

                def step(i, start=False, stop=False):
                    for j, r in enumerate(PE_SLOTS):
                        pe.wait_ge(S_("diag_ready"), i * PE_ROWS + (before + j + 1))
                        pe.wait_ge(row_landed[r], i * 16 + 16 * (n + 1))
                        for c in range(2):
                            mm = pe.matmul(sums[c], diag[:, j, :], rows_u[:, r, c * BLK:(c + 1) * BLK],
                                           start=start and j == 0, stop=stop and j == PE_ROWS - 1)
                        mm.then_inc(rows_used["tensor"], 1)

                step(0, start=True)
                with pe.Fori(1, STEPS - 1) as i:
                    step(i)
                step(STEPS - 1, stop=True)

            causal_keys = lambda t: t + 1
            all_keys = lambda t: NT

            def ada(stage, i, n):
                w = std(n)
                bank = claim(stage, i)
                for k in range(KD):
                    mm = pe.matmul(bank, c_rep[:, k, :], w[:, k, :], start=(k == 0), stop=(k == KD - 1))
                mm.then_inc(pe_filled, 1)

            pe.wait_ge(S_("c_ready"), 1)
            for i in range(4):
                ada("ada", i, i)
            pe.wait_ge(S_("rel_in"), 16)
            pe.wait_ge(S_("onehot_in"), 16)
            pe.matmul(claim("bias_rows")[0:8, :], rel_sb[:], onehot, start=True, stop=True).then_inc(pe_filled, 1)
            pe.wait_ge(S_("const_in"), 16)
            norm_T(0)
            after(pe, "T0", 3)
            transposed("z_qk", 2, HT)
            pe.wait_ge(S_("small_in"), 16)
            bank = claim("z_gate")
            wg = part(small, SMALL, "gates").rearrange("p (k n) -> p k n", k=KD)
            for t in range(NT):
                for k in range(KD):
                    mm = pe.matmul(bank[:, t * 8:(t + 1) * 8], HT[:, k, t * P:(t + 1) * P], wg[:, k, :],
                                   start=(k == 0), stop=(k == KD - 1))
            mm.then_inc(pe_filled, 1)
            natural("z_n", 5, HT)
            pe.wait_ge(S_("logf_ready"), 1)
            lf, gcol = stat(0, NT, 4), stat(16, NT, 4)
            bank = claim("m_cum")
            pe.matmul(bank[:, 0:4], tri, lf[:, 0, :], start=True, stop=True)
            pe.matmul(bank[:, 4:8], tri, lf[:, 1, :], start=True, stop=False)
            pe.matmul(bank[:, 4:8], ones, lf[:, 0, :], start=False, stop=True).then_inc(pe_filled, 1)
            pe.wait_ge(S_("g_ready"), 1)
            for p in range(2):
                bank = claim(f"m_g{p}")
                for h in range(2):
                    for t in range(NT):
                        g = gcol[:, t, 2 * p + h:2 * p + h + 1]
                        mm = pe.transpose(bank[:, h * S + t * P:h * S + (t + 1) * P], g.to_broadcast([P, P]), ident)
                mm.then_inc(pe_filled, 1)
            pe.wait_ge(S_("qk_ready"), 1)
            m_units = [(p, t) for p in range(2) for t in range(NT)]

            def m_scores(u, bank):
                p, t = m_units[u]
                for h in range(2):
                    mm = pe.matmul(bank[:, h * S:(h + 1) * S], qkT[:, 2 * p + h, t * P:(t + 1) * P],
                                   qkT[:, 4 + 2 * p + h, :], start=True, stop=True)
                return mm
            attend("m", m_units, m_scores, causal_keys, "m_probs", 0, ADA_IN_M)
            for t in range(NT):
                weighted("m_pv", t, t, range(MH), PT1, lambda h, s: Z[:, s, MV + h * MDH:MV + (h + 1) * MDH], MDH,
                         causal_keys, "m_t3")
            transposes("a_T", [lambda t, b=b: Z[:, t, AQ + b * P:AQ + (b + 1) * P] for b in range(8)],
                       lambda t: pe.wait_ge(S_("rope_done"), 1))
            after(pe, "a_T", 3)
            a_units = [(p, t) for p in range(4) for t in range(NT)]

            def a_scores(u, bank):
                p, t = a_units[u]
                for h in range(2):
                    b, q = place_of(2 * p + h, ADH)
                    mm = pe.matmul(bank[:, h * S:(h + 1) * S], aT[q, b, t * P:(t + 1) * P], aT[q, 4 + b, :],
                                   start=True, stop=True)
                return mm
            attend("a", a_units, a_scores, causal_keys, "probs_ready", 0, ADA_IN_A)
            for t in range(NT):
                weighted("a_pv", t, t, range(AH), PT1, lambda h, s: Z[:, s, AV + h * ADH:AV + (h + 1) * ADH], ADH,
                         causal_keys, "a_t7", slot=head_of)
            transposes("y_T", [lambda t, b=b: Z[:, t, MO + b * P:MO + (b + 1) * P] for b in range(8)],
                       lambda t: pe.wait_ge(S_("y_ready"), NT))
            after(pe, "y_T", 3)
            for c in range(2):
                n = tile_no["merge"] + 3 * c
                for j in range(4):
                    w = std(n + j // 2)
                    bank = claim("merge", 8 * c + j)
                    for k in range(KD):
                        mm = pe.matmul(bank, HT[:, k, (j % 2) * P:(j % 2 + 1) * P], w[:, k, :],
                                       start=(k == 0), stop=(k == KD - 1))
                    mm.then_inc(pe_filled, 1)
                w = std(n + 2)
                for j in range(4):
                    t, m = j // 2, j % 2
                    bank = claim("merge", 8 * c + 4 + j)
                    for k in range(4):
                        mm = pe.matmul(bank, yT[:, 4 * m + k, t * P:(t + 1) * P], w[:, 4 * m + k, :],
                                       start=(k == 0), stop=(k == 3))
                    mm.then_inc(pe_filled, 1)
            transposes("mg_T", [lambda t, b=b: H[:, t, b * P:(b + 1) * P] for b in range(KD)],
                       lambda t: pe.wait_ge(S_("merged_ready"), 4))
            after(pe, "mg_T", 3)
            natural("w_out", 2, HT)
            norm_T(1)
            after(pe, "T1", 3)
            for i in range(NF // 2):
                w = std(tile_no["ff_u0"] + i)
                for stage, c0 in ((f"ff_g{i}", 0), (f"ff_u{i}", 2 * P)):
                    bank = claim(stage)
                    for b in range(2):
                        for k in range(KD):
                            mm = pe.matmul(bank[:, b * S:(b + 1) * S], w[:, k, c0 + b * P:c0 + (b + 1) * P], HT[:, k, :],
                                           start=(k == 0), stop=(k == KD - 1))
                    mm.then_inc(pe_filled, 1)
                if i == 4:
                    norm_T(2)
            for i in range(4):
                claim("down", i)
            after(pe, f"ff_u{NF // 2 - 1}")
            pe.wait_ge(S_("f_ready"), NF // 2)
            for i in range(6):
                w = tile(tile_no["down"] + i).rearrange("p (k n) -> p k n", k=4)
                for j in range(min(4, NF - 4 * i)):
                    k = 4 * i + j
                    for t in range(NT):
                        for c in range(2):
                            mm = pe.matmul(banks[:, plan.bank("down", 2 * c + t), :], fT[:, k, t * P:(t + 1) * P],
                                           w[:, j, c * BLK:(c + 1) * BLK], start=(k == 0), stop=(k == NF - 1))
                mm.then_inc(pe_filled, 1)
            transposed("x_k0", 2, memT)
            natural("x_v0", 2, memT)
            norm_T(4)
            after(pe, "T4", 3)
            transposed("e_z", 4, HT)
            pe.wait_ge(S_("pooled_ready"), 1)
            pw = part(small, SMALL, "pool_w").rearrange("p (g n) -> p g n", g=4)
            for i in range(2):
                bank = claim("e_pool", i)
                for b in range(2):
                    mm = pe.matmul(bank[:, b * S:(b + 1) * S], pw[:, 2 * i + b, :], e_pool[:, 2 * i + b, :],
                                   start=True, stop=True)
                mm.then_inc(pe_filled, 1)
            after(pe, "e_pool", 1)
            natural("e_out", 2, e_yT)

            def odd():
                norm_T(7)
                after(pe, "T7", 3)
                transposed("o_ql", 2, HT)
                w = std(tile_no["o_ik"])
                bank = claim("o_ckv")
                for t in range(NT):
                    for a, b, n in ((0, 0, P), (P, 2 * P, 8)):
                        for k in range(KD):
                            mm = pe.matmul(bank[:, t * (P + 8) + a:t * (P + 8) + a + n], HT[:, k, t * P:(t + 1) * P],
                                           w[:, k, b:b + n], start=(k == 0), stop=(k == KD - 1))
                mm.then_inc(pe_filled, 1)
                bank = claim("o_ik")
                for k in range(KD):
                    mm = pe.matmul(bank[:, 0:S], w[:, k, P:2 * P], HT[:, k, :], start=(k == 0), stop=(k == KD - 1))
                mm.then_inc(pe_filled, 1)
                transposed("o_iq", 1, HT)
                transposed("o_hq", 1, HT)
                natural("o_hf", 1, HT)
                natural("o_hi", 1, HT)
                natural("o_hg", 1, HT)
                pe.wait_ge(S_("ckv_ready"), 1)
                bank = claim("o_cT")
                for t in range(NT):
                    mm = pe.transpose(bank[:, t * P:(t + 1) * P], o_c[:, t, 0:P], ident)
                mm.then_inc(pe_filled, 1)
                transposes("o_kT", [lambda t, b=b: h_kn[:, t, b * P:(b + 1) * P] for b in range(4)],
                           lambda t: pe.wait_ge(S_("forget_ready"), NT))
                pe.wait_ge(S_("hlog_ready"), NT)
                pe.wait_ge(S_("odd_in"), 64)
                after(pe, "o_kT", 1)

                def decays(n):
                    for i in range(2):
                        bank = claim(f"h_d{n}", i)
                        for j in range(2):
                            for t in range(NT):
                                m = h_mask[:, 2 * n if n else t, :]
                                hd = 2 * i + j
                                mm = pe.matmul(bank[:, j * S + t * P:j * S + (t + 1) * P],
                                               h_f[:, t, hd * P:(hd + 1) * P], m, start=True, stop=True)
                        mm.then_inc(pe_filled, 1)

                decays(0)
                for n, h in enumerate(LEVELS):
                    if n + 1 < len(LEVELS):
                        decays(n + 1)
                    pe.wait_ge(S_("level_ready"), n + 1)
                    for i in range(1 if h == P else NT):
                        bank = claim(f"h_s{n}", i)
                        for hd in range(HH):
                            s = slice(i * P, (i + 1) * P)
                            q = slice(P, 2 * P) if h == P else s
                            mm = pe.matmul(bank[:, hd * P:(hd + 1) * P], h_KE[n % 2][:, hd, s], h_QE[n % 2][:, hd, q],
                                           start=True, stop=True)
                        mm.then_inc(pe_filled, 1)
                for t in range(NT):
                    bank = claim("h_diag", t)
                    for hd in range(HH):
                        mm = pe.matmul(bank[:, hd * P:(hd + 1) * P], h_kT[:, hd, t * P:(t + 1) * P],
                                       h_qT[:, hd, t * P:(t + 1) * P], start=True, stop=True)
                    mm.then_inc(pe_filled, 1)
                pe.wait_ge(S_("hscores_ready"), NT)
                for t in range(NT):
                    bank = claim("h_pv", t)
                    for hd in range(HH):
                        d = slice(hd * P, (hd + 1) * P)
                        mm = pe.matmul(bank[:, d], h_sc[:, t, hd, :], h_i[:, t, d], start=True, stop=(t == 0))
                        if t:
                            mm = pe.matmul(bank[:, d], h_x[:, hd, :], h_i[:, 0, d], start=False, stop=True)
                    mm.then_inc(pe_filled, 1)
                for u in range(8):
                    t, p = u // 4, u % 4
                    bank = claim("idx", u)
                    for h in range(2):
                        b, q = place_of(2 * p + h, IDH)
                        mm = pe.matmul(bank[:, h * S:(h + 1) * S], o_iqT[q, b, t * P:(t + 1) * P], o_ikT[q, :],
                                       start=True, stop=True)
                    mm.then_inc(pe_filled, 1)
                o_units = [(p, t) for t in range(NT) for p in range(4)]
                pe.wait_ge(S_("hankel_in"), 32)

                def o_scores(u, bank):
                    p, t = o_units[u]
                    for h in range(2):
                        hd = 2 * p + h
                        pe.matmul(bank[:, h * S:(h + 1) * S], o_qT[:, hd, t * P:(t + 1) * P], o_cT,
                                  start=True, stop=False)
                        mm = pe.matmul(bank[:, h * S:(h + 1) * S], flip, hankel[:, t, hd * S:(hd + 1) * S],
                                       start=False, stop=True)
                    return mm
                attend("o", o_units, o_scores, causal_keys, "probs_ready", 12)
                for i in range(4):
                    t, g = i // 2, i % 2
                    weighted("o_pv", i, t, range(4 * g, 4 * g + 4), o_PT, lambda h, s: o_c[:, s, 0:P], P,
                             causal_keys, "o_t7")
                transposes("lat_T", [lambda t, b=b: H[:, t, b * P:(b + 1) * P] for b in range(KD)],
                           lambda t: after(pe, "o_pv", 2 * t + 1))
                after(pe, "lat_T", 3)
                uv = part(small, SMALL, "w_uv").rearrange("p (h n) -> p h n", h=CH)
                for t in range(NT):
                    bank = claim("o_yc", t)
                    for h in range(CH):
                        mm = pe.matmul(bank[:, h * CDH:(h + 1) * CDH], HT[:, h, t * P:(t + 1) * P], uv[:, h, :],
                                       start=True, stop=True)
                    mm.then_inc(pe_filled, 1)
                transposes("o_yT", [lambda t, b=b: H[:, t, b * P:(b + 1) * P] if b < 4 else
                                    yd[:, t, (b - 4) * P:(b - 3) * P] for b in range(KD)],
                           lambda t: after(pe, "o_yc", t))
                after(pe, "o_yT", 3)
                natural("o_out", 2, HT)

            for l in range(2):
                if l:
                    odd()
                norm_T(5 + 3 * l)
                after(pe, f"T{5 + 3 * l}", 3)
                transposed(f"x_q{l}", 2, HT)
                after(pe, f"x_q{l}", 3)
                x_units = [(p, t) for p in range(2) for t in range(NT)]

                def x_scores(u, bank):
                    p, t = x_units[u]
                    for h in range(2):
                        for j in range(2):
                            b = 2 * (2 * p + h) + j
                            mm = pe.matmul(bank[:, h * S:(h + 1) * S], x_qT[:, b, t * P:(t + 1) * P], x_kTs[l][:, b, :],
                                           start=(j == 0), stop=(j == 1))
                    return mm
                attend(f"x{l}", x_units, x_scores, all_keys, "probs_ready", 8 + 12 * l)
                for i in range(4):
                    t, g = i // 2, i % 2
                    weighted(f"x_pv{l}", i, t, (2 * g, 2 * g + 1), x_PT,
                             lambda h, s: x_vs[l][:, s, h * XDH:(h + 1) * XDH], XDH, all_keys, f"x{l}_t3")
                transposes(f"x_oT{l}", [lambda t, b=b: H[:, t, b * P:(b + 1) * P] for b in range(KD)],
                           lambda t: after(pe, f"x_pv{l}", 2 * t + 1))
                after(pe, f"x_oT{l}", 3)
                natural(f"x_o{l}", 2, HT)
                norm_T(6 + 3 * l)
                after(pe, f"T{6 + 3 * l}", 3)
                transposed(f"p_q{l}", 4, HT)
                keys = tile(tile_no[f"p_s{l}"])
                after(pe, f"p_q{l}", 7)
                for i in range(8):
                    bank = claim(f"p_s{l}", i)
                    t = i // 4
                    for j in range(4):
                        b = 4 * (i % 4) + j
                        mm = pe.matmul(bank[:, j * P:(j + 1) * P], p_qT[:, b, t * P:(t + 1) * P],
                                       keys[:, b * NK:(b + 1) * NK], start=True, stop=True)
                    mm.then_inc(pe_filled, 1)
                if l == 0:
                    transposed("x_k1", 2, memT)
                    natural("x_v1", 2, memT)
                for t in range(NT):
                    weighted_rows(l, t)

        @block.scalar
        def _(act):
            step = Steps(act, "scalar_step", "scalar")

            def rstd(n_heads, sums, out, width, signal=None):
                step(act.activation(out, sums, ACT.Ln, scale=1.0 / width, bias=eps_col))
                step(act.activation(out, out, ACT.Exp, scale=-0.5), signal)

            eps_col = stat(600, 1)

            def norm(n, src, ready):
                for t in range(NT):
                    ready(t)
                    at = n % 2 * NT + t
                    step(act.activation(junk[:], src[:, t, :], ACT.Square, accum_out=stat(604 + at, 1)))
                    rstd(1, stat(604 + at, 1), stat(608 + at, 1), D, "rstd_ready")

            def attend(name, units, scale, PT, n_keys, base, sums):
                def probabilities(u):
                    p, t = units[u]
                    act.wait_ge(S_("smax_ready"), base + u + 1)
                    for h in range(2):
                        hd = 2 * p + h
                        step(act.activation(probs[:, u % 2, h * S:(h + 1) * S], scrA[:, u % 2, h * S:(h + 1) * S], ACT.Exp,
                                            bias=stat(612 + 2 * (u % 2) + h, 1), scale=scale,
                                            accum_out=sums[:, t, hd:hd + 1]), "probs_ready" if h else None)
                probabilities(0)
                for u, (p, t) in enumerate(units):
                    if u + 1 < len(units):
                        probabilities(u + 1)
                    leave(name, u, p, t, PT, n_keys)

            def leave(name, u, p, t, PT, n_keys):
                bank = filled(act, f"{name}_t{u}")
                kt = n_keys(t)
                src = bank.rearrange("p (h s t) -> p h s t", h=2, s=NT)[:, :, 0:kt, :]
                step.free(act.activation(PT[:, 2 * p:2 * p + 2, 0:kt, t * P:(t + 1) * P], src, ACT.Copy),
                          f"{name}_t{u}")

            act.dma_start(cols[:], io["cols"]).then_inc(S_("cols_in"), 16)
            act.dma_start(X[:], io["x"].rearrange("b (t p) d -> p (b t) d", p=P)).then_inc(S_("x_in"), 16)
            a, _ = ROWS["ada_b"]
            act.dma_start(mod[:, 0:2, :].rearrange("p a b -> p (a b)"), io["rows"][0:1, a:a + 2 * D].to_broadcast([P, 2 * D]))\
                .then_inc(S_("ada_b_in"), 16)
            a, _ = ROWS["norm"]
            act.dma_start(gain[:, 0, :], io["rows"][0:1, a:a + D].to_broadcast([P, D])).then_inc(S_("first_gain_in"), 16)
            act.wait_ge(S_("cols_in"), 16)
            step(act.activation(stat(620, 8), part(cols, COLS, "c"), ACT.Silu), "silu_c")
            act.wait_ge(S_("eps_set"), 1)
            act.wait_ge(S_("x_in"), 16)
            norm(0, X, lambda t: None)
            act.wait_ge(S_("conv_ready"), 1)
            step(act.activation(qkT, qkT, ACT.Silu), "qk_ready")
            act.wait_ge(S_("mo_ready"), NT)
            for t in range(NT):
                step(act.activation(Z[:, t, MO:MO + MW], Z[:, t, MO:MO + MW], ACT.Sigmoid), "mo_gated")
            act.wait_ge(S_("absf_ready"), 1)
            step(act.activation(stat(32, 8), stat(32, 8), ACT.Exp, scale=-1.0))
            step(act.activation(stat(32, 8), stat(32, 8), ACT.Ln, bias=1.0), "log1p_ready")
            m_units = [(p, t) for p in range(2) for t in range(NT)]
            for u, (p, t) in enumerate(m_units):
                act.wait_ge(S_("m_max_ready"), u + 1)
                for h in range(2):
                    step(act.activation(scrA[:, u % 2, h * S:(h + 1) * S], scrA[:, u % 2, h * S:(h + 1) * S], ACT.Exp,
                                        bias=stat(64 + 4 * t + 2 * p + h, 1)), "m_w_ready" if h else None)
                if u:
                    leave("m", u - 1, *m_units[u - 1], PT1, lambda t: t + 1)
            leave("m", 3, *m_units[3], PT1, lambda t: t + 1)
            act.wait_ge(S_("m_stab_ready"), 1)
            step(act.activation(stat(80, 8), stat(80, 8), ACT.Exp, scale=-1.0), "m_floor_ready")
            act.wait_ge(S_("hm_squares"), 1)
            rstd(MH, stat(96, 8), stat(104, 8), MDH, "hm_rstd")
            act.wait_ge(S_("angle_ready"), 1)
            step(act.activation(stat(128, 128), stat(128, 128), ACT.Sin), "sincos_ready")
            a_units = [(p, t) for p in range(4) for t in range(NT)]
            attend("a", a_units, ADH ** -0.5, PT1, lambda t: t + 1, 0, stat(272, NT, 8))
            for c in range(2):
                act.wait_ge(S_("gate_pre"), c + 1)
                step(act.activation(sg, sg, ACT.Sigmoid), "gate_ready")
            norm(1, X, lambda t: after(act, "w_out", 2 + t))
            for i in range(NF // 2):
                bank = filled(act, f"ff_g{i}")
                if i >= 2:
                    act.wait_ge(S_("f_ready"), i - 1)
                step.free(act.activation(silu_g[:, i % 2, :], bank, ACT.Silu), f"ff_g{i}")
                if i == 2:
                    act.wait_ge(S_("mem_in"), 16)
                    norm(2, mem_in, lambda t: None)
            norm(3, X, lambda t: after(act, "down", 2 + t))
            norm(4, X, lambda t: act.wait_ge(S_("h_ready"), 3 * NT + t + 1))
            for l in range(2):
                if l:
                    norm(7, X, lambda t: act.wait_ge(S_("x_ready"), t + 1))
                    for t in range(NT):
                        bank = filled(act, "o_hf", t)
                        step.free(act.activation(h_f[:, t, :], bank, ACT.Sigmoid), "o_hf", t)
                    act.wait_ge(S_("hg_in"), NT)
                    for t in range(NT):
                        step(act.activation(h_g[:, t, :], h_g[:, t, :], ACT.Silu), "hg_ready")
                    act.wait_ge(S_("lb_diff"), 1)
                    step(act.activation(lb_row[:, 0, :], lb_row[:, 0, :], ACT.Exp))
                    step(act.activation(lb_row[:, 1, :], lb_row[:, 1, :], ACT.Exp), "lb_exp")
                    act.wait_ge(S_("ckv_squares"), 1)
                    rstd(1, stat(288, 2), stat(290, 2), CR, "ckv_rstd")
                    for t in range(NT):
                        act.wait_ge(S_("forget_ready"), t + 1)
                        step(act.activation(h_f[:, t, :], h_f[:, t, :], ACT.Ln), "hlog_ready")
                    for n in range(len(LEVELS)):
                        for i in range(2):
                            bank = filled(act, f"h_d{n}", i)
                            if n >= 2:
                                act.wait_ge(S_("level_ready"), n - 1)
                            step.free(act.activation(h_E[n % 2][:, 2 * i:2 * i + 2, :].rearrange("p a b -> p (a b)"), bank,
                                                     ACT.Exp), f"h_d{n}", i)
                    act.wait_ge(S_("yd_squares"), 1)
                    rstd(HH, stat(296, 8), stat(304, 8), P, "yd_rstd")
                    for u in range(8):
                        bank = filled(act, "idx", u)
                        if u >= 2:
                            act.wait_ge(S_("rel_used"), u - 1)
                        if u == 0:
                            act.wait_ge(S_("hgrn_done"), 1)
                        step.free(act.activation(o_rel[:, u % 2, :], bank, ACT.Relu, scale=IDH ** -0.5), "idx", u)
                    attend("o", [(p, t) for t in range(NT) for p in range(4)], 1.0, o_PT, lambda t: t + 1, 12,
                           stat(272, NT, 8))
                norm(5 + 3 * l, X, lambda t: after(act, "o_out" if l else "e_out", 2 + t))
                attend(f"x{l}", [(p, t) for p in range(2) for t in range(NT)], XDH ** -0.5, x_PT, lambda t: NT,
                       8 + 12 * l, stat(272, NT, 8))
                norm(6 + 3 * l, X, lambda t: after(act, f"x_o{l}", 2 + t))
                act.wait_ge(S_("top_ready"), NT * l + 1)
                step(act.activation(p_g[:, 0, :], p_g[:, 0, :], ACT.Exp), "top_exp")
                for t in range(NT):
                    act.wait_ge(S_("dots_ready"), NT * l + t + 1)
                    step(act.activation(p_act[:, t, :], p_act[:, t, :], ACT.Gelu_apprx_tanh), "gelu_ready")
                    act.wait_ge(S_("row_weights_ready"), NT * l + t + 1)
                    before = used_before(l, 2 * t + 1)[1]

                    def diagonals(i, first):
                        for j, r in enumerate(PE_SLOTS):
                            if not first:
                                act.wait_ge(rows_used["tensor"], i * PE_ROWS + (before - PE_ROWS + j + 1))
                            act.activation(diag[:, j, :], ident, ACT.Copy, scale=p_w[:, t, bass.ds(i * RING + r, 1)])\
                                .then_inc(S_("diag_ready"), 1)

                    diagonals(0, True)
                    with act.Fori(1, STEPS) as i:
                        diagonals(i, False)
                    if t == 0:
                        act.wait_ge(S_("top_ready"), NT * l + 2)
                        step(act.activation(p_g[:, 1, :], p_g[:, 1, :], ACT.Exp), "top_exp")
            norm(10, X, lambda t: act.wait_ge(S_("x_ready"), NT + t + 1))

        @block.vector
        def _(v):
            step = Steps(v, "vector_step", "vector")

            def tt(out, a, b, op, signal=None):
                step(v.tensor_tensor(out, a, b, op), signal)

            def ts(out, a, s1, op0, s2=None, op1=None, signal=None):
                step(v.tensor_scalar(out, a, s1, s2, op0, op1) if op1 else v.tensor_scalar(out, a, s1, None, op0), signal)

            def stt(out, a, s, b, op0, op1, signal=None, accum=None):
                step(v.scalar_tensor_tensor(out=out, in0=a, scalar=s, in1=b, op0=op0, op1=op1, accum_out=accum), signal)

            def norm(n, src, g, shift=None, signal="h_ready", dst=H):
                for t in range(NT):
                    v.wait_ge(S_("rstd_ready"), NT * n + t + 1)
                    stt(dst[:, t, :], src[:, t, :], stat(608 + n % 2 * NT + t, 1), g, ALU.mult, ALU.mult,
                        signal if shift is None else None)
                    if shift is not None:
                        tt(H[:, t, :], H[:, t, :], shift, ALU.add, signal)

            def gain_of(n):
                v.wait_ge(S_(f"gain_in{n % 2}" if n else "first_gain_in"), 16 * max(1, (n + 1) // 2))
                return gain[:, n % 2, :]

            def take_T(stage, dst, n_blocks=KD):
                i = 0
                for t in range(NT):
                    for g in range(n_blocks // 4):
                        bank = filled(v, stage, i)
                        step.free(v.tensor_copy(dst[:, 4 * g:4 * g + 4, t * P:(t + 1) * P],
                                                bank.rearrange("p (b t) -> p b t", b=4)), stage, i)
                        i += 1

            def take_blocks(stage, n, dst, scale=None, first=0):
                for i in range(first, first + n):
                    bank = filled(v, stage, i).rearrange("p (b t) -> p b t", b=2)
                    out = dst[:, 2 * i:2 * i + 2, :]
                    ins = v.tensor_copy(out, bank) if scale is None else v.tensor_scalar(out, bank, scale, None, ALU.mult)
                    step.free(ins, stage, i)

            def softmax_max(name, units, mask, scale, between={}):
                for u, (p, t) in enumerate(units):
                    bank = filled(v, f"{name}_s{u}").rearrange("p (h s) -> p h s", h=2)
                    out = scrA[:, u % 2, :].rearrange("p (h s) -> p h s", h=2)
                    if u >= 2:
                        v.wait_ge(S_("probs_ready"), self_base[0] + u - 1)
                    if mask is None:
                        ins = v.tensor_copy(out, bank)
                    else:
                        ins = v.tensor_tensor(out, bank, mask(t).unsqueeze(1).to_broadcast([P, 2, S]), ALU.add)
                    step.free(ins, f"{name}_s{u}")
                    step(v.tensor_reduce(stat(616, 2), out, AXX, ALU.max))
                    ts(stat(612 + 2 * (u % 2), 2), stat(616, 2), -scale, ALU.mult, signal="smax_ready")
                    for i in between.get(u - 1, ()):
                        take_ada(f"ada{i}", 0, i)
                self_base[0] += len(units)
            self_base = [0]

            def take_weighted(stage, i, out, sums, width, ready=None):
                n = out.shape[-1] // width
                bank = filled(v, stage, i)
                r = stat(640 - 8, n)
                if len(sums.shape) == 4:
                    r = r.rearrange("p (a b c) -> p a b c", b=2, c=2)
                step(v.reciprocal(r, sums))
                step.free(v.tensor_tensor(out.rearrange("p (h d) -> p h d", h=n), bank.rearrange("p (h d) -> p h d", h=n),
                                          stat(640 - 8, n).unsqueeze(2).to_broadcast([P, n, width]), ALU.mult), stage, i)

            def head_norm(x, heads, squares, tmp, t):
                tt(tmp, x, x, ALU.mult)
                step(v.tensor_reduce(squares[:, t, :], tmp.rearrange("p (h d) -> p h d", h=heads), AXX, ALU.add))

            def add_to_x(stage, scale=None):
                for i in range(4):
                    c, t = i // 2, i % 2
                    xs = X[:, t, c * BLK:(c + 1) * BLK]
                    bank = filled(v, stage, i)
                    if scale is None:
                        step.free(v.tensor_tensor(xs, bank, xs, ALU.add), stage, i)
                    else:
                        step(v.tensor_tensor(junk_v, bank, scale[:, c * BLK:(c + 1) * BLK], ALU.mult))
                        step.free(v.tensor_tensor(xs, junk_v, xs, ALU.add), stage, i)

            junk_v = area(22048, 512)
            step(v.memset(stat(600, 1), EPS), "eps_set")
            v.wait_ge(S_("silu_c"), 1)
            step(v.tensor_copy(c_rep[:], stat(620, 8).unsqueeze(2).to_broadcast([P, KD, P])), "c_ready")
            v.wait_ge(S_("ada_b_in"), 16)
            modf = mod.rearrange("p a b -> p (a b)")

            def take_ada(stage, i, n):
                m = modf[:, n * BLK:(n + 1) * BLK]
                bank = filled(v, stage, i)
                step.free(v.tensor_tensor(m, bank, m, ALU.add), stage, i)

            for i in range(4):
                take_ada("ada", i, i)
            stt(mod[:, 1, :], mod[:, 1, :], 1.0, gain_of(0), ALU.add, ALU.mult)
            bank = filled(v, "bias_rows")
            v.wait_ge(S_("onehot_in"), 16)
            step.free(v.tensor_copy(rb_sb, bank[0:8, :]), "bias_rows")
            step(v.tensor_copy(rb_sb[:, 0:1], rb_sb[:, 0:1]), "bias_rows_ready")
            norm(0, X, mod[:, 1, :], mod[:, 0, :])
            take_T("T0", HT)
            step(v.memset(qk_raw[:, :, 0:3], 0.0))
            bq = part(cols, COLS, "b_qk")
            for i in range(4):
                bank = filled(v, "z_qk", i)
                step(v.tensor_scalar(qk_raw[:, 2 * i, 3:], bank[:, 0:S], bq[:, 2 * i:2 * i + 1], None, ALU.add))
                step.free(v.tensor_scalar(qk_raw[:, 2 * i + 1, 3:], bank[:, S:2 * S], bq[:, 2 * i + 1:2 * i + 2], None,
                                          ALU.add), "z_qk", i)
            v.wait_ge(S_("b_rows_in"), 16)
            bank = filled(v, "z_gate")
            gates = stat(48, NT, 8)
            step.free(v.tensor_tensor(gates, bank[:, 0:16].rearrange("p (t g) -> p t g", t=NT),
                                      b_rows[:, 0:8].unsqueeze(1).to_broadcast([P, NT, 8]), ALU.add), "z_gate")
            absf = stat(32, NT, 4)
            stt(absf, gates[:, :, 4:8], -1.0, gates[:, :, 4:8], ALU.mult, ALU.max, "absf_ready")
            cw, cb = part(cols, COLS, "conv_w"), part(cols, COLS, "conv_b")
            for b in range(8):
                ts(qkT[:, b, :], qk_raw[:, b, 0:S], cw[:, b:b + 1], ALU.mult, cb[:, b:b + 1], ALU.add)
                for j in range(1, 4):
                    stt(qkT[:, b, :], qk_raw[:, b, j:j + S], cw[:, 8 * j + b:8 * j + b + 1], qkT[:, b, :],
                        ALU.mult, ALU.add, "conv_ready" if (b, j) == (7, 3) else None)
            for i in range(10):
                f, t = i // 2, i % 2
                bank = filled(v, "z_n", i)
                step.free(v.tensor_tensor(Z[:, t, f * BLK:(f + 1) * BLK], bank, b_rows[:, 8 + f * BLK:8 + (f + 1) * BLK],
                                          ALU.add), "z_n", i)
                if f == 1:
                    step(v.tensor_copy(Z[:, t, MO:MO + 1], Z[:, t, MO:MO + 1]), "mo_ready")
            v.wait_ge(S_("log1p_ready"), 1)
            lf, gcol, cum = stat(0, NT, 4), stat(16, NT, 4), stat(24, NT, 4)
            stt(lf, gates[:, :, 4:8], 0.0, absf, ALU.min, ALU.subtract, "logf_ready")
            bank = filled(v, "m_cum")
            step.free(v.tensor_copy(cum, bank[:, 0:8].rearrange("p (t g) -> p t g", t=NT)), "m_cum")
            tt(gcol, gates[:, :, 0:4], cum, ALU.subtract, "g_ready")
            negM = stat(64, NT, 4)
            m_units = [(p, t) for p in range(2) for t in range(NT)]
            den = stat(88, NT, 4)
            g_row = area(18976 + 1024, 2, 512)
            for p in range(2):
                bank = filled(v, f"m_g{p}")
                step.free(v.tensor_copy(g_row[:, p, :], bank), f"m_g{p}")

            def m_log(u):
                p, t = m_units[u]
                w = scrA[:, u % 2, :].rearrange("p (h s) -> p h s", h=2)
                tt(w, g_row[:, p, :].rearrange("p (h s) -> p h s", h=2),
                   causal[:, t, :].unsqueeze(1).to_broadcast([P, 2, S]), ALU.add)
                step(v.tensor_reduce(stat(616, 2), w, AXX, ALU.max))
                ts(negM[:, t, 2 * p:2 * p + 2], stat(616, 2), 0.0, ALU.max, -1.0, ALU.mult, signal="m_max_ready")

            v.wait_ge(S_("scratch_written"), 16)
            m_log(0)
            for u, (p, t) in enumerate(m_units):
                if u + 1 < 4:
                    m_log(u + 1)
                v.wait_ge(S_("m_w_ready"), u + 1)
                bank = filled(v, f"m_s{u}")
                if u >= 2:
                    v.wait_ge(pe_filled, plan.mark(f"m_t{u - 2}"))
                for h in range(2):
                    c = slice(h * S, (h + 1) * S)
                    ins = v.scalar_tensor_tensor(out=probs[:, u % 2, c], in0=bank[:, c], scalar=MDH ** -0.5,
                                                 in1=scrA[:, u % 2, c], op0=ALU.mult, op1=ALU.mult,
                                                 accum_out=den[:, t, 2 * p + h:2 * p + h + 1])
                    if h:
                        step.free(ins, f"m_s{u}")
                    else:
                        step(ins)
                step(v.tensor_copy(probs[:, u % 2, 0:1], probs[:, u % 2, 0:1]), "m_probs")
                if u == 1:
                    v.wait_ge(S_("ada_b_rest_in"), 16)
                if u:
                    for i in ADA_IN_M[u - 1]:
                        take_ada(f"ada{i}", 0, i)
            for i in ADA_IN_M[3]:
                take_ada(f"ada{i}", 0, i)
            step(v.memset(junk_v[:, 0:1], 0.0), "m_row_free")
            floor = stat(80, NT, 4)
            tt(floor, cum, negM, ALU.subtract, "m_stab_ready")
            stt(den, den, -1.0, den, ALU.mult, ALU.max)
            v.wait_ge(S_("m_floor_ready"), 1)
            tt(den, den, floor, ALU.max)
            step(v.reciprocal(den, den))
            hm = area(23072, NT, 512)
            sq = stat(96, NT, 4)
            for t in range(NT):
                bank = filled(v, "m_pv", t)
                step.free(v.tensor_tensor(hm[:, t, :].rearrange("p (h d) -> p h d", h=MH),
                                          bank.rearrange("p (h d) -> p h d", h=MH),
                                          den[:, t, :].unsqueeze(2).to_broadcast([P, MH, MDH]), ALU.mult), "m_pv", t)
                head_norm(hm[:, t, :], MH, sq, area(22560, 512), t)
            step(v.tensor_copy(sq, sq), "hm_squares")
            v.wait_ge(S_("hm_rstd"), 1)
            v.wait_ge(S_("m_row_in"), 16)
            v.wait_ge(S_("mo_gated"), NT)
            for t in range(NT):
                x = hm[:, t, :]
                tt(x.rearrange("p (h d) -> p h d", h=MH), x.rearrange("p (h d) -> p h d", h=MH),
                   stat(104, NT, 4)[:, t, :].unsqueeze(2).to_broadcast([P, MH, MDH]), ALU.mult)
                tt(x, x, m_row, ALU.mult)
                tt(Z[:, t, MO:MO + MW], x, Z[:, t, MO:MO + MW], ALU.mult)
            v.wait_ge(S_("pos_in"), 16)
            step(v.tensor_copy(stat(260, 2), pos_i[:]))
            TWO_PI = [6.28125, 1.9353071795e-3, 1.0253e-11]
            ang, turns = stat(320, NT, 32), stat(384, NT, 32)
            sc = stat(128, 2, NT, 32)
            for t in range(NT):
                ts(ang[:, t, :], freq, stat(260 + t, 1), ALU.mult)
            ts(turns, ang, 1 / (2 * np.pi), ALU.mult, 12582912.0, ALU.add)
            ts(turns, turns, 12582912.0, ALU.subtract)
            for c in TWO_PI:
                stt(ang, turns, -c, ang, ALU.mult, ALU.add)
            ts(sc[:, 0, :, :], ang, 3.1415925, ALU.min, -3.1415925, ALU.max)
            stt(ang, ang, -1.0, ang, ALU.mult, ALU.max)
            ts(sc[:, 1, :, :], ang, -1.0, ALU.mult, float(np.float32(np.pi / 2)), ALU.add, signal="angle_ready")
            v.wait_ge(S_("sincos_ready"), 1)
            for t in range(NT):
                x = Z[:, t, AQ:AQ + 2 * AW].rearrange("p (h a d) -> p h a d", a=2, d=32)
                tmp = [rope_t[:, j, :].rearrange("p (h d) -> p h d", d=32) for j in range(4)]
                sin, cos = (sc[:, j, t, :].unsqueeze(1).to_broadcast([P, 16, 32]) for j in range(2))
                x1, x2 = x[:, :, 0, :], x[:, :, 1, :]
                for j, (a, b) in enumerate(((x1, cos), (x2, sin), (x2, cos), (x1, sin))):
                    tt(tmp[j], a, b, ALU.mult)
                tt(x1, tmp[0], tmp[1], ALU.subtract)
                tt(x2, tmp[2], tmp[3], ALU.add, "rope_done" if t else None)
            take_T("a_T", aT)
            a_units = [(p, t) for p in range(4) for t in range(NT)]
            softmax_max("a", a_units, lambda t: causal[:, t, :], ADH ** -0.5, ADA_IN_A)
            stt(mod[:, 4, :], mod[:, 4, :], 1.0, gain_of(1), ALU.add, ALU.mult)
            sums = stat(272, NT, 8)
            for t in range(NT):
                by_head = sums[:, t, :].rearrange("p (a b c) -> p a c b", b=2, c=2)
                take_weighted("a_pv", t, Z[:, t, AQ:AQ + AW], by_head, ADH)
                step(v.tensor_copy(Z[:, t, AQ:AQ + 1], Z[:, t, AQ:AQ + 1]), "y_ready")
            take_T("y_T", yT)
            v.wait_ge(S_("b_g_in"), 16)
            b_g = area(0, 2, D)
            for c in range(2):
                for j in range(4):
                    bank = filled(v, "merge", 8 * c + j)
                    step.free(v.tensor_tensor(sg[:, j, :], bank, b_g[:, j // 2, c * BLK:(c + 1) * BLK], ALU.add),
                              "merge", 8 * c + j)
                step(v.tensor_copy(sg[:, 0, 0:1], sg[:, 0, 0:1]), "gate_pre")
                v.wait_ge(S_("gate_ready"), c + 1)
                for t in range(NT):
                    h = H[:, t, c * BLK:(c + 1) * BLK]
                    for m in range(2):
                        i = 8 * c + 4 + 2 * t + m
                        bank = filled(v, "merge", i)
                        step.free(v.tensor_tensor(sg[:, 2 * m + t, :], bank, sg[:, 2 * m + t, :], ALU.mult), "merge", i)
                    tt(h, sg[:, t, :], sg[:, 2 + t, :], ALU.add, "merged_ready")
            take_T("mg_T", HT)
            add_to_x("w_out", mod[:, 2, :])
            norm(1, X, mod[:, 4, :], mod[:, 3, :])
            take_T("T1", HT)
            for i in range(NF // 2):
                after(v, f"ff_g{i}")
                bank = filled(v, f"ff_u{i}")
                f = fT[:, 2 * i:2 * i + 2, :].rearrange("p a b -> p (a b)")
                step.free(v.tensor_tensor(f, bank, silu_g[:, i % 2, :], ALU.mult), f"ff_u{i}")
                step(v.tensor_copy(f[:, 0:1], f[:, 0:1]), "f_ready")
                if i == 3:
                    norm(2, mem_in, gain_of(2))
                if i == 4:
                    take_T("T2", memT)
            add_to_x("down", mod[:, 5, :])
            norm(3, X, gain_of(3), dst=X)
            norm(4, X, gain_of(4))

            def take_mem(l):
                take_blocks(f"x_k{l}", 4, x_kTs[l])
                if l:
                    v.wait_ge(pe_filled, plan.mark(f"x_v{l}", 3))
                for i in range(4):
                    c, t = i // 2, i % 2
                    bank = filled(v, f"x_v{l}", i)
                    step.free(v.tensor_copy(x_vs[l][:, t, c * BLK:(c + 1) * BLK], bank), f"x_v{l}", i)

            take_mem(0)
            take_T("T4", HT)
            step(v.memset(e_pv[:, :, 0:16], 0.0))
            step(v.memset(e_cu[:, :, 0:2], 0.0))
            take_blocks("e_z", 2, e_z)
            step(v.tensor_copy(e_pv[:, :, 16:], e_z[:, 0:4, :]))
            v.wait_ge(S_("inv_in"), 16)
            for g in range(4):
                src = e_pv[:, g, :]
                for j in range(g + 1):
                    dst = e_t[:, j % 2, :]
                    w = 1 << j
                    tt(dst[:, w:], src[:, w:], src[:, 0:S + 16 - w], ALU.add)
                    step(v.tensor_copy(dst[:, 0:w], src[:, 0:w]))
                    src = dst
                tt(e_pool[:, g, :], src[:, 16:], e_inv[:, g, :], ALU.mult)
                tt(e_pool[:, g, :], e_pool[:, g, :], e_pv[:, g, 16:], ALU.subtract, "pooled_ready" if g == 3 else None)
            take_blocks("e_z", 4, e_z, first=2)
            ec = part(cols, COLS, "even_conv")
            tt(e_cu[:, :, 2:], e_z[:, 8:12, :], e_z[:, 4:8, :], ALU.mult)
            for b in range(4):
                y = e_yT[:, b, :]
                ts(y, e_cu[:, b, 0:S], ec[:, b:b + 1], ALU.mult)
                for j in (1, 2):
                    stt(y, e_cu[:, b, j:j + S], ec[:, 4 * j + b:4 * j + b + 1], y, ALU.mult, ALU.add)
            take_blocks("e_z", 2, e_z, first=6)
            tt(e_yT[:, 0:4, :], e_yT[:, 0:4, :], e_z[:, 12:16, :], ALU.mult)
            ps = part(cols, COLS, "pool_scale")
            for i in range(2):
                bank = filled(v, "e_pool", i)
                for b in range(2):
                    g = 2 * i + b
                    ins = v.tensor_scalar(e_yT[:, 4 + g, :], bank[:, b * S:(b + 1) * S], ps[:, g:g + 1], None, ALU.mult)
                    if b:
                        step.free(ins, "e_pool", i)
                    else:
                        step(ins)
            add_to_x("e_out")

            def odd():
                norm(7, X, gain_of(7))
                take_T("T7", HT)
                take_blocks("o_ql", 4, o_qT, CR ** -0.5)
                bank = filled(v, "o_ckv")
                step.free(v.tensor_copy(o_c, bank[:, 0:NT * (P + 8)].rearrange("p (t n) -> p t n", t=NT)), "o_ckv")
                bank = filled(v, "o_ik")
                step.free(v.tensor_copy(o_ikT, bank[:, 0:S]), "o_ik")
                take_blocks("o_iq", 2, o_iqT)
                take_blocks("o_hq", 2, h_qT)
                v.wait_ge(S_("odd_in"), 64)
                tmp = h_KE[0][:, 0:2, :].rearrange("p a b -> p (a b)")
                tt(tmp, lb_row[:, 0, :], lb_row[:, 1, :], ALU.max)
                tt(lb_row[:, 0, :], lb_row[:, 0, :], tmp, ALU.subtract)
                tt(lb_row[:, 1, :], lb_row[:, 1, :], tmp, ALU.subtract, "lb_diff")
                for t in range(NT):
                    bank = filled(v, "o_hi", t)
                    step.free(v.tensor_copy(h_i[:, t, :], bank), "o_hi", t)
                for t in range(NT):
                    bank = filled(v, "o_hg", t)
                    step.free(v.tensor_copy(h_g[:, t, :], bank), "o_hg", t)
                    step(v.tensor_copy(h_g[:, t, 0:1], h_g[:, t, 0:1]), "hg_in")
                for t in range(NT):
                    stt(h_QE[0][:, 0, 0:P], o_c[:, t, 0:P], 1.0, o_c[:, t, 0:P], ALU.mult, ALU.mult,
                        accum=stat(288 + t, 1))
                step(v.tensor_copy(stat(288, 2), stat(288, 2)), "ckv_squares")
                v.wait_ge(S_("lb_exp"), 1)
                tt(tmp, lb_row[:, 0, :], lb_row[:, 1, :], ALU.add)
                step(v.reciprocal(tmp, tmp))
                tt(lb_row[:, 0, :], lb_row[:, 0, :], tmp, ALU.mult)
                ts(lb_row[:, 1, :], lb_row[:, 0, :], -1.0, ALU.mult, 1.0, ALU.add)
                v.wait_ge(S_("ckv_rstd"), 1)
                for t in range(NT):
                    stt(o_c[:, t, 0:P], o_c[:, t, 0:P], stat(290 + t, 1), kv_row, ALU.mult, ALU.mult,
                        "ckv_ready" if t else None)
                for t in range(NT):
                    after(v, "o_hf", t)
                    tt(h_f[:, t, :], h_f[:, t, :], lb_row[:, 1, :], ALU.mult)
                    tt(h_f[:, t, :], h_f[:, t, :], lb_row[:, 0, :], ALU.add)
                    ts(h_kn[:, t, :], h_f[:, t, :], -1.0, ALU.mult, 1.0, ALU.add, signal="forget_ready")
                bank = filled(v, "o_cT")
                step.free(v.tensor_copy(o_cT, bank[:, 0:S]), "o_cT")
                take_T("o_kT", h_kT, 4)
                for n, h in enumerate(LEVELS):
                    after(v, f"h_d{n}", 1)
                    tt(h_KE[n % 2], h_kT, h_E[n % 2], ALU.mult)
                    tt(h_QE[n % 2], h_qT, h_E[n % 2], ALU.mult, "level_ready")
                    for i in range(1 if h == P else NT):
                        bank = filled(v, f"h_s{n}", i).rearrange("p (h t) -> p h t", h=HH)
                        if h == P:
                            step.free(v.tensor_copy(h_x, bank), f"h_s{n}", i)
                        else:
                            m = h_mask[:, 2 * n + 1, :].unsqueeze(1).to_broadcast([P, HH, P])
                            if n == 1:
                                step.free(v.tensor_tensor(h_sc[:, i, :, :], bank, m, ALU.mult), f"h_s{n}", i)
                            else:
                                step.free(v.tensor_tensor(h_tmp, bank, m, ALU.mult), f"h_s{n}", i)
                                tt(h_sc[:, i, :, :], h_sc[:, i, :, :], h_tmp, ALU.add)
                for t in range(NT):
                    bank = filled(v, "h_diag", t).rearrange("p (h t) -> p h t", h=HH)
                    step.free(v.tensor_tensor(h_tmp, bank, ident.unsqueeze(1).to_broadcast([P, HH, P]), ALU.mult),
                              "h_diag", t)
                    tt(h_sc[:, t, :, :], h_sc[:, t, :, :], h_tmp, ALU.add, "hscores_ready")
                sq = stat(296, NT, 4)
                for t in range(NT):
                    bank = filled(v, "h_pv", t)
                    step.free(v.tensor_copy(h_o[:, t, :], bank), "h_pv", t)
                    head_norm(h_o[:, t, :], HH, sq, h_tmp.rearrange("p a b -> p (a b)"), t)
                step(v.tensor_copy(sq, sq), "yd_squares")
                v.wait_ge(S_("yd_rstd"), 1)
                v.wait_ge(S_("hg_ready"), NT)
                for t in range(NT):
                    x = h_o[:, t, :]
                    tt(x.rearrange("p (h d) -> p h d", h=HH), x.rearrange("p (h d) -> p h d", h=HH),
                       stat(304, NT, 4)[:, t, :].unsqueeze(2).to_broadcast([P, HH, P]), ALU.mult)
                    tt(x, x, h_row, ALU.mult)
                    tt(yd[:, t, :], x, h_g[:, t, :], ALU.mult, "hgrn_done" if t else None)
                for u in range(8):
                    t, p = u // 4, u % 4
                    after(v, "idx", u)
                    for h in range(2):
                        if h == 0 and p == 0:
                            ts(o_iw, o_c[:, t, P:P + 8], IH ** -0.5, ALU.mult)
                        hd = head_of(2 * p + h)
                        if hd == 0:
                            ts(o_score[:, t, :], o_rel[:, u % 2, 0:S], o_iw[:, 0:1], ALU.mult)
                        else:
                            stt(o_score[:, t, :], o_rel[:, u % 2, h * S:(h + 1) * S], o_iw[:, hd:hd + 1],
                                o_score[:, t, :], ALU.mult, ALU.add, "rel_used" if h else None)
                for t in range(NT):
                    tt(o_work[:, t, :], o_score[:, t, :], causal[:, t, :], ALU.add)
                    for r in range(TOPK // 8):
                        step(v.max(stat(616, 8), o_work[:, t, :]))
                        step(v.match_replace(o_work[:, t, :], stat(616, 8), o_work[:, t, :], REMOVED))
                    ts(o_work[:, t, :], o_work[:, t, :], REMOVED / 2, ALU.is_gt, NEG, ALU.mult)
                    tt(o_mask[:, t, :], o_work[:, t, :], causal[:, t, :], ALU.add)
                softmax_max("o", [(p, t) for t in range(NT) for p in range(4)], lambda t: o_mask[:, t, :], 1.0)
                for i in range(4):
                    t, g = i // 2, i % 2
                    take_weighted("o_pv", i, H[:, t, g * BLK:(g + 1) * BLK], sums[:, t, 4 * g:4 * g + 4], P)
                take_T("lat_T", HT)
                for t in range(NT):
                    bank = filled(v, "o_yc", t)
                    step.free(v.tensor_copy(H[:, t, 0:BLK], bank), "o_yc", t)
                take_T("o_yT", HT)
                add_to_x("o_out")

            o_iw = stat(312, 8)

            def top16(src, work, values, index):
                step(v.max(values[:, 0:8], src))
                step(v.max_index(index[:, 0:8], values[:, 0:8], src))
                step(v.match_replace(work, values[:, 0:8], src, REMOVED))
                step(v.max(values[:, 8:16], work))
                step(v.max_index(index[:, 8:16], values[:, 8:16], work))

            def top_lists(scores, lists):
                for b in lists:
                    top16(scores[:, b, :], p_work[:, b * NK:(b + 1) * NK], p_v16[:, b, :], p_idx[:, b, :])

            def candidates():
                step(v.tensor_copy(p_i16, p_idx[:]))
                v16 = p_v16.rearrange("p (h a) k -> p h a k", a=2)
                cand = p_cand.rearrange("p (h a b) -> p h a b", h=PH, a=PK)
                tt(cand, v16[:, :, 0, :].unsqueeze(3).to_broadcast([P, PH, PK, PK]),
                   v16[:, :, 1, :].unsqueeze(2).to_broadcast([P, PH, PK, PK]), ALU.add)

            def top_heads(heads):
                for h in heads:
                    c = slice(h * S, (h + 1) * S)
                    top16(p_cand[:, c], p_work[:, c], p_top[:, h, :], p_pos[:, h, :])

            def split_places():
                pos = p_pos[:].rearrange("p h k -> p (h k)")
                step(v.tensor_scalar(p_bits[:, 0, :], pos, 4, None, ALU.logical_shift_right))
                step(v.tensor_scalar(p_bits[:, 1, :], pos, 15, None, ALU.bitwise_and))
                step(v.tensor_copy(p_ab, p_bits[:]))

            def keys_of(a):
                i16 = p_i16.rearrange("p (h a) k -> p h a k", a=2)
                eq = p_eq.rearrange("p (n m) -> p n m", m=PK)
                tt(eq, p_ab[:, a, :].unsqueeze(2).to_broadcast([P, SEL, PK]),
                   iota.unsqueeze(1).to_broadcast([P, SEL, PK]), ALU.is_equal)
                eq4 = p_eq.rearrange("p (h k m) -> p h k m", h=PH, k=PK)
                tt(eq4, eq4, i16[:, :, a, :].unsqueeze(2).to_broadcast([P, PH, PK, PK]), ALU.mult)
                step(v.tensor_reduce(p_i12[:, a, :], eq, AXX, ALU.add))

            def experts(t):
                stt(p_eid[:, t, :], p_i12[:, 0, :], float(NK), p_i12[:, 1, :], ALU.mult, ALU.add, "eid_ready")
                g = p_g[:, t, :].rearrange("p (h k) -> p h k", h=PH)
                tt(g, p_top, p_top[:, :, 0:1].to_broadcast([P, PH, PK]), ALU.subtract, "top_ready")

            def row_softmax(l, t):
                g = p_g[:, t, :].rearrange("p (h k) -> p h k", h=PH)
                v.wait_ge(S_("top_exp"), NT * l + t + 1)
                step(v.tensor_reduce(stat(616, 8), g, AXX, ALU.add))
                step(v.reciprocal(stat(616, 8), stat(616, 8)))
                tt(g, g, stat(616, 8).unsqueeze(2).to_broadcast([P, PH, PK]), ALU.mult)

            def dots(l, t):
                phase = 2 * t
                n, before = (l * 2 * NT + phase) * STEPS, used_before(l, phase)[0]
                with v.Fori(0, STEPS) as i:
                    for r in range(RING):
                        v.wait_ge(row_landed[r], i * 16 + 16 * (n + 1))
                        v.scalar_tensor_tensor(out=rows_u[:, r, :], in0=rows_u[:, r, :], scalar=1.0, in1=H[:, t, :],
                                               op0=ALU.mult, op1=ALU.mult,
                                               accum_out=p_act[:, t, bass.ds(i * RING + r, 1)])\
                            .then_inc(rows_used["vector"], 1)
                v.wait_ge(rows_used["vector"], before + SEL)
                step(v.tensor_copy(p_act[:, t, 0:1], p_act[:, t, 0:1]), "dots_ready")
                v.wait_ge(S_("gelu_ready"), NT * l + t + 1)
                tt(p_w[:, t, :], p_act[:, t, :], p_g[:, t, :], ALU.mult, "row_weights_ready")

            def add_rows(l, t, i):
                phase = 2 * t + 1
                n, before = (l * 2 * NT + phase) * STEPS, used_before(l, phase)[0]
                for j, r in enumerate(VE_SLOTS):
                    v.wait_ge(row_landed[r], i * 16 + 16 * (n + 1))
                    v.wait_ge(rows_used["vector"], i * len(VE_SLOTS) + (before + j))
                    v.scalar_tensor_tensor(out=X[:, t, :], in0=rows_u[:, r, :],
                                           scalar=p_w[:, t, bass.ds(i * RING + r, 1)], in1=X[:, t, :],
                                           op0=ALU.mult, op1=ALU.add).then_inc(rows_used["vector"], 1)

            def add_sums(l, t):
                by_v, by_pe = used_before(l, 2 * t + 2)
                v.wait_ge(rows_used["vector"], by_v)
                v.wait_ge(rows_used["tensor"], by_pe)
                for c in range(2):
                    xs = X[:, t, c * BLK:(c + 1) * BLK]
                    step.free(v.tensor_tensor(xs, banks[:, plan.bank(f"p_v{l}{t}", c), :], xs, ALU.add), f"p_v{l}{t}", c)
                step(v.tensor_copy(X[:, t, 0:1], X[:, t, 0:1]), "x_ready")

            def peer(l):
                norm(6 + 3 * l, X, gain_of(6 + 3 * l))
                take_T(f"T{6 + 3 * l}", HT)
                take_blocks(f"p_q{l}", 8, p_qT)
                for t, scores in enumerate((p_s, p_s1)):
                    if t:
                        v.wait_ge(pe_filled, plan.mark(f"p_s{l}", 7))
                    for i in range(4):
                        bank = filled(v, f"p_s{l}", 4 * t + i)
                        step.free(v.tensor_copy(scores[:, 4 * i:4 * i + 4, :], bank.rearrange("p (b n) -> p b n", b=4)),
                                  f"p_s{l}", 4 * t + i)
                top_lists(p_s, range(16))
                candidates()
                top_heads(range(PH))
                split_places()
                keys_of(0)
                keys_of(1)
                experts(0)
                if l == 0:
                    take_mem(1)
                row_softmax(l, 0)
                dots(l, 0)
                for i in range(STEPS):
                    add_rows(l, 0, i)
                    if i < 6:
                        top_lists(p_s1, range(3 * i, min(3 * i + 3, 16)))
                    elif i == 6:
                        candidates()
                    elif i < 11:
                        top_heads(range(2 * (i - 7), 2 * (i - 7) + 2))
                    elif i == 11:
                        split_places()
                        keys_of(0)
                    elif i == 12:
                        keys_of(1)
                        experts(1)
                add_sums(l, 0)
                row_softmax(l, 1)
                dots(l, 1)
                with v.Fori(0, STEPS) as i:
                    add_rows(l, 1, i)
                add_sums(l, 1)

            for l in range(2):
                if l:
                    odd()
                norm(5 + 3 * l, X, gain_of(5 + 3 * l))
                take_T(f"T{5 + 3 * l}", HT)
                take_blocks(f"x_q{l}", 4, x_qT)
                softmax_max(f"x{l}", [(p, t) for p in range(2) for t in range(NT)], None, XDH ** -0.5)
                for i in range(4):
                    t, g = i // 2, i % 2
                    take_weighted(f"x_pv{l}", i, H[:, t, g * BLK:(g + 1) * BLK], sums[:, t, 2 * g:2 * g + 2], XDH)
                take_T(f"x_oT{l}", HT)
                add_to_x(f"x_o{l}")
                peer(l)
            norm(10, X, gain_of(10), signal="final_ready")


def constants():
    f = np.float32
    const = np.zeros((P, NCONST), f)

    def put(name, a):
        at, n = CONST[name]
        const[:, at:at + n] = a

    r = np.arange(P)
    put("ident", np.eye(P))
    put("flip", np.eye(P)[::-1])
    put("ones", 1.0)
    q = np.arange(S).reshape(NT, P).T
    put("causal", np.where(np.arange(S)[None, None] <= q[:, :, None], 0.0, NEG).reshape(P, NT * S))
    put("tri", r[:, None] <= r[None])
    half = ADH // 2
    put("freq", (f(10000.0) ** (-np.arange(half, dtype=f) / f(half)))[None])
    put("iota", np.arange(16)[None])

    dist = np.maximum(S - 1 - np.arange(2 * S), 0)
    exact = BUCKETS // 2
    ratio = np.log(np.maximum(dist, 1).astype(f) / f(exact)) / f(np.log(MAXDIST / exact))
    large = np.minimum(exact + (ratio * (BUCKETS - exact)).astype(np.int32), BUCKETS - 1)
    bucket = np.where(dist < exact, dist, large)
    onehot = (bucket[None] == np.arange(BUCKETS)[:, None]).astype(f)

    inv = np.stack([1.0 / np.minimum(np.arange(S) + 1, w) for w in (2, 4, 8, 16)]).astype(f)
    pool_inv = np.broadcast_to(inv.reshape(1, -1), (P, 4 * S)).copy()

    masks = [r[:, None] > r[None], r[:, None] <= r[None]]
    for h in LEVELS[1:]:
        mid = r // (2 * h) * 2 * h + h
        second = r % (2 * h) >= h
        a, x, m = r[:, None], r[None], mid[None]
        masks.append(np.where(second[None], (a >= m) & (a <= x), (a > x) & (a < m)))
        masks.append((r[:, None] // (2 * h) == r[None] // (2 * h)) & ~second[:, None] & second[None])
    masks = np.concatenate([m.astype(f) for m in masks], 1)
    return {"const": const, "onehot": onehot, "pool_inv": pool_inv, "masks": masks}


def lay_out(a):
    def std(w):
        k = w.shape[0] // P
        return w.reshape(k, P, w.shape[1]).transpose(1, 0, 2).reshape(P, -1)

    def cut(w):
        return [std(w[:, c:c + BLK]) for c in range(0, w.shape[1], BLK)]

    w_in = a["w_in"][0]
    o = MW * 4 + 2 * MH
    ada = cut(a["ada_w"][0])
    kv = [cut(w) for w in a["xattn_wkv_2"]]
    t = ada[:4] + cut(w_in[:, 0:2 * MW]) + cut(w_in[:, 2 * MW:4 * MW]) + cut(w_in[:, o:o + 3 * AW]) + ada[4:]
    g = o + 3 * AW
    for c in range(2):
        t.append(std(w_in[:, g + c * BLK:g + (c + 1) * BLK]))
        t.append(std(w_in[:, g + D + c * BLK:g + D + (c + 1) * BLK]))
        t.append(np.concatenate([std(a["p_mlstm"][0][:, c * BLK:(c + 1) * BLK]),
                                 std(a["p_moba"][0][:, c * BLK:(c + 1) * BLK])], 1))
    t += cut(a["w_out"][0])
    for i in range(NF // 2):
        c = slice(2 * P * i, 2 * P * (i + 1))
        t.append(std(np.concatenate([a["w_gate"][0][:, c], a["w_up"][0][:, c]], 1)))
    down = np.concatenate([a["w_down"][0], np.zeros((2 * P, D), np.float32)], 0)
    t += [std(down[4 * P * i:4 * P * (i + 1)]) for i in range(6)]
    e = cut(a["even_w_in_2"][0])
    t += kv[0] + [e[3], e[0], e[1], e[2]] + cut(a["even_w_out_2"][0])
    wi = a["odd_w_in_2"][0]
    for l in range(2):
        if l:
            t += cut(wi[:, 0:1024])
            c0 = 1024
            iq0, ik0, iw0, h0 = c0 + CR, c0 + CR + 512, c0 + CR + 576, c0 + CR + 584
            ik = wi[:, ik0:ik0 + 64]
            t.append(std(np.concatenate([wi[:, c0:c0 + CR], ik, ik, wi[:, iw0:iw0 + 8],
                                         np.zeros((D, BLK - 264), np.float32)], 1)))
            t += cut(wi[:, iq0:iq0 + 512])
            t += cut(wi[:, h0:h0 + 2048])
            t += cut(a["odd_w_out_2"][0])
        t += cut(a["xattn_wq_2"][l]) + cut(a["xattn_wo_2"][l]) + cut(a["peer_wq_2"][l])
        keys = a["peer_keys_2"][l].transpose(3, 0, 1, 2).reshape(P, 16 * NK)
        t.append(np.concatenate([keys, np.zeros((P, 4096 - 16 * NK), np.float32)], 1))
        if l == 0:
            t += kv[1]
    weights = np.stack(t)

    col = lambda x: x.reshape(-1, P).T
    cols = np.concatenate([col(a["c"][0]), col(a["b_in"][0, 0:2 * MW]),
                           *[col(a["conv_w"][0, j]) for j in range(4)], col(a["conv_b"][0]),
                           *[col(a["even_conv_w_2"][0, j, 0]) for j in range(3)], col(a["even_pool_scale_2"][0])], 1)
    gates = std(w_in[:, 4 * MW:4 * MW + 8])
    small = np.concatenate([gates, a["even_pool_w_2"][0].transpose(1, 0, 2).reshape(P, -1),
                            a["odd_w_uv_2"][0].transpose(1, 0, 2).reshape(P, -1)], 1)
    b = a["b_in"][0]
    rows = np.concatenate([a["ada_b"][0], b[4 * MW:o], b[2 * MW:4 * MW], b[o:g], b[g:], a["m_norm_g"][0],
                           a["hgrn_gamma_2"].reshape(-1), a["odd_kv_norm_2"][0], a["odd_hg_norm_2"][0],
                           a["norm1_g"][0], a["norm2_g"][0], a["mem_norm_2"], a["normf_g"], a["mix_norm_2"][0], a["xattn_norm_2"][0],
                           a["peer_norm_2"][0], a["mix_norm_2"][1], a["xattn_norm_2"][1], a["peer_norm_2"][1],
                           a["final_norm_2"]])[None]
    pos = a["positions"].reshape(NT, P).T
    return {"weights": weights, "cols": cols, "small": small, "rows": rows, "pos": pos, "rel_bias": a["rel_bias_2"],
            "x": a["x"], "mem": a["mem_2"], "u0": a["peer_u_2"][0], "u1": a["peer_u_2"][1],
            "v0": a["peer_v_2"][0], "v1": a["peer_v_2"][1], **constants()}


def kernel(**inputs):
    import concourse.bacc as bacc
    from concourse.bass_utils import run_bass_kernel_spmd

    arrays = {"in_" + n: np.ascontiguousarray(x) for n, x in lay_out({k: np.asarray(x) for k, x in inputs.items()}).items()}
    nc = bacc.Bacc("TRN2", target_bir_lowering=False, num_devices=1)
    io = {n[3:]: nc.dram_tensor(n, x.shape, mybir.dt.from_np(x.dtype), kind="ExternalInput").ap() for n, x in arrays.items()}
    io["out"] = nc.dram_tensor("out_dram", (1, S, D), F32, kind="ExternalOutput").ap()
    build(nc, io)
    return run_bass_kernel_spmd(nc, [arrays], core_ids=[0]).results[0]["out_dram"]
```

```python
from contextlib import ExitStack

import numpy as np
import concourse.bass as bass
from concourse import mybir

ALU = mybir.AluOpType
ACT = mybir.ActivationFunctionType
AXX = mybir.AxisListType.X
F32 = mybir.dt.float32
U32 = mybir.dt.uint32
I32 = mybir.dt.int32
F32R = mybir.dt.float32r

P = 128
S = 256
NT = S // P
D = 1024
KD = D // P
BLK = 512
EPS = 1e-6
NEG = -1e30
REMOVED = -3e38
MH, MDH, MW = 4, 128, 512
AH, ADH, AW = 8, 64, 512
DFF = 2816
NF = DFF // P
CH, CR, CDH = 8, 128, 64
IH, IDH = 8, 64
TOPK = 64
BUCKETS, MAXDIST = 32, 128
HH, HK = 4, 128
XH, XDH = 4, 256
PH, NK, PK = 8, 128, 16
SEL = PH * PK
LEVELS = [128, 64, 32, 16, 8, 4, 2, 1]
PARTS = 4
PW = 4096 // PARTS
RAW_RING, SPLIT_RING = 6, 3
RING = 8
HALF = RING // 2
VE_SLOTS = [0, HALF]
PE_SLOTS = [r for r in range(RING) if r not in VE_SLOTS]
PE_ROWS = len(PE_SLOTS)
STEPS = SEL // RING

COLS = {}
for _n, _w in (("c", 8), ("mod1_b", 16), ("norm1", 8), ("b_qk", 8), ("conv_w", 32), ("conv_b", 8), ("even_conv", 12), ("pool_scale", 4)):
    COLS[_n] = (sum(w for _, w in COLS.values()), _w)
NCOL = sum(w for _, w in COLS.values())
CONST = {}
for _n, _w in (("ident", P), ("flip", P), ("ones", P), ("causal", 2 * S), ("tri", P), ("freq", 32), ("iota", 16)):
    CONST[_n] = (sum(w for _, w in CONST.values()), _w)
NCONST = sum(w for _, w in CONST.values())
SMALL = {}
for _n, _w in (("gates", KD * 8), ("pool_w", 4 * P), ("w_uv", CH * CDH)):
    SMALL[_n] = (sum(w for _, w in SMALL.values()), _w)
NSMALL = sum(w for _, w in SMALL.values())
ROWS = {}
for _n, _w in (("ada_b", 6 * D), ("gate_b", 8), ("b_n", 5 * BLK), ("b_g", 2 * D), ("m_norm", MW), ("gamma", 2 * 512),
               ("kv_norm", CR), ("hg_norm", 512), ("norm", 11 * D)):
    ROWS[_n] = (sum(w for _, w in ROWS.values()), _w)
NMASK = 2 + (len(LEVELS) - 1) * 2


class Plan:

    def __init__(self):
        self.first, self.fills = {}, []
        self.marks, self.taken = 0, {"vector": 0, "scalar": 0}

    def add(self, stage, n=1, taker="vector", marks=None):
        self.first[stage] = len(self.fills), self.marks
        for i in range(n):
            self.taken[taker] += 1
            self.fills.append((self.marks + (i + 1 if marks is None else marks), taker, self.taken[taker]))
        self.marks += n if marks is None else marks

    def mark(self, stage, i=0):
        return self.fills[self.first[stage][0] + i][0]

    def bank(self, stage, i=0):
        return (self.first[stage][0] + i) % 8

    def before(self, stage, i=0):
        n = self.first[stage][0] + i - 8
        return self.fills[n][1:] if n >= 0 else None

    def took(self, stage, i=0):
        return self.fills[self.first[stage][0] + i][1:]


def head_of(slot):
    return slot // 4 * 4 + slot % 2 * 2 + slot // 2 % 2


def place_of(slot, size):
    h = head_of(slot)
    return h // 2, slice(h % 2 * size, (h % 2 + 1) * size)


def units_of(plan, name, n, between={}):
    plan.add(f"{name}_s0")
    plan.add(f"{name}_s1")
    for u in range(n):
        if u + 2 < n:
            plan.add(f"{name}_s{u + 2}")
        for i in between.get(u, ()):
            plan.add(f"ada{i}")
        plan.add(f"{name}_t{u}", taker="scalar")


ADA_IN_M = {0: [4], 1: [5], 2: [6], 3: [7]}
ADA_IN_A = {0: [8], 2: [9], 4: [10], 6: [11]}


def make_plan():
    p = Plan()
    p.add("bias_rows")
    p.add("T0", 4)
    p.add("ada", taker="scalar")
    p.add("z_qk", 4)
    p.add("z_gate")
    p.add("z_n", 10)
    p.add("a_T", 4)
    p.add("m_cum")
    p.add("m_g0")
    p.add("m_g1")
    units_of(p, "m", 4, ADA_IN_M)
    p.add("m_pv", NT)
    units_of(p, "a", 8, ADA_IN_A)
    p.add("a_pv", NT)
    p.add("y_T", 4)
    p.add("merge", 16)
    p.add("mg_T", 4)
    p.add("w_out", 4)
    p.add("T1", 4)
    for i in range(NF // 2):
        p.add(f"ff_g{i}", taker="scalar")
        p.add(f"ff_u{i}")
        if i == 4:
            p.add("T2", 4)
    p.add("down", 4, marks=6)
    p.add("x_k0", 4)
    p.add("x_v0", 4)
    p.add("T4", 4)
    p.add("e_z", 8)
    p.add("e_pool", 2)
    p.add("e_out", 4)
    for l in range(2):
        if l:
            p.add("T7", 4)
            p.add("o_ckv")
            p.add("o_ik")
            p.add("o_hf", 2, "scalar")
            p.add("o_hi", 2)
            p.add("o_hg", 2)
            p.add("o_hq", 2)
            p.add("o_iq", 2)
            p.add("o_ql", 4)
            p.add("o_cT")
            p.add("o_kT", 2)
            p.add("h_d0", 2, "scalar")
            for n, h in enumerate(LEVELS):
                if n + 1 < len(LEVELS):
                    p.add(f"h_d{n + 1}", 2, "scalar")
                p.add(f"h_s{n}", 1 if h == P else NT)
            p.add("h_diag", NT)
            p.add("h_pv", NT)
            p.add("idx", 8, "scalar")
            units_of(p, "o", 8)
            p.add("o_pv", 4)
            p.add("lat_T", 4)
            p.add("o_yc", NT)
            p.add("o_yT", 4)
            p.add("o_out", 4)
        p.add(f"T{5 + 3 * l}", 4)
        p.add(f"x_q{l}", 4)
        units_of(p, f"x{l}", 4)
        p.add(f"x_pv{l}", 4)
        p.add(f"x_oT{l}", 4)
        p.add(f"x_o{l}", 4)
        p.add(f"T{6 + 3 * l}", 4)
        for n in range(PH // 2):
            p.add(f"p_q{l}{n}", 2, taker="scalar")
            p.add(f"p_s{l}{n}")
            p.add(f"p_r{l}{n}", taker="scalar")
        if l == 0:
            p.add("x_k1", 4)
            p.add("x_v1", 4)
        for t in range(NT):
            p.add(f"p_v{l}{t}", 2, marks=0)
    return p


def tiles_in_order():
    t = [("ada", i) for i in range(4)]
    t += [("z_qk", 1), ("z_qk", 3)] + [("z_n", 2 * i + 1) for i in range(5)]
    t += [(f"ada{i}", 0) for i in range(4, 12)]
    for c in range(2):
        t += [("merge", 8 * c + 1), ("merge", 8 * c + 3), ("merge", 8 * c + 7)]
    t += [("w_out", 1), ("w_out", 3)] + [(f"ff_u{i}", 0) for i in range(NF // 2)]
    t += [("down", i) for i in range(6)] + [("x_k0", 1), ("x_k0", 3), ("x_v0", 1), ("x_v0", 3)]
    t += [("e_z", 2 * i + 1) for i in range(4)] + [("e_out", 1), ("e_out", 3)]
    for l in range(2):
        if l:
            t += [("o_ik", 0), ("o_hf", 1), ("o_hi", 1), ("o_hg", 1), ("o_hq", 1), ("o_iq", 1), ("o_ql", 1), ("o_ql", 3)]
            t += [("o_out", 1), ("o_out", 3)]
        t += [(f"x_q{l}", 1), (f"x_q{l}", 3)]
        t += [(f"x_o{l}", 1), (f"x_o{l}", 3)]
        t += [(f"p_q{l}{n}", 1) for n in range(PH // 2)]
        if l == 0:
            t += [("x_k1", 1), ("x_k1", 3), ("x_v1", 1), ("x_v1", 3)]
    return t


def is_split(stage, i):
    return not (stage.startswith("ada") or stage in ("x_k1", "x_v1") or stage == "merge" and i % 8 == 7)


def build(nc, io):
    plan = make_plan()
    tiles = tiles_in_order()
    tile_no = {}
    for n, (stage, _) in enumerate(tiles):
        tile_no.setdefault(stage, n)

    with ExitStack() as ctx:
        def sb(name, shape, dt=F32):
            return ctx.enter_context(nc.sbuf_tensor(name, shape, dt))

        def sem(name):
            return ctx.enter_context(nc.semaphore(name))

        X = sb("X", [P, NT, D])
        H = sb("H", [P, NT, D])
        HT_hi = sb("HT_hi", [P, KD, S], F32R)
        HT_lo = sb("HT_lo", [P, KD, S], F32R)
        W = sb("W", [P, RAW_RING, PW])
        W_hi = sb("W_hi", [P, SPLIT_RING, PW], F32R)
        W_lo = sb("W_lo", [P, SPLIT_RING, PW], F32R)
        gain = sb("gain", [P, 2, D])
        cols = sb("cols", [P, NCOL])
        const = sb("const", [P, NCONST])
        small = sb("small", [P, NSMALL])
        pos_i = sb("pos_i", [P, NT], I32)
        rel_sb = sb("rel_sb", [BUCKETS, 8])
        st = sb("st", [P, 640])
        arena = sb("arena", [P, 24576])
        banks = ctx.enter_context(nc.psum_tensor("banks", [P, 8, 512], F32))
        bias_scratch = nc.dram_tensor("bias_scratch", [8, 2 * S], F32).ap()

        def area(at, *shape):
            n = int(np.prod(shape))
            v = arena[:, at:at + n]
            if len(shape) == 1:
                return v
            names = "abc"[:len(shape)]
            return v.rearrange(f"p ({' '.join(names)}) -> p {' '.join(names)}", **dict(zip(names[1:], shape[1:])))

        def stat(at, *shape):
            n = int(np.prod(shape))
            v = st[:, at:at + n]
            if len(shape) == 1:
                return v
            names = "abc"[:len(shape)]
            return v.rearrange(f"p ({' '.join(names)}) -> p {' '.join(names)}", **dict(zip(names[1:], shape[1:])))

        def named_cols(t, table, name):
            a, n = table[name]
            return t[:, a:a + n]

        ident, flip, ones = (named_cols(const, CONST, n) for n in ("ident", "flip", "ones"))
        tri = named_cols(const, CONST, "tri")
        causal = named_cols(const, CONST, "causal").rearrange("p (t s) -> p t s", t=NT)
        freq, iota = named_cols(const, CONST, "freq"), named_cols(const, CONST, "iota")
        mod = area(0, 6, D)
        b_rows = area(6144, 8 + 5 * BLK)
        Z = area(8712, NT, 5 * BLK)
        ada_sum = area(8712, 4, 512)
        MV, MO, AQ, AV = 0, 512, 1024, 2048
        qk_raw = area(13832, 8, S + 3)
        aT = area(13832, 8, S)
        qkT = area(15904, 8, S)
        yT = area(15904, 8, S)
        h0T = area(17952, KD, S)
        PT1 = area(17952, 8, NT, S)
        scrA = area(22048, 2, 512)
        probs = area(23072, 2, 512)
        rope_t = area(17952, 4, 512)
        m_row = area(22048, MW)
        sg = area(17952, 4, 512)
        fT = area(8712, NF, S)
        silu_g = area(14344, 2, 512)
        memT = area(0, KD, S)
        e_z = area(2048, 16, S)
        e_cu = area(6144, 4, S + 2)
        e_pv = area(7176, 4, S + 16)
        e_t = area(8264, 2, S + 16)
        e_pool = area(8808, 4, S)
        e_inv = area(9832, 4, S)
        e_yT = area(10856, 8, S)
        x_qT = area(2048, 8, S)
        x_PT = area(8192, 4, NT, S)
        p_qT = area(2048, 2, 4, S)
        p_s1 = area(4096, 16, NK)
        p_s = area(6144, 16, NK)
        p_work = area(8192, 512)
        p_eq = area(9216, 2, 512)
        p_cand = area(10240, 512)
        p_keys = area(12288, 16, NK)
        rows_u = area(14336, RING, D)
        p_v16 = area(22528, 16, PK)
        p_top = area(22784, PH, PK)
        p_eid = sb("p_eid", [P, NT, SEL], U32)
        p_idx = sb("p_idx", [P, 16, PK], U32)
        p_pos = sb("p_pos", [P, PH, PK], U32)
        p_bits = sb("p_bits", [P, 2, SEL], U32)
        p_ab = area(22912, 2, SEL)
        p_i16 = area(23168, 16, PK)
        p_g = area(23424, NT, SEL)
        p_act = area(23680, NT, SEL)
        p_w = area(23936, NT, SEL)
        p_i12 = area(24192, 2, SEL)
        stage_idx = sb("stage_idx", [P, 2, HALF], U32)
        o_qT = area(2048, 8, S)
        o_c = area(4096, NT, P + 8)
        o_cT = area(4368, S)
        o_iqT = area(4624, 4, S)
        o_ikT = area(5648, S)
        h_qT = area(5904, HH, S)
        h_f = area(6928, NT, 512)
        h_kn = area(7952, NT, 512)
        h_kT = area(8976, HH, S)
        h_i = area(10000, NT, 512)
        h_g = area(11024, NT, 512)
        lb_row = area(12048, 2, 512)
        h_row = area(13072, 512)
        kv_row = area(13584, P)
        h_mask = area(13712, NMASK, P)
        h_E = [area(15760 + 1024 * i, HH, S) for i in range(2)]
        h_KE = [area(17808 + 1024 * i, HH, S) for i in range(2)]
        h_QE = [area(19856 + 1024 * i, HH, S) for i in range(2)]
        h_x = area(21904, HH, P)
        h_sc = area(22416, NT, HH, P)
        h_tmp = area(23440, NT, HH, P)
        h_o = area(15760, NT, 512)
        yd = area(10000, NT, 512)
        o_PT = area(11024, 8, NT, S)
        hankel = area(15120, NT, 8 * S)
        latT = area(15120, KD, S)
        o_mask = area(19216, NT, S)
        o_score = area(19728, NT, S)
        o_work = area(20240, NT, S)
        o_rel = area(20752, 2, 512)
        onehot = arena[0:BUCKETS, 22048:22560]
        rb_sb = arena[0:8, 22560:23072]
        c_rep = gain[:, 0, :].rearrange("p (k n) -> p k n", k=KD)
        x_kT1 = sb("x_kT1", [P, 8, S])
        x_kTs, x_vs = [area(12928, 8, S), x_kT1], [area(14976, NT, D), area(0, NT, D)]
        mem_in = area(15368, NT, D)
        diag = area(2048, PE_ROWS, P)

        pe_filled = sem("pe_filled")
        took = {"vector": sem("vector_took"), "scalar": sem("scalar_took")}
        part_landed = [sem(f"part_landed{i}") for i in range(RAW_RING)]
        row_landed = [sem(f"row_landed{i}") for i in range(RING)]
        rows_used = {"vector": sem("rows_used_vector"), "tensor": sem("rows_used_tensor")}
        idx_staged = sem("idx_staged")
        named = {}

        def S_(name):
            if name not in named:
                named[name] = sem(name)
            return named[name]

        class Steps:

            def __init__(self, eng, own, name):
                self.eng, self.own, self.name, self.count = eng, S_(own), name, {}

            def __call__(self, ins, signal=None):
                s = self.own if signal is None else S_(signal)
                self.count[id(s)] = self.count.get(id(s), 0) + 1
                ins.then_inc(s, 1)
                self.eng.wait_ge(s, self.count[id(s)])

            def overlap(self, ins):
                n = self.count[id(self.own)] = self.count.get(id(self.own), 0) + 1
                ins.then_inc(self.own, 1)
                if n > 1:
                    self.eng.wait_ge(self.own, n - 1)

            def all(self):
                self.eng.wait_ge(self.own, self.count[id(self.own)])

            def free(self, ins, stage, i=0, wait=True):
                who, n = plan.took(stage, i)
                assert who == self.name
                ins.then_inc(took[who], 1)
                if wait:
                    self.eng.wait_ge(took[who], n)

        def filled(eng, stage, i=0):
            eng.wait_ge(pe_filled, plan.mark(stage, i))
            return banks[:, plan.bank(stage, i), :]

        def after(eng, stage, i=0):
            who, n = plan.took(stage, i)
            eng.wait_ge(took[who], n)

        used, n_signals = [], 0
        for n, (stage, i) in enumerate(tiles):
            if stage == "ada":
                used.append([("ada_summed", PARTS * n + part + 1) for part in range(PARTS)])
                continue
            last = plan.first["down"][1] + i + 1 if stage == "down" else plan.mark(stage, i)
            if stage == "merge" and i % 8 == 7:
                used.append([(None, last - 1)] * 2 + [(None, last)] * 2)
                continue
            with_signal = 1 if (stage, i) == ("down", 5) else PARTS - 1
            used.append([("part_used", n_signals + part + 1) if part < with_signal else (None, last) for part in range(PARTS)])
            n_signals += with_signal
        split = [n for n, (stage, i) in enumerate(tiles) if is_split(stage, i)]

        def wait_used(eng, n, part):
            name, count = used[n][part]
            eng.wait_ge(S_(name) if name else pe_filled, count)

        def wait_landed(eng, n, part):
            slot, turn = (PARTS * n + part) % RAW_RING, (PARTS * n + part) // RAW_RING
            eng.wait_ge(part_landed[slot], 16 * (turn + 1))
            return W[:, slot, :]

        def parts_before(n):
            return PARTS * split.index(n)

        def used_before(layer, phase):
            v_phases, u_phases = 2 * layer + phase // 2, 2 * layer + (phase + 1) // 2
            return (u_phases * SEL + v_phases * STEPS * len(VE_SLOTS), v_phases * STEPS * PE_ROWS)

        block = ctx.enter_context(nc.Block())

        @block.sync
        def _(sp):
            sp.dma_start(X[:], io["x"].rearrange("b (t p) d -> p (b t) d", p=P)).then_inc(S_("x_in"), 16)
            sp.dma_start(const[:], io["const"]).then_inc(S_("const_in"), 16)
            for m in range(PARTS * len(tiles)):
                if m >= RAW_RING:
                    n, part = divmod(m - RAW_RING, PARTS)
                    if n in split:
                        sp.wait_ge(S_("lo_made"), parts_before(n) + part + 1)
                    else:
                        wait_used(sp, n, part)
                n, part = divmod(m, PARTS)
                sp.dma_start(W[:, m % RAW_RING, :], io["weights"][n][:, part * PW:(part + 1) * PW])\
                    .then_inc(part_landed[m % RAW_RING], 16)
            sp.wait_ge(S_("final_ready"), NT)
            sp.dma_start(io["out"].rearrange("b (t p) d -> p (b t) d", p=P), H[:]).then_inc(S_("out_written"), 16)
            sp.wait_ge(S_("out_written"), 16)

        @block.gpsimd
        def _(po):
            def row(dst, name, at=0, n=None):
                a, w = ROWS[name]
                n = n or w
                return po.dma_start(dst, io["rows"][0:1, a + at:a + at + n].to_broadcast([P, n]))

            po.dma_start(rel_sb[:], io["rel_bias"]).then_inc(S_("rel_in"), 16)
            po.dma_start(onehot, io["onehot"]).then_inc(S_("onehot_in"), 16)
            po.dma_start(pos_i[:], io["pos"]).then_inc(S_("pos_in"), 16)
            po.wait_ge(S_("ada_summed"), 3 * PARTS)
            po.dma_start(small[:], io["small"]).then_inc(S_("small_in"), 16)
            row(b_rows, "gate_b", 0, 8 + 5 * BLK).then_inc(S_("b_rows_in"), 16)
            after(po, "bias_rows")
            po.dma_start(bias_scratch, rb_sb).then_inc(S_("scratch_written"), 16)
            row(mod[:, 2:, :].rearrange("p a b -> p (a b)"), "ada_b", 2 * D, 4 * D).then_inc(S_("ada_b_rest_in"), 16)
            row(gain[:, 1, :], "norm", D, D).then_inc(S_("gain_in1"), 16)
            row(area(0, 2 * D), "b_g").then_inc(S_("b_g_in"), 16)

            lows = [0]

            def low(stage, i=None):
                first = tile_no[stage]
                count = sum(st == stage for st, _ in tiles) if i is None else 1
                for n in range(first + (i or 0), first + (i or 0) + count):
                    assert parts_before(n) == lows[0]
                    for part in range(PARTS):
                        slot = lows[0] % SPLIT_RING
                        lows[0] += 1
                        po.wait_ge(S_("hi_made"), lows[0])
                        po.tensor_tensor(W_lo[:, slot, :], W[:, (PARTS * n + part) % RAW_RING, :],
                                         W_hi[:, slot, :].bitcast(F32), ALU.subtract).then_inc(S_("lo_made"), 1)

            low("z_qk")
            low("z_n")
            po.wait_ge(S_("m_row_free"), 1)
            row(m_row, "m_norm").then_inc(S_("m_row_in"), 16)

            def load_gain(n):
                po.wait_ge(S_("h_ready"), NT * (n - 1))
                row(gain[:, n % 2, :], "norm", n * D, D).then_inc(S_(f"gain_in{n % 2}"), 16)

            po.wait_ge(pe_filled, plan.mark("ada11"))
            load_gain(2)
            for i in (0, 1, 3, 4):
                low("merge", i)
            low("w_out", 0)
            po.wait_ge(pe_filled, plan.mark("merge", 15))
            po.dma_start(mem_in, io["mem"].rearrange("b (t p) d -> p (b t) d", p=P)).then_inc(S_("mem_in"), 16)
            low("w_out", 1)
            low("ff_u0")
            load_gain(3)
            for i in range(1, NF // 2):
                low(f"ff_u{i}")
                if i == 5:
                    load_gain(4)
            low("down")
            po.wait_ge(pe_filled, plan.mark("down", 3))
            po.dma_start(e_inv.rearrange("p a b -> p (a b)"), io["pool_inv"]).then_inc(S_("inv_in"), 16)
            low("x_k0")
            load_gain(5)
            low("x_v0")
            load_gain(6)
            low("e_z")
            low("e_out")

            def load_keys(layer):
                po.wait_ge(pe_filled, plan.mark(f"x{layer}_s3"))
                po.dma_start(p_keys.rearrange("p a b -> p (a b)"), io["keys"][layer]).then_inc(S_("keys_in"), 16)

            def gathers(layer):
                for phase in range(2 * NT):
                    table = io[("u", "v")[phase % 2] + str(layer)]
                    t = phase // 2
                    by_v, by_pe = used_before(layer, phase)
                    n = (layer * 2 * NT + phase) * STEPS
                    pairs = (NT * layer + t) * (PH // 2)
                    if phase % 2 == 0:
                        po.wait_ge(S_("eid_ready"), pairs + 1)

                    def half_step(i, half, first):
                        po.tensor_copy(stage_idx[:, half, :], p_eid[:, t, bass.ds(i * RING + HALF * half, HALF)])\
                            .then_inc(idx_staged, 1)
                        po.wait_ge(idx_staged, i * 2 + (2 * n + half + 1))
                        if not first:
                            po.sem_inc(S_("gather_turns"), 1)
                        for r in range(HALF):
                            po.indirect_dma_start(rows_u[:, half * HALF + r, :], None, table,
                                                  bass.IndirectOffsetOnAxis(ap=stage_idx[:, half, r:r + 1], axis=0))\
                                .then_inc(row_landed[half * HALF + r], 16)

                    for half in range(2):
                        if phase % 2:
                            po.wait_ge(rows_used["vector"], by_v - RING + HALF * (half + 1))
                        elif n:
                            po.wait_ge(rows_used["vector"], by_v - 2 + half + 1)
                            po.wait_ge(rows_used["tensor"], by_pe - PE_ROWS + PE_ROWS // 2 * (half + 1))
                        half_step(0, half, True)
                    if phase % 2 == 0:
                        po.wait_ge(S_("eid_ready"), pairs + PH // 2)
                    with po.Fori(1, STEPS) as i:
                        for half in range(2):
                            if phase % 2:
                                po.wait_ge(rows_used["tensor"], i * PE_ROWS + (by_pe - PE_ROWS + PE_ROWS // 2 * (half + 1)))
                                po.wait_ge(rows_used["vector"], i * 2 + (by_v - 2 + half + 1))
                            else:
                                po.wait_ge(rows_used["vector"], i * RING + (by_v - RING + HALF * (half + 1)))
                            half_step(i, half, False)

            def low_cross(layer):
                low(f"x_q{layer}")
                load_keys(layer)
                low(f"x_o{layer}")
                low(f"p_q{layer}0")
                if layer == 0:
                    load_gain(7)
                load_gain(8 + 2 * layer)
                for n in range(1, PH // 2):
                    low(f"p_q{layer}{n}")

            low_cross(0)
            gathers(0)
            low("o_ik")
            after(po, "p_v01", 1)
            row(lb_row.rearrange("p a b -> p (a b)"), "gamma").then_inc(S_("odd_in"), 16)
            row(h_row, "hg_norm").then_inc(S_("odd_in"), 16)
            row(kv_row, "kv_norm").then_inc(S_("odd_in"), 16)
            po.dma_start(h_mask.rearrange("p a b -> p (a b)"), io["masks"]).then_inc(S_("odd_in"), 16)
            for name in ("hf", "hi", "hg", "hq", "iq", "ql"):
                low(f"o_{name}")
            po.wait_ge(S_("hgrn_done"), 1)
            po.wait_ge(S_("scratch_written"), 16)
            for t in range(NT):
                src = bass.AP(tensor=bias_scratch.tensor, offset=P * (1 - t), ap=[[1, P], [2 * S, 8], [1, S]])
                po.dma_start(hankel[:, t, :].rearrange("p (h s) -> p h s", h=8), src).then_inc(S_("hankel_in"), 16)
            load_gain(9)
            low("o_out")
            low_cross(1)
            gathers(1)

        @block.tensor
        def _(pe):
            def claim(stage, i=0):
                b = plan.before(stage, i)
                if b:
                    pe.wait_ge(took[b[0]], b[1])
                return banks[:, plan.bank(stage, i), :]

            def raw(n, part):
                return wait_landed(pe, n, part).rearrange("p (k n) -> p k n", k=2)

            def product(n, fills, act):
                banks_ = [claim(stage, i) for stage, i, _ in fills]
                for part in range(PARTS):
                    if act is None:
                        q = parts_before(n) + part
                        pe.wait_ge(S_("lo_made"), q + 1)
                        hi, lo = (w[:, q % SPLIT_RING, :].rearrange("p (k n) -> p k n", k=2) for w in (W_hi, W_lo))
                        pairs = [(hi, HT_hi), (lo, HT_hi), (hi, HT_lo)]
                    else:
                        pairs = [(raw(n, part), act)]
                    for (stage, i, blocks), bank in zip(fills, banks_):
                        start = part == 0
                        for out, columns, tokens, stationary in blocks:
                            for j in range(2):
                                for m, (w, a) in enumerate(pairs):
                                    x, y = w[:, j, columns], a[:, 2 * part + j, tokens]
                                    last = part == PARTS - 1 and (out, j, m) == (blocks[-1][0], 1, len(pairs) - 1)
                                    mm = pe.matmul(bank[:, out], x if stationary else y, y if stationary else x, start=start,
                                                   stop=last)
                                    start = False
                        if part == PARTS - 1:
                            mm.then_inc(pe_filled, 1)
                    if part < PARTS - 1:
                        mm.then_inc(S_("part_used"), 1)

            def cols_at(c, n):
                return slice(c, c + n)

            def transposes(stage, blocks, wait):
                i = 0
                for t in range(NT):
                    for g in range(len(blocks) // 4):
                        wait(t)
                        bank = claim(stage, i)
                        for j in range(4):
                            mm = pe.transpose(bank[:, j * P:(j + 1) * P], blocks[4 * g + j](t), ident)
                        mm.then_inc(pe_filled, 1)
                        i += 1

            def norm_T(n):
                transposes(f"T{n}", [lambda t, b=b: H[:, t, b * P:(b + 1) * P] for b in range(KD)],
                           lambda t: pe.wait_ge(S_("h_ready"), NT * n + t + 1))

            def two_blocks(stage, i, c):
                return (stage, i, [(cols_at(b * S, S), cols_at(c + b * P, P), slice(0, S), True) for b in range(2)])

            def transposed(stage, n_tiles, act=None):
                for n in range(n_tiles):
                    product(tile_no[stage] + n, [two_blocks(stage, 2 * n + j, 2 * P * j) for j in range(2)], act)

            def natural(stage, n_tiles, act=None, first=None, at=0):
                first = tile_no[stage] if first is None else first
                for n in range(n_tiles):
                    product(first + n, [(stage, at + 2 * n + t, [(slice(0, BLK), slice(0, BLK), cols_at(t * P, P), False)])
                                        for t in range(NT)], act)

            def attend(name, units, scores, n_keys, base, between={}):
                def score(u):
                    mm = scores(u, claim(f"{name}_s{u}"))
                    mm.then_inc(pe_filled, 1)
                score(0)
                score(1)
                for u, (p, t) in enumerate(units):
                    if u + 2 < len(units):
                        score(u + 2)
                    for i in between.get(u, ()):
                        pe.wait_ge(S_("c_ready"), 1)
                        ada(i)
                    if base is None:
                        after(pe, f"{name}_s{u}")
                    else:
                        pe.wait_ge(S_("probs_ready"), base + u + 1)
                    bank = claim(f"{name}_t{u}")
                    kt = n_keys(t)
                    for h in range(2):
                        for s in range(kt):
                            mm = pe.transpose(bank[:, (h * NT + s) * P:(h * NT + s + 1) * P],
                                              probs[:, u % 2, h * S + s * P:h * S + (s + 1) * P], ident)
                    mm.then_inc(pe_filled, 1)

            def weighted(stage, i, t, heads, PT, values, width, n_keys, last, slot=lambda h: h):
                after(pe, last)
                bank = claim(stage, i)
                for j, h in enumerate(heads):
                    for s in range(n_keys(t)):
                        mm = pe.matmul(bank[:, j * width:(j + 1) * width], PT[:, slot(h), s, t * P:(t + 1) * P],
                                       values(h, s),
                                       start=(s == 0), stop=(s == n_keys(t) - 1))
                mm.then_inc(pe_filled, 1)

            def weighted_rows(l, t):
                sums = [claim(f"p_v{l}{t}", c) for c in range(2)]
                phase = 2 * t + 1
                n = (l * 2 * NT + phase) * STEPS
                before = used_before(l, phase)[1]

                def step(i, start=False, stop=False):
                    for j, r in enumerate(PE_SLOTS):
                        pe.wait_ge(S_("diag_ready"), i * PE_ROWS + (before + j + 1))
                        pe.wait_ge(row_landed[r], i * 16 + 16 * (n + 1))
                        for c in range(2):
                            mm = pe.matmul(sums[c], diag[:, j, :], rows_u[:, r, c * BLK:(c + 1) * BLK],
                                           start=start and j == 0, stop=stop and j == PE_ROWS - 1)
                        mm.then_inc(rows_used["tensor"], 1)

                step(0, start=True)
                with pe.Fori(1, STEPS - 1) as i:
                    step(i)
                step(STEPS - 1, stop=True)

            causal_keys = lambda t: t + 1
            all_keys = lambda t: NT

            def ada(i):
                bank = claim(f"ada{i}")
                for part in range(PARTS):
                    w = raw(tile_no[f"ada{i}"], part)
                    for j in range(2):
                        k = 2 * part + j
                        mm = pe.matmul(bank, c_rep[:, k, :], w[:, j, :], start=(k == 0), stop=(k == KD - 1))
                    mm.then_inc(pe_filled if part == PARTS - 1 else S_("part_used"), 1)

            pe.wait_ge(S_("rel_in"), 16)
            pe.wait_ge(S_("onehot_in"), 16)
            pe.matmul(claim("bias_rows")[0:8, :], rel_sb[:], onehot, start=True, stop=True).then_inc(pe_filled, 1)
            pe.wait_ge(S_("const_in"), 16)
            norm_T(0)
            bank = claim("ada")
            for i in range(4):
                pe.wait_ge(S_("ada_summed"), PARTS * (i + 1))
                for b in range(4):
                    mm = pe.matmul(bank[:, 4 * i + b:4 * i + b + 1], ada_sum[:, i, b * P:(b + 1) * P], ones[:, 0:1],
                                   start=True, stop=True)
            mm.then_inc(pe_filled, 1)
            pe.wait_ge(S_("h0T_split"), 4)
            transposed("z_qk", 2)
            pe.wait_ge(S_("small_in"), 16)
            bank = claim("z_gate")
            wg = named_cols(small, SMALL, "gates").rearrange("p (k n) -> p k n", k=KD)
            for t in range(NT):
                for k in range(KD):
                    mm = pe.matmul(bank[:, t * 8:(t + 1) * 8], h0T[:, k, t * P:(t + 1) * P], wg[:, k, :],
                                   start=(k == 0), stop=(k == KD - 1))
            mm.then_inc(pe_filled, 1)
            natural("z_n", 5)
            transposes("a_T", [lambda t, b=b: Z[:, t, AQ + b * P:AQ + (b + 1) * P] for b in range(8)],
                       lambda t: pe.wait_ge(S_("rope_done"), 1))
            pe.wait_ge(S_("logf_ready"), 1)
            lf, gcol = stat(0, NT, 4), stat(16, NT, 4)
            bank = claim("m_cum")
            pe.matmul(bank[:, 0:4], tri, lf[:, 0, :], start=True, stop=True)
            pe.matmul(bank[:, 4:8], tri, lf[:, 1, :], start=True, stop=False)
            pe.matmul(bank[:, 4:8], ones, lf[:, 0, :], start=False, stop=True).then_inc(pe_filled, 1)
            pe.wait_ge(S_("g_ready"), 1)
            for p in range(2):
                bank = claim(f"m_g{p}")
                for h in range(2):
                    for t in range(NT):
                        g = gcol[:, t, 2 * p + h:2 * p + h + 1]
                        mm = pe.transpose(bank[:, h * S + t * P:h * S + (t + 1) * P], g.to_broadcast([P, P]), ident)
                mm.then_inc(pe_filled, 1)
            pe.wait_ge(S_("qk_ready"), 1)
            m_units = [(p, t) for p in range(2) for t in range(NT)]

            def m_scores(u, bank):
                p, t = m_units[u]
                for h in range(2):
                    mm = pe.matmul(bank[:, h * S:(h + 1) * S], qkT[:, 2 * p + h, t * P:(t + 1) * P],
                                   qkT[:, 4 + 2 * p + h, :], start=True, stop=True)
                return mm
            attend("m", m_units, m_scores, causal_keys, None, ADA_IN_M)
            for t in range(NT):
                weighted("m_pv", t, t, range(MH), PT1, lambda h, s: Z[:, s, MV + h * MDH:MV + (h + 1) * MDH], MDH,
                         causal_keys, "m_t3")
            after(pe, "a_T", 3)
            a_units = [(p, t) for p in range(4) for t in range(NT)]

            def a_scores(u, bank):
                p, t = a_units[u]
                for h in range(2):
                    b, q = place_of(2 * p + h, ADH)
                    mm = pe.matmul(bank[:, h * S:(h + 1) * S], aT[q, b, t * P:(t + 1) * P], aT[q, 4 + b, :],
                                   start=True, stop=True)
                return mm
            attend("a", a_units, a_scores, causal_keys, 0, ADA_IN_A)
            for t in range(NT):
                weighted("a_pv", t, t, range(AH), PT1, lambda h, s: Z[:, s, AV + h * ADH:AV + (h + 1) * ADH], ADH,
                         causal_keys, "a_t7", slot=head_of)
            transposes("y_T", [lambda t, b=b: Z[:, t, MO + b * P:MO + (b + 1) * P] for b in range(8)],
                       lambda t: after(pe, "a_pv", 1))
            after(pe, "y_T", 3)
            for c in range(2):
                n = tile_no["merge"] + 3 * c
                natural("merge", 2, first=n, at=8 * c)
                for j in range(4):
                    t, m = j // 2, j % 2
                    bank = claim("merge", 8 * c + 4 + j)
                    for k in range(4):
                        w = raw(n + 2, 2 * m + k // 2)[:, k % 2, :]
                        mm = pe.matmul(bank, yT[:, 4 * m + k, t * P:(t + 1) * P], w, start=(k == 0), stop=(k == 3))
                    mm.then_inc(pe_filled, 1)
            transposes("mg_T", [lambda t, b=b: H[:, t, b * P:(b + 1) * P] for b in range(KD)],
                       lambda t: pe.wait_ge(S_("merged_ready"), 4))
            after(pe, "mg_T", 3)
            natural("w_out", 2)
            norm_T(1)
            after(pe, "T1", 3)
            for i in range(NF // 2):
                product(tile_no[f"ff_u{i}"], [two_blocks(f"ff_g{i}", 0, 0), two_blocks(f"ff_u{i}", 0, 2 * P)], None)
                if i == 4:
                    norm_T(2)
            for i in range(4):
                claim("down", i)
            for i in range(6):
                pe.wait_ge(S_("f_split"), i + 1)
                n_parts = min(PARTS, NF - PARTS * i)
                for part in range(n_parts):
                    q = parts_before(tile_no["down"] + i) + part
                    pe.wait_ge(S_("lo_made"), q + 1)
                    hi, lo = W_hi[:, q % SPLIT_RING, :], W_lo[:, q % SPLIT_RING, :]
                    k = PARTS * (i % 2) + part
                    for t in range(NT):
                        for c in range(2):
                            for m, (x, w) in enumerate(((HT_hi, hi), (HT_lo, hi), (HT_hi, lo))):
                                mm = pe.matmul(banks[:, plan.bank("down", 2 * c + t), :], x[:, k, t * P:(t + 1) * P],
                                               w[:, c * BLK:(c + 1) * BLK], start=(i + part + m == 0),
                                               stop=(PARTS * i + part == NF - 1 and m == 2))
                    mm.then_inc(pe_filled if part == n_parts - 1 else S_("part_used"), 1)
            pe.wait_ge(S_("mem_split"), 2)
            transposed("x_k0", 2)
            natural("x_v0", 2)
            norm_T(4)
            after(pe, "T4", 3)
            transposed("e_z", 4)
            pe.wait_ge(S_("pooled_ready"), 1)
            pw = named_cols(small, SMALL, "pool_w").rearrange("p (g n) -> p g n", g=4)
            for i in range(2):
                bank = claim("e_pool", i)
                for b in range(2):
                    mm = pe.matmul(bank[:, b * S:(b + 1) * S], pw[:, 2 * i + b, :], e_pool[:, 2 * i + b, :],
                                   start=True, stop=True)
                mm.then_inc(pe_filled, 1)
            after(pe, "e_pool", 1)
            pe.wait_ge(S_("e_split"), 2)
            natural("e_out", 2)

            def odd():
                norm_T(7)
                after(pe, "T7", 3)
                product(tile_no["o_ik"], [
                    ("o_ckv", 0, [(cols_at(t * (P + 8), P + 8), slice(0, P + 8), cols_at(t * P, P), False) for t in range(NT)]),
                    ("o_ik", 0, [(slice(0, S), cols_at(P + 8, P), slice(0, S), True)])], None)
                natural("o_hf", 1)
                natural("o_hi", 1)
                natural("o_hg", 1)
                transposed("o_hq", 1)
                transposed("o_iq", 1)
                transposed("o_ql", 2)
                pe.wait_ge(S_("ckv_ready"), 1)
                bank = claim("o_cT")
                for t in range(NT):
                    mm = pe.transpose(bank[:, t * P:(t + 1) * P], o_c[:, t, 0:P], ident)
                mm.then_inc(pe_filled, 1)
                transposes("o_kT", [lambda t, b=b: h_kn[:, t, b * P:(b + 1) * P] for b in range(4)],
                           lambda t: pe.wait_ge(S_("forget_ready"), NT))
                pe.wait_ge(S_("hlog_ready"), NT)
                pe.wait_ge(S_("odd_in"), 64)
                after(pe, "o_kT", 1)

                def decays(n):
                    for i in range(2):
                        bank = claim(f"h_d{n}", i)
                        for j in range(2):
                            for t in range(NT):
                                m = h_mask[:, 2 * n if n else t, :]
                                hd = 2 * i + j
                                mm = pe.matmul(bank[:, j * S + t * P:j * S + (t + 1) * P],
                                               h_f[:, t, hd * P:(hd + 1) * P], m, start=True, stop=True)
                        mm.then_inc(pe_filled, 1)

                decays(0)
                for n, h in enumerate(LEVELS):
                    if n + 1 < len(LEVELS):
                        decays(n + 1)
                    pe.wait_ge(S_("level_ready"), n + 1)
                    for i in range(1 if h == P else NT):
                        bank = claim(f"h_s{n}", i)
                        for hd in range(HH):
                            s = slice(i * P, (i + 1) * P)
                            q = slice(P, 2 * P) if h == P else s
                            mm = pe.matmul(bank[:, hd * P:(hd + 1) * P], h_KE[n % 2][:, hd, s], h_QE[n % 2][:, hd, q],
                                           start=True, stop=True)
                        mm.then_inc(pe_filled, 1)
                for t in range(NT):
                    bank = claim("h_diag", t)
                    for hd in range(HH):
                        mm = pe.matmul(bank[:, hd * P:(hd + 1) * P], h_kT[:, hd, t * P:(t + 1) * P],
                                       h_qT[:, hd, t * P:(t + 1) * P], start=True, stop=True)
                    mm.then_inc(pe_filled, 1)
                pe.wait_ge(S_("hscores_ready"), NT)
                for t in range(NT):
                    bank = claim("h_pv", t)
                    for hd in range(HH):
                        d = slice(hd * P, (hd + 1) * P)
                        mm = pe.matmul(bank[:, d], h_sc[:, t, hd, :], h_i[:, t, d], start=True, stop=(t == 0))
                        if t:
                            mm = pe.matmul(bank[:, d], h_x[:, hd, :], h_i[:, 0, d], start=False, stop=True)
                    mm.then_inc(pe_filled, 1)
                for u in range(8):
                    t, p = u // 4, u % 4
                    bank = claim("idx", u)
                    for h in range(2):
                        b, q = place_of(2 * p + h, IDH)
                        mm = pe.matmul(bank[:, h * S:(h + 1) * S], o_iqT[q, b, t * P:(t + 1) * P], o_ikT[q, :],
                                       start=True, stop=True)
                    mm.then_inc(pe_filled, 1)
                o_units = [(p, t) for t in range(NT) for p in range(4)]
                pe.wait_ge(S_("hankel_in"), 32)

                def o_scores(u, bank):
                    p, t = o_units[u]
                    for h in range(2):
                        hd = 2 * p + h
                        pe.matmul(bank[:, h * S:(h + 1) * S], o_qT[:, hd, t * P:(t + 1) * P], o_cT,
                                  start=True, stop=False)
                        mm = pe.matmul(bank[:, h * S:(h + 1) * S], flip, hankel[:, t, hd * S:(hd + 1) * S],
                                       start=False, stop=True)
                    return mm
                attend("o", o_units, o_scores, causal_keys, 12)
                for i in range(4):
                    t, g = i // 2, i % 2
                    weighted("o_pv", i, t, range(4 * g, 4 * g + 4), o_PT, lambda h, s: o_c[:, s, 0:P], P,
                             causal_keys, "o_t7")
                transposes("lat_T", [lambda t, b=b: H[:, t, b * P:(b + 1) * P] for b in range(KD)],
                           lambda t: after(pe, "o_pv", 2 * t + 1))
                after(pe, "lat_T", 3)
                uv = named_cols(small, SMALL, "w_uv").rearrange("p (h n) -> p h n", h=CH)
                for t in range(NT):
                    bank = claim("o_yc", t)
                    for h in range(CH):
                        mm = pe.matmul(bank[:, h * CDH:(h + 1) * CDH], latT[:, h, t * P:(t + 1) * P], uv[:, h, :],
                                       start=True, stop=True)
                    mm.then_inc(pe_filled, 1)
                transposes("o_yT", [lambda t, b=b: H[:, t, b * P:(b + 1) * P] if b < 4 else
                                    yd[:, t, (b - 4) * P:(b - 3) * P] for b in range(KD)],
                           lambda t: after(pe, "o_yc", t))
                after(pe, "o_yT", 3)
                natural("o_out", 2)

            for l in range(2):
                if l:
                    odd()
                norm_T(5 + 3 * l)
                after(pe, f"T{5 + 3 * l}", 3)
                transposed(f"x_q{l}", 2)
                after(pe, f"x_q{l}", 3)
                x_units = [(p, t) for p in range(2) for t in range(NT)]

                def x_scores(u, bank):
                    p, t = x_units[u]
                    for h in range(2):
                        for j in range(2):
                            b = 2 * (2 * p + h) + j
                            mm = pe.matmul(bank[:, h * S:(h + 1) * S], x_qT[:, b, t * P:(t + 1) * P], x_kTs[l][:, b, :],
                                           start=(j == 0), stop=(j == 1))
                    return mm
                attend(f"x{l}", x_units, x_scores, all_keys, 8 + 12 * l)
                for i in range(4):
                    t, g = i // 2, i % 2
                    weighted(f"x_pv{l}", i, t, (2 * g, 2 * g + 1), x_PT,
                             lambda h, s: x_vs[l][:, s, h * XDH:(h + 1) * XDH], XDH, all_keys, f"x{l}_t3")
                transposes(f"x_oT{l}", [lambda t, b=b: H[:, t, b * P:(b + 1) * P] for b in range(KD)],
                           lambda t: after(pe, f"x_pv{l}", 2 * t + 1))
                after(pe, f"x_oT{l}", 3)
                natural(f"x_o{l}", 2)
                norm_T(6 + 3 * l)
                after(pe, f"T{6 + 3 * l}", 3)
                for n in range(PH // 2):
                    transposed(f"p_q{l}{n}", 1)
                    if n == 0:
                        pe.wait_ge(S_("keys_in"), 16 * (l + 1))
                    after(pe, f"p_q{l}{n}", 1)
                    for t in range(NT):
                        bank = claim(f"p_{'sr'[t]}{l}{n}")
                        for j in range(4):
                            mm = pe.matmul(bank[:, j * P:(j + 1) * P], p_qT[:, n % 2, j, t * P:(t + 1) * P],
                                           p_keys[:, 4 * n + j, :], start=True, stop=True)
                        mm.then_inc(pe_filled, 1)
                if l == 0:
                    transposed("x_k1", 2, memT)
                    natural("x_v1", 2, memT)
                for t in range(NT):
                    weighted_rows(l, t)

        @block.scalar
        def _(act):
            step = Steps(act, "scalar_step", "scalar")

            def rstd(n_heads, sums, out, width, signal=None):
                step(act.activation(out, sums, ACT.Ln, scale=1.0 / width, bias=eps_col))
                step(act.activation(out, out, ACT.Exp, scale=-0.5), signal)

            eps_col = stat(600, 1)

            highs = [0]

            def high(stage, first=0, end=PARTS, i=0):
                n = tile_no[stage] + i
                for part in range(first, end):
                    q = highs[0]
                    assert q == parts_before(n) + part, (stage, i, part)
                    highs[0] += 1
                    if q >= SPLIT_RING:
                        former = split[(q - SPLIT_RING) // PARTS]
                        wait_used(act, former, (q - SPLIT_RING) % PARTS)
                        if tiles[former] == ("down", 5):
                            act.wait_ge(S_("lo_made"), q - SPLIT_RING + 1)
                    act.activation(W_hi[:, q % SPLIT_RING, :], wait_landed(act, n, part), ACT.Copy).then_inc(S_("hi_made"), 1)

            def high_T(stage):
                for i in range(4):
                    t, g = i // 2, i % 2
                    bank = filled(act, stage, i).rearrange("p (b t) -> p b t", b=4)
                    act.activation(HT_hi[:, 4 * g:4 * g + 4, t * P:(t + 1) * P], bank, ACT.Copy).then_inc(S_("hT_hi"), 1)

            def high_S(src, b):
                act.activation(HT_hi[:, b:b + src.shape[1], :], src, ACT.Copy).then_inc(S_("hT_hi"), 1)

            def norm(n, src, ready):
                for t in range(NT):
                    ready(t)
                    at = n % 2 * NT + t
                    step(act.activation(H[:, t, :], src[:, t, :], ACT.Square, accum_out=stat(604 + at, 1)))
                    rstd(1, stat(604 + at, 1), stat(608 + at, 1), D, "rstd_ready")

            def attend(name, units, scale, PT, n_keys, base, sums):
                def probabilities(u):
                    p, t = units[u]
                    act.wait_ge(S_("smax_ready"), base + u + 1)
                    for h in range(2):
                        hd = 2 * p + h
                        step(act.activation(probs[:, u % 2, h * S:(h + 1) * S], scrA[:, u % 2, h * S:(h + 1) * S], ACT.Exp,
                                            bias=stat(612 + 2 * (u % 2) + h, 1), scale=scale,
                                            accum_out=sums[:, t, hd:hd + 1]), "probs_ready" if h else None)
                probabilities(0)
                for u, (p, t) in enumerate(units):
                    if u + 1 < len(units):
                        probabilities(u + 1)
                    leave(name, u, p, t, PT, n_keys)

            def leave(name, u, p, t, PT, n_keys):
                bank = filled(act, f"{name}_t{u}")
                kt = n_keys(t)
                src = bank.rearrange("p (h s t) -> p h s t", h=2, s=NT)[:, :, 0:kt, :]
                step.free(act.activation(PT[:, 2 * p:2 * p + 2, 0:kt, t * P:(t + 1) * P], src, ACT.Copy),
                          f"{name}_t{u}")

            act.dma_start(cols[:], io["cols"]).then_inc(S_("cols_in"), 16)
            act.wait_ge(S_("cols_in"), 16)
            step(act.activation(stat(620, 8), named_cols(cols, COLS, "c"), ACT.Silu), "silu_c")
            act.wait_ge(S_("eps_set"), 1)
            act.wait_ge(S_("x_in"), 16)
            norm(0, X, lambda t: None)
            step.free(act.activation(stat(448, 2 * KD), filled(act, "ada")[:, 0:2 * KD], ACT.Copy), "ada")
            for i in range(4):
                after(act, "T0", i)
                t, g = i // 2, i % 2
                p = (slice(None), slice(4 * g, 4 * g + 4), slice(t * P, (t + 1) * P))
                act.activation(HT_hi[p], h0T[p], ACT.Copy).then_inc(S_("hT_hi"), 1)
                if i == 0:
                    high("z_qk", 0, 2)
            high("z_qk", 2)
            high("z_qk", i=1)
            high("z_n")
            act.wait_ge(S_("conv_ready"), 1)
            step(act.activation(qkT, qkT, ACT.Silu), "qk_ready")
            high("z_n", i=1)
            high("z_n", i=2)
            act.wait_ge(S_("angle_ready"), 1)
            step(act.activation(stat(128, 128), stat(128, 128), ACT.Sin), "sincos_ready")
            high("z_n", i=3)
            high("z_n", i=4)
            for t in range(NT):
                after(act, "z_n", 2 + t)
                step(act.activation(Z[:, t, MO:MO + MW], Z[:, t, MO:MO + MW], ACT.Sigmoid), "mo_gated")
            act.wait_ge(S_("absf_ready"), 1)
            step(act.activation(stat(32, 8), stat(32, 8), ACT.Exp, scale=-1.0))
            step(act.activation(stat(32, 8), stat(32, 8), ACT.Ln, bias=1.0), "log1p_ready")
            m_units = [(p, t) for p in range(2) for t in range(NT)]
            for u, (p, t) in enumerate(m_units):
                act.wait_ge(S_("m_max_ready"), u + 1)
                for h in range(2):
                    step(act.activation(scrA[:, u % 2, h * S:(h + 1) * S], scrA[:, u % 2, h * S:(h + 1) * S], ACT.Exp,
                                        bias=stat(64 + 4 * t + 2 * p + h, 1)), "m_w_ready" if h else None)
                if u:
                    leave("m", u - 1, *m_units[u - 1], PT1, lambda t: t + 1)
            leave("m", 3, *m_units[3], PT1, lambda t: t + 1)
            act.wait_ge(S_("m_stab_ready"), 1)
            step(act.activation(stat(80, 8), stat(80, 8), ACT.Exp, scale=-1.0), "m_floor_ready")
            act.wait_ge(S_("hm_squares"), 1)
            rstd(MH, stat(96, 8), stat(104, 8), MDH, "hm_rstd")
            a_units = [(p, t) for p in range(4) for t in range(NT)]
            attend("a", a_units, ADH ** -0.5, PT1, lambda t: t + 1, 0, stat(272, NT, 8))
            high("merge")
            high("merge", i=1)
            for c in range(2):
                after(act, "merge", 8 * c + 3)
                step(act.activation(sg, sg, ACT.Sigmoid), "gate_ready")
                if c == 0:
                    high("merge", i=3)
                    high("merge", i=4)
            high("w_out", 0, 3)
            high_T("mg_T")
            high("w_out", 3)
            high("w_out", i=1)
            high("ff_u0", 0, 2)
            norm(1, X, lambda t: after(act, "w_out", 2 + t))
            high("ff_u0", 2, 3)
            high_T("T1")
            high("ff_u0", 3)
            for i in range(NF // 2):
                if i + 1 < NF // 2:
                    high(f"ff_u{i + 1}", 0, 3)
                bank = filled(act, f"ff_g{i}")
                if i >= 2:
                    after(act, f"ff_u{i - 2}")
                step.free(act.activation(silu_g[:, i % 2, :], bank, ACT.Silu), f"ff_g{i}")
                if i + 1 < NF // 2:
                    high(f"ff_u{i + 1}", 3)
                if i == 2:
                    act.wait_ge(S_("mem_in"), 16)
                    norm(2, mem_in, lambda t: None)
            high("down", 0, 2)
            for i in range(6):
                act.wait_ge(pe_filled, plan.mark(f"ff_u{NF // 2 - 1}") if i < 2 else plan.first["down"][1] + i - 1)
                after(act, f"ff_u{min(2 * i + 1, NF // 2 - 1)}")
                high_S(fT[:, 4 * i:4 * i + 4, :] if i < 5 else fT[:, 4 * i:4 * i + 2, :], PARTS * (i % 2))
                if i == 0:
                    high("down", 2, 3)
                elif i == 1:
                    high("down", 3)
                if i:
                    high("down", i=i)
            for b in range(2):
                act.wait_ge(pe_filled, plan.first["down"][1] + 5 + b)
                high_S(memT[:, 4 * b:4 * b + 4, :], 4 * b)
            high("x_k0", 0, 3)
            high("x_k0", 3)
            high("x_k0", 0, 2, i=1)
            norm(3, X, lambda t: after(act, "down", 2 + t))
            high("x_k0", 2, i=1)
            high("x_v0", 0, 1)
            norm(4, X, lambda t: act.wait_ge(S_("h_ready"), 3 * NT + t + 1))
            high("x_v0", 1)
            high("x_v0", i=1)
            high("e_z", 0, 3)
            high_T("T4")
            high("e_z", 3)
            for i in range(1, 4):
                high("e_z", i=i)
            high("e_out", 0, 2)
            act.wait_ge(pe_filled, plan.mark("e_z", 7))
            for b in range(2):
                act.wait_ge(S_("e_yT_ready"), b + 1)
                high_S(e_yT[:, 4 * b:4 * b + 4, :], 4 * b)
            high("e_out", 2)
            high("e_out", i=1)
            for l in range(2):
                if l:
                    high("o_ik", 0, 3)
                    norm(7, X, lambda t: after(act, f"p_v0{t}", 1))
                    high_T("T7")
                    high("o_ik", 3)
                    high("o_hf")
                    high("o_hi")
                    for t in range(NT):
                        bank = filled(act, "o_hf", t)
                        step.free(act.activation(h_f[:, t, :], bank, ACT.Sigmoid), "o_hf", t)
                    high("o_hg")
                    act.wait_ge(S_("lb_diff"), 1)
                    step(act.activation(lb_row[:, 0, :], lb_row[:, 0, :], ACT.Exp))
                    step(act.activation(lb_row[:, 1, :], lb_row[:, 1, :], ACT.Exp), "lb_exp")
                    high("o_hq")
                    for t in range(NT):
                        after(act, "o_hg", t)
                        step(act.activation(h_g[:, t, :], h_g[:, t, :], ACT.Silu), "hg_ready")
                    act.wait_ge(S_("ckv_squares"), 1)
                    rstd(1, stat(288, 2), stat(290, 2), CR, "ckv_rstd")
                    high("o_iq")
                    for t in range(NT):
                        act.wait_ge(S_("forget_ready"), t + 1)
                        step(act.activation(h_f[:, t, :], h_f[:, t, :], ACT.Ln), "hlog_ready")
                    high("o_ql")
                    high("o_ql", i=1)
                    for n in range(len(LEVELS)):
                        for i in range(2):
                            bank = filled(act, f"h_d{n}", i)
                            if n >= 2:
                                act.wait_ge(S_("level_ready"), n - 1)
                            step.free(act.activation(h_E[n % 2][:, 2 * i:2 * i + 2, :].rearrange("p a b -> p (a b)"), bank,
                                                     ACT.Exp), f"h_d{n}", i)
                    act.wait_ge(S_("yd_squares"), 1)
                    rstd(HH, stat(296, 8), stat(304, 8), P, "yd_rstd")
                    for u in range(8):
                        bank = filled(act, "idx", u)
                        if u >= 2:
                            act.wait_ge(S_("rel_used"), u - 1)
                        if u == 0:
                            act.wait_ge(S_("hgrn_done"), 1)
                        step.free(act.activation(o_rel[:, u % 2, :], bank, ACT.Relu, scale=IDH ** -0.5), "idx", u)
                    attend("o", [(p, t) for t in range(NT) for p in range(4)], 1.0, o_PT, lambda t: t + 1, 12,
                           stat(272, NT, 8))
                    high("o_out", 0, 3)
                    high_T("o_yT")
                    high("o_out", 3)
                    high("o_out", i=1)
                high(f"x_q{l}", 0, 2)
                norm(5 + 3 * l, X, lambda t: after(act, "o_out" if l else "e_out", 2 + t))
                high(f"x_q{l}", 2, 3)
                high_T(f"T{5 + 3 * l}")
                high(f"x_q{l}", 3)
                high(f"x_q{l}", i=1)
                attend(f"x{l}", [(p, t) for p in range(2) for t in range(NT)], XDH ** -0.5, x_PT, lambda t: NT,
                       8 + 12 * l, stat(272, NT, 8))
                high(f"x_o{l}", 0, 3)
                high_T(f"x_oT{l}")
                high(f"x_o{l}", 3)
                high(f"x_o{l}", i=1)
                high(f"p_q{l}0", 0, 2)
                norm(6 + 3 * l, X, lambda t: after(act, f"x_o{l}", 2 + t))
                high(f"p_q{l}0", 2, 3)
                high_T(f"T{6 + 3 * l}")
                high(f"p_q{l}0", 3)
                for n in range(PH // 2):
                    if n + 1 < PH // 2:
                        high(f"p_q{l}{n + 1}", 0, 2)
                    for j in range(2):
                        bank = filled(act, f"p_q{l}{n}", j).rearrange("p (b t) -> p b t", b=2)
                        step.free(act.activation(p_qT[:, n % 2, 2 * j:2 * j + 2, :], bank, ACT.Copy), f"p_q{l}{n}", j)
                    if n + 1 < PH // 2:
                        high(f"p_q{l}{n + 1}", 2, 3)
                    bank = filled(act, f"p_r{l}{n}").rearrange("p (b n) -> p b n", b=4)
                    step.free(act.activation(p_s1[:, 4 * n:4 * n + 4, :], bank, ACT.Copy), f"p_r{l}{n}")
                    if n + 1 < PH // 2:
                        high(f"p_q{l}{n + 1}", 3)
                act.wait_ge(S_("top_ready"), NT * l + 1)
                step(act.activation(p_g[:, 0, :], p_g[:, 0, :], ACT.Exp), "top_exp")
                for t in range(NT):
                    act.wait_ge(S_("dots_ready"), NT * l + t + 1)
                    step(act.activation(p_act[:, t, :], p_act[:, t, :], ACT.Gelu_apprx_tanh), "gelu_ready")
                    act.wait_ge(S_("row_weights_ready"), NT * l + t + 1)
                    before = used_before(l, 2 * t + 1)[1]

                    def diagonals(i, first):
                        for j, r in enumerate(PE_SLOTS):
                            if not first:
                                act.wait_ge(rows_used["tensor"], i * PE_ROWS + (before - PE_ROWS + j + 1))
                            act.activation(diag[:, j, :], ident, ACT.Copy, scale=p_w[:, t, bass.ds(i * RING + r, 1)])\
                                .then_inc(S_("diag_ready"), 1)

                    diagonals(0, True)
                    with act.Fori(1, STEPS) as i:
                        diagonals(i, False)
                    if t == 0:
                        act.wait_ge(S_("top_ready"), NT * l + 2)
                        step(act.activation(p_g[:, 1, :], p_g[:, 1, :], ACT.Exp), "top_exp")
            norm(10, X, lambda t: after(act, f"p_v1{t}", 1))

        @block.vector
        def _(v):
            step = Steps(v, "vector_step", "vector")

            def tt(out, a, b, op, signal=None):
                step(v.tensor_tensor(out, a, b, op), signal)

            def ts(out, a, s1, op0, s2=None, op1=None, signal=None):
                step(v.tensor_scalar(out, a, s1, s2, op0, op1) if op1 else v.tensor_scalar(out, a, s1, None, op0), signal)

            def stt(out, a, s, b, op0, op1, signal=None, accum=None):
                step(v.scalar_tensor_tensor(out=out, in0=a, scalar=s, in1=b, op0=op0, op1=op1, accum_out=accum), signal)

            def norm(n, src, g, shift=None, signal="h_ready", dst=H):
                for t in range(NT):
                    v.wait_ge(S_("rstd_ready"), NT * n + t + 1)
                    stt(dst[:, t, :], src[:, t, :], stat(608 + n % 2 * NT + t, 1), g, ALU.mult, ALU.mult,
                        signal if shift is None else None)
                    if shift is not None:
                        tt(H[:, t, :], H[:, t, :], shift, ALU.add, signal)

            def gain_of(n):
                v.wait_ge(S_(f"gain_in{n % 2}"), 16 * ((n + 1) // 2))
                return gain[:, n % 2, :]

            def take_T(stage, dst, n_blocks=KD):
                i = 0
                for t in range(NT):
                    for g in range(n_blocks // 4):
                        bank = filled(v, stage, i)
                        step.free(v.tensor_copy(dst[:, 4 * g:4 * g + 4, t * P:(t + 1) * P],
                                                bank.rearrange("p (b t) -> p b t", b=4)), stage, i, wait=False)
                        i += 1
                after(v, stage, i - 1)

            splits = [0]

            def split_T(stage):
                for i in range(4):
                    t, g = i // 2, i % 2
                    p = (slice(None), slice(4 * g, 4 * g + 4), slice(t * P, (t + 1) * P))
                    bank = filled(v, stage, i).rearrange("p (b t) -> p b t", b=4)
                    splits[0] += 1
                    v.wait_ge(S_("hT_hi"), splits[0])
                    step.free(v.tensor_tensor(HT_lo[p], bank, HT_hi[p].bitcast(F32), ALU.subtract), stage, i, wait=(i == 3))

            def split_S(src, b, signal):
                p = (slice(None), slice(b, b + src.shape[1]))
                splits[0] += 1
                v.wait_ge(S_("hT_hi"), splits[0])
                step(v.tensor_tensor(HT_lo[p], src, HT_hi[p].bitcast(F32), ALU.subtract), signal)

            def take_blocks(stage, n, dst, scale=None, first=0):
                for i in range(first, first + n):
                    bank = filled(v, stage, i).rearrange("p (b t) -> p b t", b=2)
                    out = dst[:, 2 * i:2 * i + 2, :]
                    ins = v.tensor_copy(out, bank) if scale is None else v.tensor_scalar(out, bank, scale, None, ALU.mult)
                    step.free(ins, stage, i, wait=(i == first + n - 1))

            def softmax_max(name, units, mask, scale, between={}):
                for u, (p, t) in enumerate(units):
                    bank = filled(v, f"{name}_s{u}").rearrange("p (h s) -> p h s", h=2)
                    out = scrA[:, u % 2, :].rearrange("p (h s) -> p h s", h=2)
                    if u >= 2:
                        v.wait_ge(S_("probs_ready"), self_base[0] + u - 1)
                    if mask is None:
                        ins = v.tensor_copy(out, bank)
                    else:
                        ins = v.tensor_tensor(out, bank, mask(t).unsqueeze(1).to_broadcast([P, 2, S]), ALU.add)
                    step.free(ins, f"{name}_s{u}")
                    step(v.tensor_reduce(stat(616, 2), out, AXX, ALU.max))
                    ts(stat(612 + 2 * (u % 2), 2), stat(616, 2), -scale, ALU.mult, signal="smax_ready")
                    for i in between.get(u - 2, ()):
                        take_ada(f"ada{i}", 0, i)
                for u in (len(units) - 2, len(units) - 1):
                    for i in between.get(u, ()):
                        take_ada(f"ada{i}", 0, i)
                self_base[0] += len(units)
            self_base = [0]

            def take_weighted(stage, i, out, sums, width, ready=None):
                n = out.shape[-1] // width
                bank = filled(v, stage, i)
                r = stat(640 - 8, n)
                if len(sums.shape) == 4:
                    r = r.rearrange("p (a b c) -> p a b c", b=2, c=2)
                step(v.reciprocal(r, sums))
                step.free(v.tensor_tensor(out.rearrange("p (h d) -> p h d", h=n), bank.rearrange("p (h d) -> p h d", h=n),
                                          stat(640 - 8, n).unsqueeze(2).to_broadcast([P, n, width]), ALU.mult), stage, i)

            def head_norm(x, heads, squares, tmp, t):
                tt(tmp, x, x, ALU.mult)
                step(v.tensor_reduce(squares[:, t, :], tmp.rearrange("p (h d) -> p h d", h=heads), AXX, ALU.add))

            def add_to_x(stage, scale=None):
                for i in range(4):
                    c, t = i // 2, i % 2
                    xs = X[:, t, c * BLK:(c + 1) * BLK]
                    bank = filled(v, stage, i)
                    if scale is None:
                        step.free(v.tensor_tensor(xs, bank, xs, ALU.add), stage, i)
                    else:
                        step(v.tensor_tensor(junk_v, bank, scale[:, c * BLK:(c + 1) * BLK], ALU.mult))
                        step.free(v.tensor_tensor(xs, junk_v, xs, ALU.add), stage, i)

            junk_v = area(22048, 512)
            step(v.memset(stat(600, 1), EPS), "eps_set")
            def sum_ada(i):
                acc = ada_sum[:, i, :]
                for k in range(KD):
                    if k % 2 == 0:
                        w = wait_landed(v, i, k // 2).rearrange("p (k n) -> p k n", k=2)
                    if k == 0:
                        ts(acc, w[:, 0, :], stat(620, 1), ALU.mult)
                    else:
                        stt(acc, w[:, k % 2, :], stat(620 + k, 1), acc, ALU.mult, ALU.add, "ada_summed" if k % 2 else None)

            v.wait_ge(S_("silu_c"), 1)
            sum_ada(0)
            for t in range(NT):
                v.wait_ge(S_("rstd_ready"), t + 1)
                ts(H[:, t, :], X[:, t, :], stat(608 + t, 1), ALU.mult, signal="h_ready")
            v.wait_ge(S_("onehot_in"), 16)
            bank = filled(v, "bias_rows")
            step.free(v.tensor_copy(rb_sb, bank[0:8, :]), "bias_rows")
            for i in range(1, 4):
                sum_ada(i)
            shift, scale = stat(448, KD), stat(456, KD)
            after(v, "ada")
            tt(stat(448, 2 * KD), stat(448, 2 * KD), named_cols(cols, COLS, "mod1_b"), ALU.add)
            stt(scale, scale, 1.0, named_cols(cols, COLS, "norm1"), ALU.add, ALU.mult)
            for i in range(4):
                t, g = i // 2, i % 2
                bank = filled(v, "T0", i)
                for j in range(4):
                    b = 4 * g + j
                    ins = v.tensor_scalar(h0T[:, b, t * P:(t + 1) * P], bank[:, j * P:(j + 1) * P], scale[:, b:b + 1],
                                          shift[:, b:b + 1], ALU.mult, ALU.add)
                    if j < 3:
                        step.overlap(ins)
                    else:
                        step.free(ins, "T0", i)
            for i in range(4):
                t, g = i // 2, i % 2
                p = (slice(None), slice(4 * g, 4 * g + 4), slice(t * P, (t + 1) * P))
                splits[0] += 1
                v.wait_ge(S_("hT_hi"), splits[0])
                step(v.tensor_tensor(HT_lo[p], h0T[p], HT_hi[p].bitcast(F32), ALU.subtract), "h0T_split")
            step(v.tensor_copy(c_rep, stat(620, 8).unsqueeze(2).to_broadcast([P, KD, P])), "c_ready")
            modf = mod.rearrange("p a b -> p (a b)")

            def take_ada(stage, i, n):
                m = modf[:, n * BLK:(n + 1) * BLK]
                bank = filled(v, stage, i)
                step.free(v.tensor_tensor(m, bank, m, ALU.add), stage, i)

            step(v.memset(qk_raw[:, :, 0:3], 0.0))
            bq = named_cols(cols, COLS, "b_qk")
            for i in range(4):
                bank = filled(v, "z_qk", i)
                step(v.tensor_scalar(qk_raw[:, 2 * i, 3:], bank[:, 0:S], bq[:, 2 * i:2 * i + 1], None, ALU.add))
                step.free(v.tensor_scalar(qk_raw[:, 2 * i + 1, 3:], bank[:, S:2 * S], bq[:, 2 * i + 1:2 * i + 2], None,
                                          ALU.add), "z_qk", i)
            v.wait_ge(S_("b_rows_in"), 16)
            bank = filled(v, "z_gate")
            gates = stat(48, NT, 8)
            step.free(v.tensor_tensor(gates, bank[:, 0:16].rearrange("p (t g) -> p t g", t=NT),
                                      b_rows[:, 0:8].unsqueeze(1).to_broadcast([P, NT, 8]), ALU.add), "z_gate")
            absf = stat(32, NT, 4)
            stt(absf, gates[:, :, 4:8], -1.0, gates[:, :, 4:8], ALU.mult, ALU.max, "absf_ready")
            cw, cb = named_cols(cols, COLS, "conv_w"), named_cols(cols, COLS, "conv_b")
            for b0 in range(0, 8, 2):
                for j in range(4):
                    for b in (b0, b0 + 1):
                        if j == 0:
                            step.overlap(v.tensor_scalar(qkT[:, b, :], qk_raw[:, b, 0:S], cw[:, b:b + 1], cb[:, b:b + 1],
                                                         ALU.mult, ALU.add))
                        else:
                            step.overlap(v.scalar_tensor_tensor(
                                out=qkT[:, b, :], in0=qk_raw[:, b, j:j + S], scalar=cw[:, 8 * j + b:8 * j + b + 1],
                                in1=qkT[:, b, :], op0=ALU.mult, op1=ALU.add))
            step.all()
            step(v.memset(qk_raw[:, 0, 0:1], 0.0), "conv_ready")
            v.wait_ge(S_("pos_in"), 16)
            step(v.tensor_copy(stat(260, 2), pos_i[:]))
            TWO_PI = [6.28125, 1.9353071795e-3, 1.0253e-11]
            ang, turns = stat(320, NT, 32), stat(384, NT, 32)
            sc = stat(128, 2, NT, 32)
            for t in range(NT):
                ts(ang[:, t, :], freq, stat(260 + t, 1), ALU.mult)
            ts(turns, ang, 1 / (2 * np.pi), ALU.mult, 12582912.0, ALU.add)
            ts(turns, turns, 12582912.0, ALU.subtract)
            for c in TWO_PI:
                stt(ang, turns, -c, ang, ALU.mult, ALU.add)
            ts(sc[:, 0, :, :], ang, 3.1415925, ALU.min, -3.1415925, ALU.max)
            stt(ang, ang, -1.0, ang, ALU.mult, ALU.max)
            ts(sc[:, 1, :, :], ang, -1.0, ALU.mult, float(np.float32(np.pi / 2)), ALU.add, signal="angle_ready")

            def rotate():
                v.wait_ge(S_("sincos_ready"), 1)
                for t in range(NT):
                    x = Z[:, t, AQ:AQ + 2 * AW].rearrange("p (h a d) -> p h a d", a=2, d=32)
                    tmp = [rope_t[:, j, :].rearrange("p (h d) -> p h d", d=32) for j in range(4)]
                    sin, cos = (sc[:, j, t, :].unsqueeze(1).to_broadcast([P, 16, 32]) for j in range(2))
                    x1, x2 = x[:, :, 0, :], x[:, :, 1, :]
                    for j, (a, b) in enumerate(((x1, cos), (x2, sin), (x2, cos), (x1, sin))):
                        tt(tmp[j], a, b, ALU.mult)
                    tt(x1, tmp[0], tmp[1], ALU.subtract)
                    tt(x2, tmp[2], tmp[3], ALU.add, "rope_done" if t else None)

            for i in range(10):
                f, t = i // 2, i % 2
                bank = filled(v, "z_n", i)
                step.free(v.tensor_tensor(Z[:, t, f * BLK:(f + 1) * BLK], bank, b_rows[:, 8 + f * BLK:8 + (f + 1) * BLK],
                                          ALU.add), "z_n", i, wait=i in (7, 9))
                if i == 7:
                    rotate()
            take_T("a_T", aT)
            v.wait_ge(S_("log1p_ready"), 1)
            lf, gcol, cum = stat(0, NT, 4), stat(16, NT, 4), stat(24, NT, 4)
            stt(lf, gates[:, :, 4:8], 0.0, absf, ALU.min, ALU.subtract, "logf_ready")
            bank = filled(v, "m_cum")
            step.free(v.tensor_copy(cum, bank[:, 0:8].rearrange("p (t g) -> p t g", t=NT)), "m_cum")
            tt(gcol, gates[:, :, 0:4], cum, ALU.subtract, "g_ready")
            negM = stat(64, NT, 4)
            m_units = [(p, t) for p in range(2) for t in range(NT)]
            den = stat(88, NT, 4)
            g_row = area(18976 + 1024, 2, 512)
            for p in range(2):
                bank = filled(v, f"m_g{p}")
                step.free(v.tensor_copy(g_row[:, p, :], bank), f"m_g{p}")

            def m_log(u):
                p, t = m_units[u]
                w = scrA[:, u % 2, :].rearrange("p (h s) -> p h s", h=2)
                tt(w, g_row[:, p, :].rearrange("p (h s) -> p h s", h=2),
                   causal[:, t, :].unsqueeze(1).to_broadcast([P, 2, S]), ALU.add)
                step(v.tensor_reduce(stat(616, 2), w, AXX, ALU.max))
                ts(negM[:, t, 2 * p:2 * p + 2], stat(616, 2), 0.0, ALU.max, -1.0, ALU.mult, signal="m_max_ready")

            v.wait_ge(S_("scratch_written"), 16)
            m_log(0)
            for u, (p, t) in enumerate(m_units):
                if u + 1 < 4:
                    m_log(u + 1)
                v.wait_ge(S_("m_w_ready"), u + 1)
                bank = filled(v, f"m_s{u}")
                if u >= 2:
                    v.wait_ge(pe_filled, plan.mark(f"m_t{u - 2}"))
                for h in range(2):
                    c = slice(h * S, (h + 1) * S)
                    ins = v.scalar_tensor_tensor(out=probs[:, u % 2, c], in0=bank[:, c], scalar=MDH ** -0.5,
                                                 in1=scrA[:, u % 2, c], op0=ALU.mult, op1=ALU.mult,
                                                 accum_out=den[:, t, 2 * p + h:2 * p + h + 1])
                    if h:
                        step.free(ins, f"m_s{u}")
                    else:
                        step(ins)
                if u == 2:
                    v.wait_ge(S_("ada_b_rest_in"), 16)
                if u >= 2:
                    for i in ADA_IN_M[u - 2]:
                        take_ada(f"ada{i}", 0, i)
            for i in ADA_IN_M[2] + ADA_IN_M[3]:
                take_ada(f"ada{i}", 0, i)
            step(v.memset(junk_v[:, 0:1], 0.0), "m_row_free")
            floor = stat(80, NT, 4)
            tt(floor, cum, negM, ALU.subtract, "m_stab_ready")
            stt(den, den, -1.0, den, ALU.mult, ALU.max)
            v.wait_ge(S_("m_floor_ready"), 1)
            tt(den, den, floor, ALU.max)
            step(v.reciprocal(den, den))
            hm = area(23072, NT, 512)
            sq = stat(96, NT, 4)
            for t in range(NT):
                bank = filled(v, "m_pv", t)
                step.free(v.tensor_tensor(hm[:, t, :].rearrange("p (h d) -> p h d", h=MH),
                                          bank.rearrange("p (h d) -> p h d", h=MH),
                                          den[:, t, :].unsqueeze(2).to_broadcast([P, MH, MDH]), ALU.mult), "m_pv", t)
                head_norm(hm[:, t, :], MH, sq, area(22560, 512), t)
            step(v.tensor_copy(sq, sq), "hm_squares")
            v.wait_ge(S_("hm_rstd"), 1)
            v.wait_ge(S_("m_row_in"), 16)
            v.wait_ge(S_("mo_gated"), NT)
            for t in range(NT):
                x = hm[:, t, :]
                tt(x.rearrange("p (h d) -> p h d", h=MH), x.rearrange("p (h d) -> p h d", h=MH),
                   stat(104, NT, 4)[:, t, :].unsqueeze(2).to_broadcast([P, MH, MDH]), ALU.mult)
                tt(x, x, m_row, ALU.mult)
                tt(Z[:, t, MO:MO + MW], x, Z[:, t, MO:MO + MW], ALU.mult)
            a_units = [(p, t) for p in range(4) for t in range(NT)]
            softmax_max("a", a_units, lambda t: causal[:, t, :], ADH ** -0.5, ADA_IN_A)
            stt(mod[:, 4, :], mod[:, 4, :], 1.0, gain_of(1), ALU.add, ALU.mult)
            sums = stat(272, NT, 8)
            for t in range(NT):
                by_head = sums[:, t, :].rearrange("p (a b c) -> p a c b", b=2, c=2)
                take_weighted("a_pv", t, Z[:, t, AQ:AQ + AW], by_head, ADH)
            take_T("y_T", yT)
            v.wait_ge(S_("b_g_in"), 16)
            b_g = area(0, 2, D)
            for c in range(2):
                for j in range(4):
                    bank = filled(v, "merge", 8 * c + j)
                    step.free(v.tensor_tensor(sg[:, j, :], bank, b_g[:, j // 2, c * BLK:(c + 1) * BLK], ALU.add),
                              "merge", 8 * c + j)
                v.wait_ge(S_("gate_ready"), c + 1)
                for t in range(NT):
                    h = H[:, t, c * BLK:(c + 1) * BLK]
                    for m in range(2):
                        i = 8 * c + 4 + 2 * t + m
                        bank = filled(v, "merge", i)
                        step.free(v.tensor_tensor(sg[:, 2 * m + t, :], bank, sg[:, 2 * m + t, :], ALU.mult), "merge", i)
                    tt(h, sg[:, t, :], sg[:, 2 + t, :], ALU.add, "merged_ready")
            split_T("mg_T")
            add_to_x("w_out", mod[:, 2, :])
            norm(1, X, mod[:, 4, :], mod[:, 3, :])
            split_T("T1")
            for i in range(NF // 2):
                after(v, f"ff_g{i}")
                bank = filled(v, f"ff_u{i}")
                f = fT[:, 2 * i:2 * i + 2, :].rearrange("p a b -> p (a b)")
                step.free(v.tensor_tensor(f, bank, silu_g[:, i % 2, :], ALU.mult), f"ff_u{i}")
                if i == 3:
                    norm(2, mem_in, gain_of(2))
                if i == 4:
                    take_T("T2", memT)
            for i in range(6):
                split_S(fT[:, 4 * i:4 * i + 4, :] if i < 5 else fT[:, 4 * i:4 * i + 2, :], PARTS * (i % 2), "f_split")
            for b in range(2):
                split_S(memT[:, 4 * b:4 * b + 4, :], 4 * b, "mem_split")
            add_to_x("down", mod[:, 5, :])
            norm(3, X, gain_of(3), dst=X)
            norm(4, X, gain_of(4))

            def take_mem_keys(l):
                take_blocks(f"x_k{l}", 4, x_kTs[l])

            def take_mem_values(l):
                if l:
                    v.wait_ge(pe_filled, plan.mark(f"x_v{l}", 3))
                for i in range(4):
                    c, t = i // 2, i % 2
                    bank = filled(v, f"x_v{l}", i)
                    step.free(v.tensor_copy(x_vs[l][:, t, c * BLK:(c + 1) * BLK], bank), f"x_v{l}", i)

            take_mem_keys(0)
            take_mem_values(0)
            split_T("T4")
            step(v.memset(e_pv[:, :, 0:16], 0.0))
            step(v.memset(e_cu[:, :, 0:2], 0.0))
            take_blocks("e_z", 2, e_z)
            step(v.tensor_copy(e_pv[:, :, 16:], e_z[:, 0:4, :]))
            v.wait_ge(S_("inv_in"), 16)
            for g in range(4):
                src = e_pv[:, g, :]
                for j in range(g + 1):
                    dst = e_t[:, j % 2, :]
                    w = 1 << j
                    tt(dst[:, w:], src[:, w:], src[:, 0:S + 16 - w], ALU.add)
                    step(v.tensor_copy(dst[:, 0:w], src[:, 0:w]))
                    src = dst
                tt(e_pool[:, g, :], src[:, 16:], e_inv[:, g, :], ALU.mult)
                tt(e_pool[:, g, :], e_pool[:, g, :], e_pv[:, g, 16:], ALU.subtract, "pooled_ready" if g == 3 else None)
            take_blocks("e_z", 4, e_z, first=2)
            ec = named_cols(cols, COLS, "even_conv")
            tt(e_cu[:, :, 2:], e_z[:, 8:12, :], e_z[:, 4:8, :], ALU.mult)
            for b in range(4):
                y = e_yT[:, b, :]
                ts(y, e_cu[:, b, 0:S], ec[:, b:b + 1], ALU.mult)
                for j in (1, 2):
                    stt(y, e_cu[:, b, j:j + S], ec[:, 4 * j + b:4 * j + b + 1], y, ALU.mult, ALU.add)
            take_blocks("e_z", 2, e_z, first=6)
            tt(e_yT[:, 0:4, :], e_yT[:, 0:4, :], e_z[:, 12:16, :], ALU.mult, "e_yT_ready")
            split_S(e_yT[:, 0:4, :], 0, "e_split")
            ps = named_cols(cols, COLS, "pool_scale")
            for i in range(2):
                bank = filled(v, "e_pool", i)
                for b in range(2):
                    g = 2 * i + b
                    ins = v.tensor_scalar(e_yT[:, 4 + g, :], bank[:, b * S:(b + 1) * S], ps[:, g:g + 1], None, ALU.mult)
                    if b:
                        step.free(ins, "e_pool", i)
                    else:
                        step(ins)
            step(v.tensor_copy(e_yT[:, 7, 0:1], e_yT[:, 7, 0:1]), "e_yT_ready")
            split_S(e_yT[:, 4:8, :], 4, "e_split")
            add_to_x("e_out")

            def odd():
                norm(7, X, gain_of(7))
                split_T("T7")
                bank = filled(v, "o_ckv")
                step.free(v.tensor_copy(o_c, bank[:, 0:NT * (P + 8)].rearrange("p (t n) -> p t n", t=NT)), "o_ckv")
                bank = filled(v, "o_ik")
                step.free(v.tensor_copy(o_ikT, bank[:, 0:S]), "o_ik")
                v.wait_ge(S_("odd_in"), 64)
                tmp = h_KE[0][:, 0:2, :].rearrange("p a b -> p (a b)")
                tt(tmp, lb_row[:, 0, :], lb_row[:, 1, :], ALU.max)
                tt(lb_row[:, 0, :], lb_row[:, 0, :], tmp, ALU.subtract)
                tt(lb_row[:, 1, :], lb_row[:, 1, :], tmp, ALU.subtract, "lb_diff")
                for t in range(NT):
                    bank = filled(v, "o_hi", t)
                    step.free(v.tensor_copy(h_i[:, t, :], bank), "o_hi", t)
                for t in range(NT):
                    bank = filled(v, "o_hg", t)
                    step.free(v.tensor_copy(h_g[:, t, :], bank), "o_hg", t)
                for t in range(NT):
                    stt(h_QE[0][:, 0, 0:P], o_c[:, t, 0:P], 1.0, o_c[:, t, 0:P], ALU.mult, ALU.mult,
                        accum=stat(288 + t, 1))
                step(v.tensor_copy(stat(288, 2), stat(288, 2)), "ckv_squares")
                v.wait_ge(S_("lb_exp"), 1)
                tt(tmp, lb_row[:, 0, :], lb_row[:, 1, :], ALU.add)
                step(v.reciprocal(tmp, tmp))
                tt(lb_row[:, 0, :], lb_row[:, 0, :], tmp, ALU.mult)
                ts(lb_row[:, 1, :], lb_row[:, 0, :], -1.0, ALU.mult, 1.0, ALU.add)
                v.wait_ge(S_("ckv_rstd"), 1)
                for t in range(NT):
                    stt(o_c[:, t, 0:P], o_c[:, t, 0:P], stat(290 + t, 1), kv_row, ALU.mult, ALU.mult,
                        "ckv_ready" if t else None)
                for t in range(NT):
                    after(v, "o_hf", t)
                    tt(h_f[:, t, :], h_f[:, t, :], lb_row[:, 1, :], ALU.mult)
                    tt(h_f[:, t, :], h_f[:, t, :], lb_row[:, 0, :], ALU.add)
                    ts(h_kn[:, t, :], h_f[:, t, :], -1.0, ALU.mult, 1.0, ALU.add, signal="forget_ready")
                take_blocks("o_hq", 2, h_qT)
                take_blocks("o_iq", 2, o_iqT)
                take_blocks("o_ql", 4, o_qT, CR ** -0.5)
                bank = filled(v, "o_cT")
                step.free(v.tensor_copy(o_cT, bank[:, 0:S]), "o_cT")
                take_T("o_kT", h_kT, 4)
                def decay(n):
                    after(v, f"h_d{n}", 1)
                    step.overlap(v.tensor_tensor(h_KE[n % 2], h_kT, h_E[n % 2], ALU.mult))
                    tt(h_QE[n % 2], h_qT, h_E[n % 2], ALU.mult, "level_ready")

                decay(0)
                for n, h in enumerate(LEVELS):
                    if n + 1 < len(LEVELS):
                        decay(n + 1)
                    n_fills = 1 if h == P else NT
                    for i in range(n_fills):
                        bank = filled(v, f"h_s{n}", i).rearrange("p (h t) -> p h t", h=HH)
                        if h == P:
                            step.free(v.tensor_copy(h_x, bank), f"h_s{n}", i)
                        else:
                            m = h_mask[:, 2 * n + 1, :].unsqueeze(1).to_broadcast([P, HH, P])
                            out = h_sc[:, i, :, :] if n == 1 else h_tmp[:, i, :, :]
                            step.free(v.tensor_tensor(out, bank, m, ALU.mult), f"h_s{n}", i, wait=(i == NT - 1))
                    if n > 1:
                        tt(h_sc, h_sc, h_tmp, ALU.add)
                for t in range(NT):
                    bank = filled(v, "h_diag", t).rearrange("p (h t) -> p h t", h=HH)
                    step.free(v.tensor_tensor(h_tmp[:, t, :, :], bank, ident.unsqueeze(1).to_broadcast([P, HH, P]),
                                              ALU.mult), "h_diag", t)
                    tt(h_sc[:, t, :, :], h_sc[:, t, :, :], h_tmp[:, t, :, :], ALU.add, "hscores_ready")
                sq = stat(296, NT, 4)
                for t in range(NT):
                    bank = filled(v, "h_pv", t)
                    step.free(v.tensor_copy(h_o[:, t, :], bank), "h_pv", t)
                    head_norm(h_o[:, t, :], HH, sq, h_tmp[:, 0].rearrange("p a b -> p (a b)"), t)
                step(v.tensor_copy(sq, sq), "yd_squares")
                v.wait_ge(S_("yd_rstd"), 1)
                v.wait_ge(S_("hg_ready"), NT)
                for t in range(NT):
                    x = h_o[:, t, :]
                    tt(x.rearrange("p (h d) -> p h d", h=HH), x.rearrange("p (h d) -> p h d", h=HH),
                       stat(304, NT, 4)[:, t, :].unsqueeze(2).to_broadcast([P, HH, P]), ALU.mult)
                    tt(x, x, h_row, ALU.mult)
                    tt(yd[:, t, :], x, h_g[:, t, :], ALU.mult, "hgrn_done" if t else None)
                for u in range(8):
                    t, p = u // 4, u % 4
                    after(v, "idx", u)
                    for h in range(2):
                        if h == 0 and p == 0:
                            ts(o_iw, o_c[:, t, P:P + 8], IH ** -0.5, ALU.mult)
                        hd = head_of(2 * p + h)
                        if hd == 0:
                            ts(o_score[:, t, :], o_rel[:, u % 2, 0:S], o_iw[:, 0:1], ALU.mult)
                        else:
                            stt(o_score[:, t, :], o_rel[:, u % 2, h * S:(h + 1) * S], o_iw[:, hd:hd + 1],
                                o_score[:, t, :], ALU.mult, ALU.add, "rel_used" if h else None)
                tt(o_work, o_score, causal, ALU.add)
                for r in range(TOPK // 8):
                    for t in range(NT):
                        step.overlap(v.max(stat(464 + 8 * t, 8), o_work[:, t, :]))
                    for t in range(NT):
                        step.overlap(v.match_replace(o_work[:, t, :], stat(464 + 8 * t, 8), o_work[:, t, :], REMOVED))
                step.all()
                ts(o_work, o_work, REMOVED / 2, ALU.is_gt, NEG, ALU.mult)
                tt(o_mask, o_work, causal, ALU.add)
                softmax_max("o", [(p, t) for t in range(NT) for p in range(4)], lambda t: o_mask[:, t, :], 1.0)
                for i in range(4):
                    t, g = i // 2, i % 2
                    take_weighted("o_pv", i, H[:, t, g * BLK:(g + 1) * BLK], sums[:, t, 4 * g:4 * g + 4], P)
                take_T("lat_T", latT)
                for t in range(NT):
                    bank = filled(v, "o_yc", t)
                    step.free(v.tensor_copy(H[:, t, 0:BLK], bank), "o_yc", t)
                split_T("o_yT")
                add_to_x("o_out")

            o_iw = stat(312, 8)

            def top16(jobs):
                for values, index, src, work in jobs:
                    step.overlap(v.max(values[:, 0:8], src))
                for values, index, src, work in jobs:
                    step.overlap(v.max_index(index[:, 0:8], values[:, 0:8], src))
                for values, index, src, work in jobs:
                    step.overlap(v.match_replace(work, values[:, 0:8], src, REMOVED))
                for values, index, src, work in jobs:
                    step.overlap(v.max(values[:, 8:16], work))
                for values, index, src, work in jobs:
                    step.overlap(v.max_index(index[:, 8:16], values[:, 8:16], work))
                step.all()

            def top_lists(scores, b0, b1):
                top16([(p_v16[:, b, :], p_idx[:, b, :], scores[:, b, :], p_work[:, (b - b0) * NK:(b - b0 + 1) * NK])
                       for b in range(b0, b1)])

            def candidates(h0, h1):
                step(v.tensor_copy(p_i16[:, 2 * h0:2 * h1, :], p_idx[:, 2 * h0:2 * h1, :]))
                v16 = p_v16.rearrange("p (h a) k -> p h a k", a=2)[:, h0:h1]
                cand = p_cand.rearrange("p (h a b) -> p h a b", a=PK, b=PK)
                shape = [P, h1 - h0, PK, PK]
                tt(cand, v16[:, :, 0, :].unsqueeze(3).to_broadcast(shape),
                   v16[:, :, 1, :].unsqueeze(2).to_broadcast(shape), ALU.add)

            def top_heads(h0, h1):
                cut = [slice((h - h0) * S, (h - h0 + 1) * S) for h in range(h0, h1)]
                top16([(p_top[:, h, :], p_pos[:, h, :], p_cand[:, c], p_work[:, c]) for h, c in zip(range(h0, h1), cut)])

            def keys_of(t, h0, h1):
                e = slice(h0 * PK, h1 * PK)
                pos = p_pos[:].rearrange("p h k -> p (h k)")[:, e]
                step.overlap(v.tensor_scalar(p_bits[:, 0, e], pos, 4, None, ALU.logical_shift_right))
                step(v.tensor_scalar(p_bits[:, 1, e], pos, 15, None, ALU.bitwise_and))
                step(v.tensor_copy(p_ab[:, :, e], p_bits[:, :, e]))
                i16 = p_i16.rearrange("p (h a) k -> p h a k", a=2)[:, h0:h1]
                n = (h1 - h0) * PK
                eq = [p_eq[:, a, :] for a in range(2)]
                for a in range(2):
                    step.overlap(v.tensor_tensor(eq[a].rearrange("p (n m) -> p n m", m=PK),
                                                 p_ab[:, a, e].unsqueeze(2).to_broadcast([P, n, PK]),
                                                 iota.unsqueeze(1).to_broadcast([P, n, PK]), ALU.is_equal))
                for a in range(2):
                    eq4 = eq[a].rearrange("p (h k m) -> p h k m", k=PK, m=PK)
                    step.overlap(v.tensor_tensor(eq4, eq4, i16[:, :, a, :].unsqueeze(2).to_broadcast([P, h1 - h0, PK, PK]),
                                                 ALU.mult))
                for a in range(2):
                    step.overlap(v.tensor_reduce(p_i12[:, a, e], eq[a].rearrange("p (n m) -> p n m", m=PK), AXX, ALU.add))
                step.all()
                stt(p_eid[:, t, e], p_i12[:, 0, e], float(NK), p_i12[:, 1, e], ALU.mult, ALU.add, "eid_ready")

            def top_exponents(t):
                g = p_g[:, t, :].rearrange("p (h k) -> p h k", h=PH)
                tt(g, p_top, p_top[:, :, 0:1].to_broadcast([P, PH, PK]), ALU.subtract, "top_ready")

            def row_softmax(l, t):
                g = p_g[:, t, :].rearrange("p (h k) -> p h k", h=PH)
                v.wait_ge(S_("top_exp"), NT * l + t + 1)
                step(v.tensor_reduce(stat(616, 8), g, AXX, ALU.add))
                step(v.reciprocal(stat(616, 8), stat(616, 8)))
                tt(g, g, stat(616, 8).unsqueeze(2).to_broadcast([P, PH, PK]), ALU.mult)

            def dots(l, t):
                phase = 2 * t
                n, before = (l * 2 * NT + phase) * STEPS, used_before(l, phase)[0]
                with v.Fori(0, STEPS) as i:
                    for r in range(RING):
                        v.wait_ge(row_landed[r], i * 16 + 16 * (n + 1))
                        v.scalar_tensor_tensor(out=rows_u[:, r, :], in0=rows_u[:, r, :], scalar=1.0, in1=H[:, t, :],
                                               op0=ALU.mult, op1=ALU.mult,
                                               accum_out=p_act[:, t, bass.ds(i * RING + r, 1)])\
                            .then_inc(rows_used["vector"], 1)
                v.wait_ge(rows_used["vector"], before + SEL)
                step(v.tensor_copy(p_act[:, t, 0:1], p_act[:, t, 0:1]), "dots_ready")
                v.wait_ge(S_("gelu_ready"), NT * l + t + 1)
                tt(p_w[:, t, :], p_act[:, t, :], p_g[:, t, :], ALU.mult, "row_weights_ready")

            def add_rows(l, t, i):
                phase = 2 * t + 1
                n, before = (l * 2 * NT + phase) * STEPS, used_before(l, phase)[0]
                for j, r in enumerate(VE_SLOTS):
                    v.wait_ge(row_landed[r], i * 16 + 16 * (n + 1))
                    v.wait_ge(rows_used["vector"], i * len(VE_SLOTS) + (before + j))
                    v.scalar_tensor_tensor(out=X[:, t, :], in0=rows_u[:, r, :],
                                           scalar=p_w[:, t, bass.ds(i * RING + r, 1)], in1=X[:, t, :],
                                           op0=ALU.mult, op1=ALU.add).then_inc(rows_used["vector"], 1)

            def add_sums(l, t):
                by_v, by_pe = used_before(l, 2 * t + 2)
                v.wait_ge(rows_used["vector"], by_v)
                v.wait_ge(rows_used["tensor"], by_pe)
                for c in range(2):
                    xs = X[:, t, c * BLK:(c + 1) * BLK]
                    step.free(v.tensor_tensor(xs, banks[:, plan.bank(f"p_v{l}{t}", c), :], xs, ALU.add), f"p_v{l}{t}", c)

            def peer(l):
                norm(6 + 3 * l, X, gain_of(6 + 3 * l))
                split_T(f"T{6 + 3 * l}")
                for n in range(PH // 2):
                    bank = filled(v, f"p_s{l}{n}")
                    step.free(v.tensor_copy(p_s[:, 4 * n:4 * n + 4, :], bank.rearrange("p (b n) -> p b n", b=4)), f"p_s{l}{n}")
                    top_lists(p_s, 4 * n, 4 * n + 4)
                    candidates(2 * n, 2 * n + 2)
                    top_heads(2 * n, 2 * n + 2)
                    keys_of(0, 2 * n, 2 * n + 2)
                top_exponents(0)
                if l == 0:
                    take_mem_keys(1)
                row_softmax(l, 0)
                dots(l, 0)
                after(v, f"p_r{l}{PH // 2 - 1}")
                for i in range(STEPS):
                    add_rows(l, 0, i)
                    h0, h1 = i // 3 * 2, i // 3 * 2 + 2
                    if i < 12 and i % 3 == 0:
                        top_lists(p_s1, 2 * h0, 2 * h1)
                    elif i < 12 and i % 3 == 1:
                        candidates(h0, h1)
                        top_heads(h0, h1)
                    elif i < 12:
                        keys_of(1, h0, h1)
                    elif i == 12:
                        top_exponents(1)
                    elif i == 13 and l == 0:
                        take_mem_values(1)
                add_sums(l, 0)
                row_softmax(l, 1)
                dots(l, 1)
                with v.Fori(0, STEPS) as i:
                    add_rows(l, 1, i)
                add_sums(l, 1)

            for l in range(2):
                if l:
                    odd()
                norm(5 + 3 * l, X, gain_of(5 + 3 * l))
                split_T(f"T{5 + 3 * l}")
                take_blocks(f"x_q{l}", 4, x_qT)
                softmax_max(f"x{l}", [(p, t) for p in range(2) for t in range(NT)], None, XDH ** -0.5)
                for i in range(4):
                    t, g = i // 2, i % 2
                    take_weighted(f"x_pv{l}", i, H[:, t, g * BLK:(g + 1) * BLK], sums[:, t, 2 * g:2 * g + 2], XDH)
                split_T(f"x_oT{l}")
                add_to_x(f"x_o{l}")
                peer(l)
            norm(10, X, gain_of(10), signal="final_ready")


def constants():
    f = np.float32
    const = np.zeros((P, NCONST), f)

    def put(name, a):
        at, n = CONST[name]
        const[:, at:at + n] = a

    r = np.arange(P)
    put("ident", np.eye(P))
    put("flip", np.eye(P)[::-1])
    put("ones", 1.0)
    q = np.arange(S).reshape(NT, P).T
    put("causal", np.where(np.arange(S)[None, None] <= q[:, :, None], 0.0, NEG).reshape(P, NT * S))
    put("tri", r[:, None] <= r[None])
    half = ADH // 2
    put("freq", (f(10000.0) ** (-np.arange(half, dtype=f) / f(half)))[None])
    put("iota", np.arange(16)[None])

    dist = np.maximum(S - 1 - np.arange(2 * S), 0)
    exact = BUCKETS // 2
    ratio = np.log(np.maximum(dist, 1).astype(f) / f(exact)) / f(np.log(MAXDIST / exact))
    large = np.minimum(exact + (ratio * (BUCKETS - exact)).astype(np.int32), BUCKETS - 1)
    bucket = np.where(dist < exact, dist, large)
    onehot = (bucket[None] == np.arange(BUCKETS)[:, None]).astype(f)

    inv = np.stack([1.0 / np.minimum(np.arange(S) + 1, w) for w in (2, 4, 8, 16)]).astype(f)
    pool_inv = np.broadcast_to(inv.reshape(1, -1), (P, 4 * S)).copy()

    masks = [r[:, None] > r[None], r[:, None] <= r[None]]
    for h in LEVELS[1:]:
        mid = r // (2 * h) * 2 * h + h
        second = r % (2 * h) >= h
        a, x, m = r[:, None], r[None], mid[None]
        masks.append(np.where(second[None], (a >= m) & (a <= x), (a > x) & (a < m)))
        masks.append((r[:, None] // (2 * h) == r[None] // (2 * h)) & ~second[:, None] & second[None])
    masks = np.concatenate([m.astype(f) for m in masks], 1)
    return {"const": const, "onehot": onehot, "pool_inv": pool_inv, "masks": masks}


def lay_out(a):
    def std(w):
        k = w.shape[0] // P
        return w.reshape(k, P, w.shape[1]).transpose(1, 0, 2).reshape(P, -1)

    def cut(w):
        return [std(w[:, c:c + BLK]) for c in range(0, w.shape[1], BLK)]

    w_in = a["w_in"][0]
    o = MW * 4 + 2 * MH
    ada = cut(a["ada_w"][0])
    kv = [cut(w) for w in a["xattn_wkv_2"]]
    t = ada[:4] + cut(w_in[:, 0:2 * MW]) + cut(w_in[:, 2 * MW:4 * MW]) + cut(w_in[:, o:o + 3 * AW]) + ada[4:]
    g = o + 3 * AW
    for c in range(2):
        t.append(std(w_in[:, g + c * BLK:g + (c + 1) * BLK]))
        t.append(std(w_in[:, g + D + c * BLK:g + D + (c + 1) * BLK]))
        t.append(np.concatenate([std(a["p_mlstm"][0][:, c * BLK:(c + 1) * BLK]),
                                 std(a["p_moba"][0][:, c * BLK:(c + 1) * BLK])], 1))
    t += cut(a["w_out"][0])
    for i in range(NF // 2):
        c = slice(2 * P * i, 2 * P * (i + 1))
        t.append(std(np.concatenate([a["w_gate"][0][:, c], a["w_up"][0][:, c]], 1)))
    down = np.concatenate([a["w_down"][0], np.zeros((2 * P, D), np.float32)], 0)
    t += [std(down[4 * P * i:4 * P * (i + 1)]) for i in range(6)]
    e = cut(a["even_w_in_2"][0])
    t += kv[0] + [e[3], e[0], e[1], e[2]] + cut(a["even_w_out_2"][0])
    wi = a["odd_w_in_2"][0]
    for l in range(2):
        if l:
            c0 = 1024
            iq0, ik0, iw0, h0 = c0 + CR, c0 + CR + 512, c0 + CR + 576, c0 + CR + 584
            ik = wi[:, ik0:ik0 + 64]
            t.append(std(np.concatenate([wi[:, c0:c0 + CR], wi[:, iw0:iw0 + 8], ik, ik,
                                         np.zeros((D, BLK - 264), np.float32)], 1)))
            hq, hf, hi, hg = cut(wi[:, h0:h0 + 2048])
            t += [hf, hi, hg, hq] + cut(wi[:, iq0:iq0 + 512]) + cut(wi[:, 0:1024])
            t += cut(a["odd_w_out_2"][0])
        t += cut(a["xattn_wq_2"][l]) + cut(a["xattn_wo_2"][l]) + cut(a["peer_wq_2"][l])
        if l == 0:
            t += kv[1]
    weights = np.stack(t)

    col = lambda x: x.reshape(-1, P).T
    cols = np.concatenate([col(a["c"][0]), col(a["ada_b"][0, 0:2 * D]), col(a["norm1_g"][0]), col(a["b_in"][0, 0:2 * MW]),
                           *[col(a["conv_w"][0, j]) for j in range(4)], col(a["conv_b"][0]),
                           *[col(a["even_conv_w_2"][0, j, 0]) for j in range(3)], col(a["even_pool_scale_2"][0])], 1)
    gates = std(w_in[:, 4 * MW:4 * MW + 8])
    small = np.concatenate([gates, a["even_pool_w_2"][0].transpose(1, 0, 2).reshape(P, -1),
                            a["odd_w_uv_2"][0].transpose(1, 0, 2).reshape(P, -1)], 1)
    b = a["b_in"][0]
    rows = np.concatenate([a["ada_b"][0], b[4 * MW:o], b[2 * MW:4 * MW], b[o:g], b[g:], a["m_norm_g"][0],
                           a["hgrn_gamma_2"].reshape(-1), a["odd_kv_norm_2"][0], a["odd_hg_norm_2"][0],
                           a["norm1_g"][0], a["norm2_g"][0], a["mem_norm_2"], a["normf_g"], a["mix_norm_2"][0], a["xattn_norm_2"][0],
                           a["peer_norm_2"][0], a["mix_norm_2"][1], a["xattn_norm_2"][1], a["peer_norm_2"][1],
                           a["final_norm_2"]])[None]
    pos = a["positions"].reshape(NT, P).T
    keys = a["peer_keys_2"].transpose(0, 4, 1, 2, 3).reshape(2, P, 16 * NK)
    return {"weights": weights, "cols": cols, "small": small, "rows": rows, "pos": pos, "rel_bias": a["rel_bias_2"],
            "x": a["x"], "mem": a["mem_2"], "keys": keys, "u0": a["peer_u_2"][0], "u1": a["peer_u_2"][1],
            "v0": a["peer_v_2"][0], "v1": a["peer_v_2"][1], **constants()}


def kernel(**inputs):
    import concourse.bacc as bacc
    from concourse.bass_utils import run_bass_kernel_spmd

    arrays = {"in_" + n: np.ascontiguousarray(x) for n, x in lay_out({k: np.asarray(x) for k, x in inputs.items()}).items()}
    nc = bacc.Bacc("TRN2", target_bir_lowering=False, num_devices=1)
    io = {n[3:]: nc.dram_tensor(n, x.shape, mybir.dt.from_np(x.dtype), kind="ExternalInput").ap() for n, x in arrays.items()}
    io["out"] = nc.dram_tensor("out_dram", (1, S, D), F32, kind="ExternalOutput").ap()
    build(nc, io)
    return run_bass_kernel_spmd(nc, [arrays], core_ids=[0]).results[0]["out_dram"]
```
